# Optimizing a Trainium2 kernel written in Bass

```python
import functools
import jax, jax.numpy as jnp
from jax import lax
import numpy as np

D_MODEL = 1024
BATCH = 1
SEQ = 512
DEPTH = 2
DEC_BATCH = 8
DEC_SEQ = 8
PAST_LEN = 2048
PAGE_SIZE = 128

N_EVEN = (DEPTH + 1) // 2
N_ODD = DEPTH // 2
EPS = 1e-6
CHUNK = 128
A_W = D_MODEL // 2
A_G = 4
A_C = A_W // A_G
B_W = D_MODEL // 2
HB = 8
NB = B_W // HB
W_LORA = 64
A_LORA = 64
G_LORA = 128
P_B = 3 * B_W + W_LORA + A_LORA + G_LORA
GN_EPS = 64e-5
C_W = D_MODEL // 2
NBLK = 8
BW = C_W // NBLK
CONV_W = 4
LRU_C = 8.0
H_D = 8
HD = 64
N_KV = 2
H_I = 8
D_I = 32
TOPK_MAX = 256
Q_BLOCK = 128
P_D = H_D * HD + 2 * N_KV * HD + H_I * D_I + D_I + H_I
ROPE_THETA = 500000.0
P_EVEN = 2 * A_W + P_B
P_ODD = 2 * C_W + P_D
MEM = 256
XH = 4
XHD = D_MODEL // XH
D_FF = ((8 * D_MODEL // 3 + 255) // 256) * 256

kernel_name = 'hybrid_gmlp_rwkv7_rglru_dsa_decode_step'

def rms_norm(x, g):
    xf = x.astype(jnp.float32)
    y = xf * lax.rsqrt(jnp.mean(xf * xf, -1, keepdims=True) + EPS)
    return (y * g.astype(jnp.float32)).astype(x.dtype)

def layer_norm(x, g, b):
    xf = x.astype(jnp.float32)
    mu = jnp.mean(xf, -1, keepdims=True)
    var = jnp.mean(jnp.square(xf - mu), -1, keepdims=True)
    return ((xf - mu) * lax.rsqrt(var + EPS) * g + b).astype(x.dtype)

def split_cols(p, sizes):
    return jnp.split(p, np.cumsum(sizes)[:-1].tolist(), axis=-1)

def gather_rows(a, idx):
    return jax.vmap(lambda ab, ib: ab[ib])(a, idx)

def rope(x, pos):
    rot = x.shape[-1] // 4
    half = rot // 2
    inv = ROPE_THETA ** (-jnp.arange(half, dtype=jnp.float32) * 2.0 / rot)
    ang = pos.astype(jnp.float32)[:, None] * inv[None, :]
    cos = jnp.cos(ang)[:, None, :]
    sin = jnp.sin(ang)[:, None, :]
    xf = x.astype(jnp.float32)
    x1, x2 = xf[..., :half], xf[..., half:rot]
    out = jnp.concatenate([x1 * cos - x2 * sin, x2 * cos + x1 * sin, xf[..., rot:]], -1)
    return out.astype(x.dtype)

def chunk_mixer(pa, ln_g, ln_b, ws, bs):
    z = jax.nn.gelu(pa)
    u, v = z[..., :A_W], z[..., A_W:]
    v = layer_norm(v, ln_g, ln_b)
    B, S, _ = v.shape
    n = -(-S // CHUNK)
    vp = jnp.pad(v, ((0, 0), (0, n * CHUNK - S), (0, 0))).reshape(B, n, CHUNK, A_G, A_C)
    s = jnp.einsum('gts,bnsgc->bntgc', jnp.tril(ws), vp) + bs.T[:, :, None]
    s = s.reshape(B, n * CHUNK, A_W)[:, :S]
    return u * s, v

def rwkv_scan(S0, r, w, k, v, kk, a):
    def step(St, inp):
        r_t, w_t, k_t, v_t, kk_t, a_t = inp
        sa = jnp.einsum('bhij,bhj->bhi', St, kk_t)
        St = St * w_t[:, :, None, :] - sa[..., None] * (kk_t * a_t)[:, :, None, :] + v_t[..., None] * k_t[:, :, None, :]
        return St, jnp.einsum('bhij,bhj->bhi', St, r_t)
    xs = tuple(jnp.moveaxis(t, 1, 0) for t in (r, w, k, v, kk, a))
    S_last, ys = lax.scan(step, S0, xs)
    return jnp.moveaxis(ys, 0, 1), S_last

def rwkv_mixer(pb, S0, shift0, mu, w0, wB, a0, aB, gB, k_k, k_a, r_k, gn_g, gn_b):
    B, S, _ = pb.shape
    prev = jnp.concatenate([shift0[:, None].astype(pb.dtype), pb[:, :-1]], 1)
    pm = (pb + (prev - pb) * mu).astype(jnp.float32)
    r, w_lo, k, v, a_lo, g_lo = split_cols(pm, [B_W, W_LORA, B_W, B_W, A_LORA, G_LORA])
    w = -jax.nn.softplus(-(w0 + jnp.tanh(w_lo) @ wB)) - 0.5
    decay = jnp.exp(-jnp.exp(w))
    a = jax.nn.sigmoid(a0 + a_lo @ aB)
    g = jax.nn.sigmoid(g_lo) @ gB
    hs = lambda t: t.reshape(B, S, HB, NB)
    kk = hs(k * k_k)
    kk = kk * lax.rsqrt(jnp.sum(kk * kk, -1, keepdims=True) + 1e-12)
    k = k * (1.0 + (a - 1.0) * k_a)
    r, k, v, a, decay = hs(r), hs(k), hs(v), hs(a), hs(decay)
    y, S_last = rwkv_scan(S0.astype(jnp.float32), r, decay, k, v, kk, a)
    mean = jnp.mean(y, -1, keepdims=True)
    var = jnp.mean(jnp.square(y - mean), -1, keepdims=True)
    y = ((y - mean) * lax.rsqrt(var + GN_EPS)).reshape(B, S, B_W) * gn_g + gn_b
    y = y + (jnp.sum(r * k * r_k, -1, keepdims=True) * v).reshape(B, S, B_W)
    y = y * g
    return y.astype(pb.dtype), S_last.astype(pb.dtype), pb[:, -1]

def causal_conv(x, buf, w, b):
    S = x.shape[1]
    xc = jnp.concatenate([buf.astype(x.dtype), x], 1)
    y = b + xc[:, 0:S] * w[0]
    for j in range(1, CONV_W):
        y = y + xc[:, j:j + S] * w[j]
    return y, xc[:, S:]

def lru_combine(e1, e2):
    a1, b1 = e1
    a2, b2 = e2
    return a1 * a2, a2 * b1 + b2

def rg_lru(x, h0, reset, wx, bx, wa, ba, lam):
    B, S, _ = x.shape
    xb = x.reshape(B, S, NBLK, BW)
    gx = jax.nn.sigmoid(jnp.einsum('bsnc,ncd->bsnd', xb, wx).reshape(B, S, C_W) + bx)
    ga = jax.nn.sigmoid(jnp.einsum('bsnc,ncd->bsnd', xb, wa).reshape(B, S, C_W) + ba)
    log_a = LRU_C * ga * jax.nn.log_sigmoid(lam)
    a = jnp.exp(log_a)
    mult = jnp.sqrt(-jnp.expm1(2.0 * log_a))
    mult = jnp.where(reset[None, :, None], 1.0, mult)
    bterm = x * gx * mult
    bterm = bterm.at[:, 0].add(a[:, 0] * h0)
    _, h = lax.associative_scan(lru_combine, (a, bterm), axis=1)
    return h, h[:, -1]

def lru_mixer(pc, h0, conv0, reset, conv_w, conv_b, wx, bx, wa, ba, lam):
    gate_pre, xin = split_cols(pc, [C_W, C_W])
    xconv, conv_new = causal_conv(xin, conv0, conv_w, conv_b)
    h, h_last = rg_lru(xconv.astype(jnp.float32), h0.astype(jnp.float32), reset, wx, bx, wa, ba, lam)
    y = h * jax.nn.gelu(gate_pre.astype(jnp.float32))
    return y.astype(pc.dtype), h_last.astype(pc.dtype), conv_new

def indexer_scores(qi, wi, ki):
    s = jax.nn.relu(jnp.einsum('bthd,bld->bthl', qi, ki).astype(jnp.float32))
    return jnp.einsum('bthl,bth->btl', s, wi.astype(jnp.float32) * (H_I ** -0.5 * D_I ** -0.5))

def gqa_attend(q, kg, vg, valid):
    B, T = q.shape[0], q.shape[1]
    qg = q.reshape(B, T, N_KV, H_D // N_KV, HD)
    logits = jnp.einsum('btkgd,btnkd->btkgn', qg, kg).astype(jnp.float32) * (HD ** -0.5)
    logits = jnp.where(valid[:, :, None, None, :], logits, -jnp.inf)
    p = jax.nn.softmax(logits, -1).astype(vg.dtype)
    return jnp.einsum('btkgn,btnkd->btkgd', p, vg).reshape(B, T, H_D * HD)

def dsa_prompt(q, k, v, qi, ki, wi):
    B, S = q.shape[0], q.shape[1]
    topk = min(TOPK_MAX, S // 4)
    key_pos = jnp.arange(S)

    def block(i):
        t0 = i * Q_BLOCK
        sl = lambda t: lax.dynamic_slice_in_dim(t, t0, Q_BLOCK, axis=1)
        qpos = t0 + jnp.arange(Q_BLOCK)
        score = indexer_scores(sl(qi), sl(wi), ki)
        score = jnp.where((key_pos[None, :] <= qpos[:, None])[None], score, -jnp.inf)
        _, idx = lax.top_k(score, topk)
        valid = idx <= qpos[None, :, None]
        return gqa_attend(sl(q), gather_rows(k, idx), gather_rows(v, idx), valid)

    out = lax.map(block, jnp.arange(S // Q_BLOCK))
    return jnp.moveaxis(out, 0, 1).reshape(B, S, H_D * HD)

def dsa_sample(q, k_new, v_new, qi, ki_new, wi, pool_k, pool_v, pool_ki, page_table):
    B, T = q.shape[0], q.shape[1]
    past = page_table.shape[1] * PAGE_SIZE
    L = past + T
    topk = min(TOPK_MAX, L // 4)
    ki_past = pool_ki[page_table].reshape(B, past, D_I)
    ki_all = jnp.concatenate([ki_past.astype(ki_new.dtype), ki_new], 1)
    qpos = past + jnp.arange(T)
    score = indexer_scores(qi, wi, ki_all)
    score = jnp.where(jnp.arange(L)[None, None, :] <= qpos[None, :, None], score, -jnp.inf)
    _, idx = lax.top_k(score, topk)
    valid = idx <= qpos[None, :, None]
    in_past = (idx < past)[..., None, None]
    pidx = jnp.minimum(idx, past - 1)
    phys = jnp.take_along_axis(page_table, (pidx // PAGE_SIZE).reshape(B, -1), axis=1).reshape(idx.shape)
    off = pidx % PAGE_SIZE
    nidx = jnp.clip(idx - past, 0, T - 1)
    kg = jnp.where(in_past, pool_k[phys, off].astype(k_new.dtype), gather_rows(k_new, nidx))
    vg = jnp.where(in_past, pool_v[phys, off].astype(v_new.dtype), gather_rows(v_new, nidx))
    return gqa_attend(q, kg, vg, valid)

def dsa_mixer(pd, pos, attend):
    B, S, _ = pd.shape
    q, k, v, qi, ki, wi = split_cols(pd, [H_D * HD, N_KV * HD, N_KV * HD, H_I * D_I, D_I, H_I])
    q = rope(q.reshape(B, S, H_D, HD), pos)
    k = rope(k.reshape(B, S, N_KV, HD), pos)
    v = v.reshape(B, S, N_KV, HD)
    qi = rope(qi.reshape(B, S, H_I, D_I), pos)
    ki = rope(ki[:, :, None, :], pos)[:, :, 0]
    return attend(q, k, v, qi, ki, wi), k, v, ki

def cross_attend(h, mk, mv, wq, wo):
    B, S, _ = h.shape
    q = (h @ wq).reshape(B, S, XH, XHD)
    logits = jnp.einsum('bshd,bmhd->bhsm', q, mk).astype(jnp.float32) * (XHD ** -0.5)
    p = jax.nn.softmax(logits, -1).astype(mv.dtype)
    return jnp.einsum('bhsm,bmhd->bshd', p, mv).reshape(B, S, XH * XHD) @ wo

def swiglu(h, wg, wu, wd):
    return (jax.nn.silu(h @ wg) * (h @ wu)) @ wd

def memory_kv(mem, norm_mem, w_xk, w_xv):
    B, M, _ = mem.shape
    ks, vs = [], []
    for layer in range(DEPTH):
        m = rms_norm(mem, norm_mem[layer])
        ks.append((m @ w_xk[layer]).reshape(B, M, XH, XHD))
        vs.append((m @ w_xv[layer]).reshape(B, M, XH, XHD))
    return jnp.stack(ks, 0), jnp.stack(vs, 0)

def trunk(x, pos0, rwkv_s0, rwkv_shift0, lru_h0, lru_conv0, mem_k, mem_v, attend, P):
    B, S, _ = x.shape
    pos = pos0 + jnp.arange(S, dtype=jnp.int32)
    reset = pos == 0
    chunk_v, rwkv_s, rwkv_sh, lru_h, lru_cv, att_k, att_v, att_ki = [], [], [], [], [], [], [], []
    for layer in range(DEPTH):
        j = layer // 2
        h = rms_norm(x, P['norm_mix'][layer])
        if layer % 2 == 0:
            pa, pb = split_cols(h @ P['e_w_in'][j], [2 * A_W, P_B])
            ya, v_rows = chunk_mixer(pa, P['a_ln_g'][j], P['a_ln_b'][j], P['a_ws'][j], P['a_bs'][j])
            yb, s_new, sh_new = rwkv_mixer(pb, rwkv_s0[j], rwkv_shift0[j], P['b_mu'][j], P['b_w0'][j], P['b_wB'][j],
                                           P['b_a0'][j], P['b_aB'][j], P['b_gB'][j], P['b_kk'][j], P['b_ka'][j],
                                           P['b_rk'][j], P['b_gn_g'][j], P['b_gn_b'][j])
            mix = jnp.concatenate([ya, yb.astype(ya.dtype)], -1) @ P['e_w_out'][j]
            chunk_v.append(v_rows)
            rwkv_s.append(s_new)
            rwkv_sh.append(sh_new)
        else:
            pc, pd = split_cols(h @ P['o_w_in'][j], [2 * C_W, P_D])
            yc, h_last, conv_new = lru_mixer(pc, lru_h0[j], lru_conv0[j], reset, P['c_conv_w'][j], P['c_conv_b'][j],
                                             P['c_wx'][j], P['c_bx'][j], P['c_wa'][j], P['c_ba'][j], P['c_lambda'][j])
            yd, k, v, ki = dsa_mixer(pd, pos, functools.partial(attend, j))
            mix = jnp.concatenate([yc, yd.astype(yc.dtype)], -1) @ P['o_w_out'][j]
            lru_h.append(h_last)
            lru_cv.append(conv_new)
            att_k.append(k)
            att_v.append(v)
            att_ki.append(ki)
        x = x + mix
        h = rms_norm(x, P['norm_x'][layer])
        x = x + cross_attend(h, mem_k[layer], mem_v[layer], P['w_xq'][layer], P['w_xo'][layer])
        h = rms_norm(x, P['norm_ffn'][layer])
        x = x + swiglu(h, P['w_ff_gate'][layer], P['w_ff_up'][layer], P['w_ff_down'][layer])
    y = rms_norm(x, P['norm_final'])
    st = lambda l: jnp.stack(l, 0)
    return y, st(chunk_v), st(rwkv_s), st(rwkv_sh), st(lru_h), st(lru_cv), st(att_k), st(att_v), st(att_ki)

def setup_inputs(seed: int = 0) -> dict:
    key = jax.random.key(seed)
    ks = iter(jax.random.split(key, 80))
    f32 = jnp.float32

    def nrm(shape, scale=1.0):
        return jax.random.normal(next(ks), shape, f32) * scale

    def gain(shape):
        return 1.0 + 0.02 * jax.random.normal(next(ks), shape, f32)

    n_pages = PAST_LEN // PAGE_SIZE
    n_used = DEC_BATCH * n_pages
    n_pool = n_used + max(1, n_used // 4)
    page_table = jax.random.permutation(next(ks), n_pool)[:n_used].reshape(DEC_BATCH, n_pages).astype(jnp.int32)
    lam_p = jax.random.uniform(next(ks), (N_ODD, C_W), f32, 0.9, 0.999)
    return {
        'x_prompt': nrm((BATCH, SEQ, D_MODEL)),
        'x_sample': nrm((DEC_BATCH, DEC_SEQ, D_MODEL)),
        'mem_prompt': nrm((BATCH, MEM, D_MODEL)),
        'state_rwkv': nrm((N_EVEN, DEC_BATCH, HB, NB, NB), 0.5),
        'state_rwkv_shift': nrm((N_EVEN, DEC_BATCH, P_B)),
        'state_lru_h': nrm((N_ODD, DEC_BATCH, C_W), 0.5),
        'state_lru_conv': nrm((N_ODD, DEC_BATCH, CONV_W - 1, C_W)),
        'cache_attn_k': nrm((N_ODD, n_pool, PAGE_SIZE, N_KV, HD)),
        'cache_attn_v': nrm((N_ODD, n_pool, PAGE_SIZE, N_KV, HD)),
        'cache_attn_kidx': nrm((N_ODD, n_pool, PAGE_SIZE, D_I)),
        'cache_mem_k': nrm((DEPTH, DEC_BATCH, MEM, XH, XHD)),
        'cache_mem_v': nrm((DEPTH, DEC_BATCH, MEM, XH, XHD)),
        'page_table': page_table,
        'norm_mix': gain((DEPTH, D_MODEL)),
        'norm_x': gain((DEPTH, D_MODEL)),
        'norm_mem': gain((DEPTH, D_MODEL)),
        'norm_ffn': gain((DEPTH, D_MODEL)),
        'norm_final': gain((D_MODEL,)),
        'w_xq': nrm((DEPTH, D_MODEL, XH * XHD), D_MODEL ** -0.5),
        'w_xk': nrm((DEPTH, D_MODEL, XH * XHD), D_MODEL ** -0.5),
        'w_xv': nrm((DEPTH, D_MODEL, XH * XHD), D_MODEL ** -0.5),
        'w_xo': nrm((DEPTH, XH * XHD, D_MODEL), (XH * XHD) ** -0.5),
        'w_ff_gate': nrm((DEPTH, D_MODEL, D_FF), D_MODEL ** -0.5),
        'w_ff_up': nrm((DEPTH, D_MODEL, D_FF), D_MODEL ** -0.5),
        'w_ff_down': nrm((DEPTH, D_FF, D_MODEL), D_FF ** -0.5),
        'e_w_in': nrm((N_EVEN, D_MODEL, P_EVEN), D_MODEL ** -0.5),
        'e_w_out': nrm((N_EVEN, A_W + B_W, D_MODEL), (A_W + B_W) ** -0.5),
        'a_ln_g': gain((N_EVEN, A_W)),
        'a_ln_b': nrm((N_EVEN, A_W), 0.02),
        'a_ws': nrm((N_EVEN, A_G, CHUNK, CHUNK), CHUNK ** -0.5),
        'a_bs': gain((N_EVEN, A_G, CHUNK)),
        'b_mu': jax.random.uniform(next(ks), (N_EVEN, P_B), f32),
        'b_w0': jax.random.uniform(next(ks), (N_EVEN, B_W), f32, -5.0, -1.0),
        'b_wB': nrm((N_EVEN, W_LORA, B_W), 0.1),
        'b_a0': nrm((N_EVEN, B_W), 0.1),
        'b_aB': nrm((N_EVEN, A_LORA, B_W), 0.1),
        'b_gB': nrm((N_EVEN, G_LORA, B_W), G_LORA ** -0.5),
        'b_kk': 1.0 + nrm((N_EVEN, B_W), 0.1),
        'b_ka': 1.0 + nrm((N_EVEN, B_W), 0.1),
        'b_rk': nrm((N_EVEN, HB, NB), 0.1),
        'b_gn_g': gain((N_EVEN, B_W)),
        'b_gn_b': nrm((N_EVEN, B_W), 0.02),
        'o_w_in': nrm((N_ODD, D_MODEL, P_ODD), D_MODEL ** -0.5),
        'o_w_out': nrm((N_ODD, C_W + H_D * HD, D_MODEL), (C_W + H_D * HD) ** -0.5),
        'c_conv_w': nrm((N_ODD, CONV_W, C_W), CONV_W ** -0.5),
        'c_conv_b': nrm((N_ODD, C_W), 0.02),
        'c_wx': nrm((N_ODD, NBLK, BW, BW), BW ** -0.5),
        'c_bx': nrm((N_ODD, C_W), 0.02),
        'c_wa': nrm((N_ODD, NBLK, BW, BW), BW ** -0.5),
        'c_ba': nrm((N_ODD, C_W), 0.02),
        'c_lambda': jnp.log(lam_p) - jnp.log1p(-lam_p),
    }

def reference(x_prompt, x_sample, mem_prompt, state_rwkv, state_rwkv_shift, state_lru_h, state_lru_conv,
              cache_attn_k, cache_attn_v, cache_attn_kidx, cache_mem_k, cache_mem_v, page_table,
              norm_mix, norm_x, norm_mem, norm_ffn, norm_final,
              w_xq, w_xk, w_xv, w_xo, w_ff_gate, w_ff_up, w_ff_down,
              e_w_in, e_w_out, a_ln_g, a_ln_b, a_ws, a_bs,
              b_mu, b_w0, b_wB, b_a0, b_aB, b_gB, b_kk, b_ka, b_rk, b_gn_g, b_gn_b,
              o_w_in, o_w_out, c_conv_w, c_conv_b, c_wx, c_bx, c_wa, c_ba, c_lambda):
    P = dict(norm_mix=norm_mix, norm_x=norm_x, norm_ffn=norm_ffn, norm_final=norm_final,
             w_xq=w_xq, w_xo=w_xo, w_ff_gate=w_ff_gate, w_ff_up=w_ff_up, w_ff_down=w_ff_down,
             e_w_in=e_w_in, e_w_out=e_w_out, a_ln_g=a_ln_g, a_ln_b=a_ln_b, a_ws=a_ws, a_bs=a_bs,
             b_mu=b_mu, b_w0=b_w0, b_wB=b_wB, b_a0=b_a0, b_aB=b_aB, b_gB=b_gB, b_kk=b_kk, b_ka=b_ka,
             b_rk=b_rk, b_gn_g=b_gn_g, b_gn_b=b_gn_b,
             o_w_in=o_w_in, o_w_out=o_w_out, c_conv_w=c_conv_w, c_conv_b=c_conv_b,
             c_wx=c_wx, c_bx=c_bx, c_wa=c_wa, c_ba=c_ba, c_lambda=c_lambda)
    dt = x_prompt.dtype
    bp = x_prompt.shape[0]

    p_mem_k, p_mem_v = memory_kv(mem_prompt, norm_mem, w_xk, w_xv)

    def attend_prompt(j, q, k, v, qi, ki, wi):
        return dsa_prompt(q, k, v, qi, ki, wi)

    (y_prompt, _, p_rwkv_state, p_rwkv_shift, p_lru_h, p_lru_conv,
     p_attn_k, p_attn_v, p_attn_kidx) = trunk(
        x_prompt, 0,
        jnp.zeros((N_EVEN, bp, HB, NB, NB), dt), jnp.zeros((N_EVEN, bp, P_B), dt),
        jnp.zeros((N_ODD, bp, C_W), dt), jnp.zeros((N_ODD, bp, CONV_W - 1, C_W), dt),
        p_mem_k, p_mem_v, attend_prompt, P)

    def attend_sample(j, q, k, v, qi, ki, wi):
        return dsa_sample(q, k, v, qi, ki, wi, cache_attn_k[j], cache_attn_v[j], cache_attn_kidx[j], page_table)

    (y_sample, s_chunk_v, s_rwkv_state, s_rwkv_shift, s_lru_h, s_lru_conv,
     s_attn_k, s_attn_v, s_attn_kidx) = trunk(
        x_sample, PAST_LEN, state_rwkv, state_rwkv_shift, state_lru_h, state_lru_conv,
        cache_mem_k, cache_mem_v, attend_sample, P)

    return (y_prompt, y_sample,
            p_rwkv_state, p_rwkv_shift, p_lru_h, p_lru_conv, p_attn_k, p_attn_v, p_attn_kidx, p_mem_k, p_mem_v,
            s_chunk_v, s_rwkv_state, s_rwkv_shift, s_lru_h, s_lru_conv, s_attn_k, s_attn_v, s_attn_kidx)


_drawn_inputs = setup_inputs


def setup_inputs(seed=0):
    import zlib

    import numpy as np

    out = dict(_drawn_inputs(seed))
    spreads = {}
    factors = {'norm_x': 8.0,
     'norm_mem': 2.899,
     'norm_ffn': 2.83,
     'norm_final': 8.293,
     'a_ln_g': 2.739,
     'a_ln_b': 2.82,
     'a_bs': 4.289,
     'b_gn_g': 5.485,
     'b_gn_b': 3.755,
     'c_bx': 7.209,
     'c_ba': 8.0,
     'cache_attn_k': 5.078,
     'cache_attn_v': 4.002,
     'cache_attn_kidx': 4.232}
    for name, (base, spread) in spreads.items():
        noise = np.random.default_rng([zlib.crc32(name.encode()), seed]).standard_normal(out[name].shape)
        drawn = base * np.exp(spread * noise) if base else spread * noise
        out[name] = __import__('jax').numpy.asarray(drawn.astype(out[name].dtype))
    for name, factor in factors.items():
        out[name] = (out[name] * factor).astype(out[name].dtype)
    return out
```

```python
from contextlib import ExitStack

import numpy as np

import concourse.bass as bass
from concourse import mybir

ALU = mybir.AluOpType
ACT = mybir.ActivationFunctionType
F32 = mybir.dt.float32
I32 = mybir.dt.int32
AX_X = mybir.AxisListType.X
ds = bass.ds

P = 128
D = 1024
KT = D // P
TP, NS, LS = 512, 8, 8
TS = NS * LS
T = TP + TS
HT = T // 2
EPS = 1e-6
GN_EPS = 64e-5
PAST, PAGE, NPG = 2048, 128, 16
MEM = 256
XH, XHD = 4, 256
DFF = 2816
FT = DFF // P
AW = 512
WT = AW // P
A_G = 4
NCH, CH = 4, 128
RC = 64
NRC = TP // RC
LEVELS = 6
SLOTS = 4
SLOT = 1408
DECAY = float(np.exp(-0.5))
TOPK_P, TOPK_S = 128, 256
LK = PAST + LS
BIG = 1e30
TAKEN = -3e38
EW_T, OW_T = 22, 17

CREDIT = 1
CREDITED = ("c_yout", "s_read", "s_smm", "x_outmm", "y_logits", "x_p", "y_p",
            "y_out", "x_out", "x_turned", "silu", "p_logits", "p_masked", "p_pt", "p_out",
            "p_turned", "p_outmm", "t_sum", "u_outmm", "u_exp", "u_out", "u_turned", "u_logits", "x_logits")

PCOL = {}
_n = 0
for _name, _w in (("mix0", 8), ("mix1", 8), ("x0", 8), ("x1", 8), ("mem0", 8), ("mem1", 8), ("ffn0", 8), ("ffn1", 8),
                  ("final", 8), ("ln_g", 4), ("ln_b", 4), ("mu", 14), ("w0", 4), ("a0", 4), ("k_k", 4), ("k_a", 4),
                  ("r_k", 4), ("gn_g", 4), ("gn_b", 4), ("conv_w", 16), ("conv_b", 4), ("bx", 4), ("ba", 4),
                  ("lam", 4)):
    PCOL[_name] = (_n, _w)
    _n += _w
NPAR = _n


def shape_constants():
    c = {}
    i = np.arange(P)
    f = lambda m: np.ascontiguousarray(m, np.float32)
    head = i // 64
    same = head[:, None] == head[None, :]
    c["ident"] = f(np.eye(P))
    c["heads"] = f(same)
    c["upper"] = f(i[:, None] <= i[None, :])
    s, t = i[:, None] % 64, i[None, :] % 64
    c["strict"] = f(same & (s < t))
    c["incl"] = f((s <= t)[:, :64])
    seq = same & (s // LS == t // LS)
    c["strict_s"] = f(seq & (s < t))
    c["incl_s"] = f(((s // LS == t // LS) & (s <= t))[:, :64])
    for l in range(LEVELS):
        b = 2 ** l
        c[f"level{l}"] = f(same & (s // (2 * b) == t // (2 * b)) & (s // b % 2 == 0) & (t // b % 2 == 1))
    c["causal"] = f(np.where(i[None, :] <= i[:, None], 0.0, -BIG))
    r64, r32 = np.zeros((P, P)), np.zeros((P, P))
    for o in range(P):
        d = o % 64
        if d < 8:
            r64[o + 8, o] = -1
        elif d < 16:
            r64[o - 8, o] = 1
        d = o % 32
        if d < 4:
            r32[o + 4, o] = -1
        elif d < 8:
            r32[o - 4, o] = 1
    c["rot64"], c["rot32"] = f(r64), f(r32)
    c["rep32"] = f(np.vstack([np.tile(np.eye(32), (1, 4)), np.zeros((96, P))]))
    c["rotrep"] = f(np.vstack([np.tile(r32[:32, :32], (1, 4)), np.zeros((96, P))]))
    e = np.zeros((P, 64))
    for h in range(8):
        e[32 + h, 8 * h:8 * h + 8] = 1
    c["spread"] = f(e)
    c["same_t"] = f(np.pad((i[:64, None] % 8 == i[None, :64] % 8), ((0, 64), (0, 0))))
    cn = np.zeros((P, LS))
    cn[:64] = np.where(np.arange(LS)[None, :] <= (i[:64] % LS)[:, None], 0.0, -BIG)
    c["causal_n"] = f(cn)
    eb = np.zeros((P, NS, 64))
    for b in range(NS):
        for r in range(64):
            eb[8 * b + r % 8, b, r] = 1
    c["mask_rows"] = f(eb.reshape(P, -1))
    c["seq_cols"] = f(np.broadcast_to((np.arange(64)[None, :] // LS == np.arange(NS)[:, None]).reshape(1, -1),
                                      (P, NS * 64)))
    c["seq_rows"] = f((i[:, None] % 64) // LS == np.arange(NS)[None, :])
    return c


def rotary(head, theta=500000.0):
    rot = head // 4
    half = rot // 2
    inv = (np.float32(theta) ** (-np.arange(half, dtype=np.float32) * np.float32(2.0) / np.float32(rot))).astype(np.float32)
    pos = np.concatenate([np.arange(TP), np.tile(PAST + np.arange(LS), NS)]).astype(np.float32)
    ang = (pos[:, None] * inv[None, :]).astype(np.float32)
    cos, sin = np.ones((P, T), np.float32), np.zeros((P, T), np.float32)
    for p in range(P):
        if p % head < rot:
            cos[p] = np.cos(ang[:, p % head % half])
            sin[p] = np.sin(ang[:, p % head % half])
    return cos, sin


CONST = shape_constants()
CCOL = {}
_n = 0
for _name, _a in CONST.items():
    CCOL[_name] = (_n, _a.shape[1])
    _n += _a.shape[1]
NCONST = _n


class Chain:

    def __init__(self, eng, sem):
        self.eng, self.sem, self.n, self.k = eng, sem, 0, 0

    def __call__(self, ins):
        ins.then_inc(self.sem, 1)
        self.n = self.n + 1
        self.k += 1
        self.eng.wait_ge(self.sem, self.n)

    def enter(self, i, per):
        self.base, self.per, self.k = self.n, per, 0
        self.n = i * per + self.base

    def leave(self, count):
        assert self.k == self.per, (self.k, self.per)
        self.n = self.base + count * self.per


class Gemm:

    blocks = 0
    outs = 0

    def __init__(self, src, n_out, kt, per_out=1):
        self.src, self.n_out, self.kt, self.per_out = src, n_out, kt, per_out
        self.g0, self.o0 = Gemm.blocks, Gemm.outs
        self.n = n_out * per_out
        Gemm.blocks += self.n
        Gemm.outs += n_out
        self.g1, self.o1 = Gemm.blocks, Gemm.outs

    def steps(self):
        at, left = 0, self.n
        if self.g0 == 0:
            yield 0, SLOTS, 1
            at, left = SLOTS, left - SLOTS
        if left // SLOTS:
            yield at, SLOTS, left // SLOTS
        at += left // SLOTS * SLOTS
        if left % SLOTS:
            yield at, left % SLOTS, 1


def build(nc, a, out):
    Gemm.blocks = Gemm.outs = 0
    ctx = ExitStack()
    sems = {}

    def S(name):
        if name not in sems:
            sems[name] = ctx.enter_context(nc.semaphore(name))
        return sems[name]

    with ctx:
        def sb(name, width):
            return ctx.enter_context(nc.sbuf_tensor(name, [P, width], F32))

        X = sb("X", KT * T)[:, :].rearrange("p (k t) -> p k t", k=KT)
        H = sb("H", KT * T)[:, :].rearrange("p (k t) -> p k t", k=KT)
        PJt = sb("PJ", EW_T * T)
        PJ = PJt[:, :].rearrange("p (k t) -> p k t", k=EW_T)
        PMt = sb("PM", 14 * T)
        PM = PMt[:, :].rearrange("p (k t) -> p k t", k=14)
        ring = sb("ring", SLOTS * SLOT)[:, :].rearrange("p (s n) -> p s n", s=SLOTS)
        cst = sb("cst", NCONST)
        par = sb("par", NPAR)
        ones = sb("ones", P)
        eps = sb("eps", 4)
        SC = sb("SC", 13720)
        ps = ctx.enter_context(nc.psum_tensor("ps", [P, 8, 512], F32))

        def C(name):
            o, w = CCOL[name]
            return cst[:, o:o + w]

        def G(name, k=0):
            o, _ = PCOL[name]
            return par[:, o + k:o + k + 1]

        def two(ap):
            return ap.rearrange("p (a b) -> p a b", a=2)

        def pair(b):
            return ps[:, b:b + 2, 0:HT]

        G_EIN = Gemm("w_ein", EW_T, KT)
        G_EOUT = Gemm("w_eout", KT, KT)
        layers = []
        G_MIX = [G_EIN, G_EOUT]
        plan = [G_EIN, G_EOUT]
        for l in range(2):
            if l == 1:
                G_OIN, G_OOUT = Gemm("w_oin", OW_T, KT), Gemm("w_oout", KT, KT)
                plan += [G_OIN, G_OOUT]
            g = dict(k=Gemm(f"w_xk{l}", KT, KT), v=Gemm(f"w_xv{l}", KT, KT), q=Gemm(f"w_xq{l}", KT, KT),
                     o=Gemm(f"w_xo{l}", KT, KT), gu=Gemm(f"w_gu{l}", 2 * FT, KT), d=Gemm(f"w_d{l}", KT, FT // 2, 2))
            layers.append(g)
            plan += list(g.values())

        def weights_in(sp, g):
            src = a[g.src]
            w = g.kt * P
            for at, k, reps in g.steps():
                def body(it):
                    for j in range(k):
                        b = g.g0 + at + j
                        if b >= SLOTS or reps > 1:
                            sp.wait_ge(S("block_done"), it * SLOTS + (b - SLOTS + 1))
                        sp.dma_start(ring[:, b % SLOTS, 0:w], src[it * SLOTS + (at + j)]).then_inc(S(f"slot{b % SLOTS}"), 16)
                if reps == 1:
                    body(0)
                else:
                    with sp.Fori(0, reps) as it:
                        body(it)

        def product(pe, g, rhs, free=None, norm=None):
            for at, k, reps in g.steps():
                def body(it):
                    for j in range(k):
                        b = g.g0 + at + j
                        o = g.o0 + (at + j) // g.per_out
                        sub = (at + j) % g.per_out
                        outs = SLOTS // g.per_out
                        pe.wait_ge(S(f"slot{b % SLOTS}"), it * 16 + 16 * (b // SLOTS + 1))
                        if sub == 0 and free:
                            free(it, o)
                        elif sub == 0 and (o >= 2 or reps > 1):
                            pe.wait_ge(S("out_taken"), it * outs + (o - 1))
                        for kt in range(g.kt):
                            if norm is not None and at == 0 and j == 0:
                                pe.wait_ge(S("normed"), KT * norm + kt + 1)
                            for h in range(2):
                                mm = nc.tensor.matmul(ps[:, 2 * (o % 2) + h, 0:HT], ring[:, b % SLOTS, kt * P:(kt + 1) * P],
                                                      rhs[:, sub * g.kt + kt, h * HT:(h + 1) * HT],
                                                      start=(sub == 0 and kt == 0),
                                                      stop=(sub == g.per_out - 1 and kt == g.kt - 1))
                        mm.then_inc(S("block_done"), 1)
                if reps == 1:
                    body(0)
                else:
                    with pe.Fori(0, reps) as it:
                        body(it)

        def take(dve, g, dst, add):
            for at, k, reps in g.steps():
                def body(it):
                    for j in range(k):
                        if (at + j) % g.per_out != g.per_out - 1:
                            continue
                        b = g.g0 + at + j
                        o = (at + j) // g.per_out
                        bank = 2 * ((g.o0 + o) % 2)
                        dve.wait_ge(S("block_done"), it * SLOTS + (b + 1))
                        d = dst[:, ds(it * (SLOTS // g.per_out) + o, 1), :].rearrange("p o (a b) -> p (o a) b", a=2)
                        if add:
                            nc.vector.tensor_tensor(d, pair(bank), d, ALU.add).then_inc(S("out_taken"), 1)
                        else:
                            nc.vector.tensor_copy(d, pair(bank)).then_inc(S("out_taken"), 1)
                if reps == 1:
                    body(0)
                else:
                    with dve.Fori(0, reps) as it:
                        body(it)

        SQ = PM[:, 0:KT, :]
        RMS = PM[:, KT, :]
        RINV = PM[:, KT + 1, :]

        def norm_act(act, n, x_ready):
            x_ready(act)
            for k in range(0, KT, 2):
                nc.scalar.activation(SQ[:, k, :], X[:, k, :], ACT.Square).then_inc(S("square_even"), 1)
            act.wait_ge(S("norm_sum"), n + 1)
            nc.scalar.activation(two(RMS), pair(4), ACT.Sqrt, bias=eps[:, 0:1], scale=1.0 / D).then_inc(S("norm_root"), 1)

        def norm_pe(pe, n):
            for k in range(KT):
                pe.wait_ge(S("square_odd" if k % 2 else "square_even"), 4 * n + k // 2 + 1)
                for h in range(2):
                    mm = nc.tensor.matmul(ps[:, 4 + h, 0:HT], ones[:, :], SQ[:, k, h * HT:(h + 1) * HT],
                                          start=(k == 0), stop=(k == KT - 1))
            mm.then_inc(S("norm_sum"), 1)

        def norm_dve(dve, n, x_ready, gain, link):
            x_ready(dve)
            for k in range(1, KT, 2):
                nc.vector.tensor_tensor(SQ[:, k, :], X[:, k, :], X[:, k, :], ALU.mult).then_inc(S("square_odd"), 1)
            dve.wait_ge(S("norm_root"), n + 1)
            link(nc.vector.reciprocal(RINV, RMS))
            for k in range(KT):
                nc.vector.scalar_tensor_tensor(H[:, k, :], X[:, k, :], G(gain, k), RINV, ALU.mult, ALU.mult)\
                  .then_inc(S("normed"), 1)

        def taken(g):
            return lambda eng: eng.wait_ge(S("out_taken"), g.o1)

        A_V = PJ[:, 4:8, :]
        A_U = PJ[:, 0:4, :]
        A_SQ = PM[:, 0:4, :]
        A_MU = PM[:, 4, :]
        A_VT = PMt[:, 5 * T:5 * T + 5 * 512].rearrange("p (c n) -> p c n", c=5)
        WS = SC[:, 0:512].rearrange("p (g t) -> p g t", g=4)
        WSS = SC[0:TS, 512:768].rearrange("p (g t) -> p g t", g=4)
        BS = SC[0:1, 768:1280]
        BSS = SC[0:1, 1280:1536]

        def bc(ap, n):
            return ap.unsqueeze(1).broadcast_to([ap.shape[0], n, ap.shape[1]])

        def a_act(act):
            taken(G_EIN)(act)
            nc.scalar.activation(A_V, A_V, ACT.Gelu_apprx_tanh).then_inc(S("a_gelu"), 1)
            nc.scalar.activation(A_U, A_U, ACT.Gelu_apprx_tanh).then_inc(S("a_gelu"), 1)
            act.wait_ge(S("a_products"), 2)
            nc.scalar.activation(two(A_MU), pair(6), ACT.Sqrt, bias=eps[:, 0:1], scale=1.0 / AW).then_inc(S("a_root"), 1)

        def column_sums(pe, src, bank, lhsT, n=4):
            for k in range(n):
                for h in range(2):
                    mm = nc.tensor.matmul(ps[:, bank + h, 0:HT], lhsT, src[:, k, h * HT:(h + 1) * HT],
                                          start=(k == 0), stop=(k == n - 1))
            return mm

        def a_pe(pe):
            pe.wait_ge(S("a_gelu"), 1)
            column_sums(pe, A_V, 4, ones[:, :]).then_inc(S("a_products"), 1)
            pe.wait_ge(S("a_squares"), 1)
            column_sums(pe, A_SQ, 6, ones[:, :]).then_inc(S("a_products"), 1)
            pe.wait_ge(S("a_normed"), 1)
            for c in range(5):
                n = CH if c < NCH else TS
                for g in range(4):
                    mm = nc.tensor.transpose(ps[0:n, c, g * P:(g + 1) * P], A_V[:, g, c * CH:c * CH + n], C("ident"))
            mm.then_inc(S("a_products"), 1)
            pe.wait_ge(S("a_rows"), 2)
            for g in range(4):
                for c in range(NCH):
                    o = ps[:, g, c * CH:(c + 1) * CH]
                    nc.tensor.matmul(o, A_VT[:, c, g * P:(g + 1) * P], WS[:, g, :], start=True, stop=False)
                    nc.tensor.matmul(o, ones[0:1, :], BS[:, g * CH:(g + 1) * CH], start=False, stop=True)
                o = ps[:, 4, g * TS:(g + 1) * TS]
                nc.tensor.matmul(o, A_VT[0:TS, 4, g * P:(g + 1) * P], WSS[:, g, :], start=True, stop=False)
                mm = nc.tensor.matmul(o, ones[0:1, :], BSS[:, g * TS:(g + 1) * TS], start=False, stop=True)
            mm.then_inc(S("a_products"), 1)

        def a_dve(dve, link):
            dve.wait_ge(S("a_products"), 1)
            link(nc.vector.tensor_scalar(two(A_MU), pair(4), 1.0 / AW, None, ALU.mult))
            dve.wait_ge(S("a_gelu"), 1)
            link(nc.vector.tensor_tensor(A_V, A_V, bc(A_MU, 4), ALU.subtract))
            nc.vector.tensor_tensor(A_SQ, A_V, A_V, ALU.mult).then_inc(S("a_squares"), 1)
            dve.wait_ge(S("a_root"), 1)
            link(nc.vector.reciprocal(A_MU, A_MU))
            link(nc.vector.tensor_tensor(A_V, A_V, bc(A_MU, 4), ALU.mult))
            for k in range(4):
                ins = nc.vector.tensor_scalar(A_V[:, k, :], A_V[:, k, :], G("ln_g", k), G("ln_b", k), ALU.mult, ALU.add)
                if k < 3:
                    link(ins)
            ins.then_inc(S("a_normed"), 1)
            dve.wait_ge(S("a_in"), 64)
            link(nc.vector.tensor_tensor(WS, WS, bc(C("upper"), 4), ALU.mult))
            link(nc.vector.tensor_tensor(WSS, WSS, bc(C("upper")[0:TS, 0:TS], 4), ALU.mult))
            dve.wait_ge(S("a_products"), 3)
            nc.vector.tensor_copy(A_VT[:, 0:4, :], ps[:, 0:4, :]).then_inc(S("a_rows"), 1)
            nc.vector.tensor_copy(A_VT[0:TS, 4, :], ps[0:TS, 4, :]).then_inc(S("a_rows"), 1)
            dve.wait_ge(S("a_products"), 4)
            dve.wait_ge(S("a_gelu"), 2)
            nc.vector.tensor_tensor(H[:, 0:4, 0:TP], A_U[:, :, 0:TP], ps[:, 0:4, :], ALU.mult).then_inc(S("a_out"), 1)
            nc.vector.tensor_tensor(H[:, 0:4, TP:T], A_U[:, :, TP:T],
                                    ps[:, 4, 0:4 * TS].rearrange("p (g t) -> p g t", g=4), ALU.mult).then_inc(S("a_out"), 1)

        PB = PJ[:, 8:22, :]
        R, K, V = PM[:, 0:4, :], PM[:, 4:8, :], PM[:, 8:12, :]
        WA, GL = PM[:, 12, :], PM[:, 13, :]
        KI, LC = PJ[:, 0:4, :], PJ[:, 4:8, :]
        KD, BI, GT = PJ[:, 8:12, :], PJ[:, 12:16, :], PJ[:, 16:20, :]
        RD = H[:, 4:8, :]
        LORA = SC[:, 1536:1536 + 1024]
        SH0 = SC[:, 2560:2560 + 14 * NS].rearrange("p (k b) -> p k b", k=14)
        RESET = SC[:, 2700:2700 + T]
        SHO = SC[:, 13584:13584 + 14 * 9].rearrange("p (k b) -> p k b", k=14)
        at = [0]

        def carve(n):
            v = SC[:, at[0]:at[0] + n]
            at[0] += n
            return v
        f4 = lambda ap: ap.rearrange("p (q n) -> p q n", q=4)
        XBt = carve(2048)
        XB = XBt.rearrange("p (x q n) -> p x q n", x=4, q=4)
        TM = carve(2048).rearrange("p (x q n) -> p x q n", x=4, q=4)
        ALt = carve(2560)
        AL = ALt.rearrange("p (l q n) -> p l q n", l=5, q=4)
        MTb, Mb, Yb, Gb, W1, Ub, Sb, AKK = (f4(carve(512)) for _ in range(8))
        ARt = carve(512).rearrange("p (q x n) -> p q x n", q=4, x=2)
        RDc = f4(carve(256))
        PC = carve(4)
        S0 = carve(NS * 256).rearrange("p (b q n) -> p b q n", b=NS, q=4)
        assert at[0] <= 13584, at
        W1b, Ub2, Vb2, Sbb = (f4(ALt[:, n * 512:(n + 1) * 512]) for n in range(4))

        def seqs(ap):
            return ap.rearrange("p k (b t) -> p k b t", b=NS)

        def b_pre_dve(dve, link):
            taken(G_EIN)(dve)
            dve.wait_ge(S("a_products"), 4)
            dve.wait_ge(S("b_in"), 80)
            PMa = PM[:, :, :]
            link(nc.vector.tensor_tensor(PMa[:, :, 1:TP], PB[:, :, 0:TP - 1], PB[:, :, 1:TP], ALU.subtract))
            link(nc.vector.tensor_scalar(PMa[:, :, 0:1], PB[:, :, 0:1], -1.0, None, ALU.mult))
            s, d = PB[:, :, TP:T], PMa[:, :, TP:T]
            for t in range(1, LS):
                nc.vector.tensor_tensor(seqs(d)[:, :, :, t], seqs(s)[:, :, :, t - 1], seqs(s)[:, :, :, t], ALU.subtract)\
                  .then_inc(S("b_shift"), 1)
            nc.vector.tensor_tensor(seqs(d)[:, :, :, 0], SH0, seqs(s)[:, :, :, 0], ALU.subtract).then_inc(S("b_shift"), 1)
            dve.wait_ge(S("b_shift"), LS)
            for k in (12, 13, 0, 1, 2, 3, 4, 5, 6, 7, 8, 9, 10, 11):
                nc.vector.scalar_tensor_tensor(PM[:, k, :], PM[:, k, :], G("mu", k), PB[:, k, :], ALU.mult, ALU.add)\
                  .then_inc(S("b_mixed"), 1)
            nc.vector.tensor_copy(SHO[:, :, 0:1], PB[:, :, TP - 1:TP]).then_inc(S("b_shift"), 1)
            nc.vector.tensor_copy(SHO[:, :, 1:9], seqs(PB[:, :, TP:T])[:, :, :, LS - 1]).then_inc(S("b_shift"), 1)
            dve.wait_ge(S("b_shift"), LS + 2)
            dve.wait_ge(S("b_mixed"), 14)
            dve.wait_ge(S("cv_stored"), 16)
            dve.wait_ge(S("b_sig"), 5)
            link(nc.vector.tensor_scalar(KD, KD, -DECAY, None, ALU.mult))
            for k in range(4):
                nc.vector.tensor_tensor_scan(LC[:, k, :], RESET, KD[:, k, :], 0.0, ALU.mult, ALU.add).then_inc(S("b_scan"), 1)
            dve.wait_ge(S("b_sig"), 9)
            dve.wait_ge(S("b_products"), 3)
            nc.vector.tensor_copy(GT, all_banks).then_inc(S("b_gate"), 1)
            for k in range(4):
                nc.vector.tensor_scalar(KI[:, k, :], K[:, k, :], G("k_k", k), None, ALU.mult).then_inc(S("b_kk"), 1)
            dve.wait_ge(S("b_kk"), 4)
            nc.vector.tensor_tensor(RD, KI, KI, ALU.mult).then_inc(S("b_kk"), 1)
            dve.wait_ge(S("b_root"), 1)
            link(nc.vector.reciprocal(RD, RD))
            link(nc.vector.tensor_tensor(KI, KI, RD, ALU.mult))
            for k in range(4):
                link(nc.vector.tensor_scalar(RD[:, k, :], BI[:, k, :], -1.0, G("k_a", k), ALU.add, ALU.mult))
                link(nc.vector.scalar_tensor_tensor(K[:, k, :], RD[:, k, :], 1.0, K[:, k, :], ALU.add, ALU.mult))
            link(nc.vector.tensor_tensor(BI, BI, KI, ALU.mult))
            dve.wait_ge(S("b_scan"), 4)
            nc.vector.tensor_tensor(KD, LC, KD, ALU.subtract).then_inc(S("b_before"), 1)
            dve.wait_ge(S("b_decay"), 1)
            link(nc.vector.tensor_tensor(KD, KD, KI, ALU.mult))
            dve.wait_ge(S("b_decay"), 2)
            link(nc.vector.tensor_tensor(BI, BI, RD, ALU.mult))
            link(nc.vector.tensor_tensor(KI, K, RD, ALU.mult))
            dve.wait_ge(S("b_decay"), 3)
            link(nc.vector.tensor_tensor(RD, R, LC, ALU.mult))

        all_banks = ps[:, :, 0:HT]

        def b_pre_act(act):
            act.wait_ge(S("b_mixed"), 2)
            nc.scalar.activation(WA[0:64, :], WA[0:64, :], ACT.Tanh).then_inc(S("b_tanh"), 1)
            nc.scalar.activation(GL, GL, ACT.Sigmoid).then_inc(S("b_sig"), 1)
            act.wait_ge(S("b_products"), 1)
            act.wait_ge(S("b_shift"), LS + 2)
            act.wait_ge(S("b_mixed"), 14)
            for k in range(4):
                nc.scalar.activation(two(KD[:, k, :]), pair(2 * k), ACT.Sigmoid, bias=G("w0", k)).then_inc(S("b_sig"), 1)
            act.wait_ge(S("b_products"), 2)
            for k in range(4):
                nc.scalar.activation(two(BI[:, k, :]), pair(2 * k), ACT.Sigmoid, bias=G("a0", k)).then_inc(S("b_sig"), 1)
            act.wait_ge(S("b_products"), 4)
            nc.scalar.activation(RD.rearrange("p k (a b) -> p (k a) b", a=2), all_banks, ACT.Sqrt, bias=eps[:, 2:3])\
              .then_inc(S("b_root"), 1)
            act.wait_ge(S("b_before"), 1)
            nc.scalar.activation(KD, KD, ACT.Exp).then_inc(S("b_decay"), 1)
            nc.scalar.activation(RD, LC, ACT.Exp, scale=-1.0).then_inc(S("b_decay"), 1)
            act.wait_ge(S("b_decay"), 2)
            nc.scalar.activation(LC, LC, ACT.Exp).then_inc(S("b_decay"), 1)

        def b_pre_pe(pe):
            def lora(lhs_rows, cols, rhs):
                for k in range(4):
                    for h in range(2):
                        mm = nc.tensor.matmul(ps[:, 2 * k + h, 0:HT], LORA[lhs_rows, cols + k * P:cols + (k + 1) * P],
                                              rhs[:, h * HT:(h + 1) * HT], start=True, stop=True)
                mm.then_inc(S("b_products"), 1)

            pe.wait_ge(S("a_out"), 2)
            pe.wait_ge(S("b_tanh"), 1)
            pe.wait_ge(S("b_mixed"), 2)
            lora(slice(0, 64), 0, WA[0:64, :])
            pe.wait_ge(S("b_sig"), 5)
            lora(slice(64, 128), 0, WA[64:128, :])
            pe.wait_ge(S("b_sig"), 9)
            lora(slice(0, 128), 512, GL)
            pe.wait_ge(S("b_kk"), 5)
            pe.wait_ge(S("b_gate"), 1)
            head_sums(RD).then_inc(S("b_products"), 1)

        def head_sums(src):
            for k in range(4):
                for h in range(2):
                    mm = nc.tensor.matmul(ps[:, 2 * k + h, 0:HT], C("heads"), src[:, k, h * HT:(h + 1) * HT],
                                          start=True, stop=True)
            return mm

        heads3 = C("heads").rearrange("p (h t) -> p h t", h=2)

        def banks(b):
            return f4(ps[:, b, :])

        def spread(dst, src, mask=None):
            d = dst.rearrange("p q (h t) -> p q h t", h=2)
            s = src.unsqueeze(2).broadcast_to([P, 4, 2, 64])
            m = heads3.unsqueeze(1).broadcast_to([P, 4, 2, 64]) if mask is None else mask
            return nc.vector.tensor_tensor(d, s, m, ALU.mult)

        def mm4(bank, lhsT, rhs, start=True, stop=True):
            for q in range(4):
                mm = nc.tensor.matmul(banks(bank)[:, q, :], lhsT[:, q, :], rhs[:, q, :], start=start, stop=stop)
            return mm

        STREAMS = [slice(0, 2), slice(2, 4)]

        def stream(b, s):
            return banks(b)[:, 0:2, :]

        def turn_pe(pe, n, k):
            pe.wait_ge(S("c_spread"), 6 * n + (6 * k + 4))
            for x in range(4):
                for q in range(4):
                    mm = nc.tensor.transpose(banks(x)[:, q, :], XB[:, x, q, :], C("ident"))
            mm.then_inc(S("c_turned"), 1)

        def chunk_pe(pe, n, levels, sample):
            W = lambda sem, v: pe.wait_ge(S(sem), v)
            mm4(4, XB[:, 1], XB[:, 0])
            W("c_yout", n + CREDIT)
            mm4(5, XB[:, 2], XB[:, 0])
            W("c_spread", 6 * n + 6)
            for q in range(4):
                o = ps[:, 6, q * P:(q + 1) * P]
                nc.tensor.matmul(o[:, 0:64], XB[:, 1, q, :], RDc[:, q, :], start=True, stop=True)
                mm = nc.tensor.matmul(o[:, 64:128], XB[:, 2, q, :], RDc[:, q, :], start=True, stop=True)
            mm.then_inc(S("c_products"), 1)
            W("c_mt0", n + 1)
            for q in range(4):
                mm = nc.tensor.transpose(banks(7)[:, q, :], MTb[:, q, :], C("ident"))
            mm.then_inc(S("c_mturned"), 1)
            W("c_m0", n + 1)
            W("c_tm", n + 1)
            W("c_masked", 3 * n + 3)
            for l in range(1, levels):
                k = 5 * n + l
                W("c_level", k)
                for s, qs in enumerate(STREAMS):
                    if l > 1:
                        W("c_inverse", 4 * k + (2 * s - 6))
                    for j, q in enumerate(range(4)[qs]):
                        mm = nc.tensor.matmul(stream(3 * s, s)[:, j, :], AL[:, l - 1, q, :], Mb[:, q, :], start=True, stop=True)
                    mm.then_inc(S("c_ymm"), 1)
                for s, qs in enumerate(STREAMS):
                    W("c_y", 2 * k + (s - 1))
                    for j, q in enumerate(range(4)[qs]):
                        nc.tensor.matmul(stream(3 * s + 1, s)[:, j, :], Yb[:, q, :], MTb[:, q, :], start=True, stop=True)
                    for j, q in enumerate(range(4)[qs]):
                        mm = nc.tensor.matmul(stream(3 * s + 2, s)[:, j, :], MTb[:, q, :], Yb[:, q, :], start=True, stop=True)
                    mm.then_inc(S("c_mm"), 1)
            W("c_inverse", 4 * (5 * n + levels - 1))
            mm4(6, TM[:, 0], MTb)
            mm4(7, AKK, TM[:, 3]).then_inc(S("c_w1mm"), 1)
            if sample:
                return
            W("c_g", n + 1)
            W("c_w1", n + 1)
            for q in range(4):
                nc.tensor.matmul(banks(4)[:, q, :], W1[:, q, :], Sb[:, q, :], start=True, stop=False)
                mm = nc.tensor.matmul(banks(4)[:, q, :], MTb[:, q, :], Gb[:, q, :], start=False, stop=True)
            mm.then_inc(S("c_umm"), 1)
            turn_pe(pe, n, 1)
            W("c_u", n + 1)
            for q in range(4):
                o = ps[:, 5, q * 64:(q + 1) * 64]
                nc.tensor.matmul(o, Sb[:, q, :], RDc[:, q, :], start=True, stop=False)
                nc.tensor.matmul(o, Ub[:, q, :], ARt[:, q, 0, :], start=False, stop=False)
                mm = nc.tensor.matmul(o, TM[:, 3, q, :], ARt[:, q, 1, :], start=False, stop=True)
            for q in range(4):
                nc.tensor.matmul(banks(7)[:, q, :], TM[:, 1, q, :], Ub[:, q, :], start=True, stop=False)
                mm = nc.tensor.matmul(banks(7)[:, q, :], TM[:, 2, q, :], TM[:, 3, q, :], start=False, stop=True)
            mm.then_inc(S("c_smm"), 1)

        def chunk_act(act, n, levels, sample):
            act.wait_ge(S("c_turned"), n + 1)
            nc.scalar.activation(TM.rearrange("p x q n -> p x (q n)"), ps[:, 0:4, :], ACT.Copy).then_inc(S("c_tm"), 1)
            for l in range(1, levels):
                for s, qs in enumerate(STREAMS):
                    act.wait_ge(S("c_ymm"), 2 * (5 * n + l) + (s - 1))
                    nc.scalar.activation(Yb[:, qs], stream(3 * s, s), ACT.Copy).then_inc(S("c_y"), 1)
            act.wait_ge(S("c_w1mm"), n + 1)
            nc.scalar.activation(W1, banks(6), ACT.Copy).then_inc(S("c_w1"), 1)
            if sample:
                return
            act.wait_ge(S("c_smm"), n + 1)
            nc.scalar.activation(KD[:, :, ds(n * 64, 64)], ps[:, 5, 0:256].rearrange("p (q t) -> p q t", q=4),
                                 ACT.Copy).then_inc(S("c_yout"), 1)

        def chunk_pool(pool, n, levels, sample):
            pool.wait_ge(S("c_at"), n + 1)
            for l in range(1, levels):
                nc.gpsimd.tensor_tensor(AL[:, l - 1], AT4, bc(C(f"level{l}"), 4), ALU.mult).then_inc(S("c_level"), 1)

        AT4 = Ub

        def spread_x(x, n, k):
            spread(XB[:, x], (KD, BI, KI, V)[x][:, :, ds(n * 64 + 64 * k, 64)]).then_inc(S("c_spread"), 1)

        def chunk_rest(n, k):
            nc.vector.tensor_copy(RDc, RD[:, :, ds(n * 64 + 64 * k, 64)]).then_inc(S("c_spread"), 1)
            nc.vector.tensor_copy(PC, LC[:, :, ds(n * 64 + (64 * k + 63), 1)].rearrange("p q o -> p (q o)"))\
              .then_inc(S("c_spread"), 1)

        def chunk_dve(dve, n, levels, sample, link):
            strict, incl = (C("strict_s"), C("incl_s")) if sample else (C("strict"), C("incl"))
            dve.wait_ge(S("c_products"), n + 1)
            nc.vector.tensor_tensor(AT4, banks(4), bc(strict, 4), ALU.mult).then_inc(S("c_at"), 1)
            dve.wait_ge(S("c_at"), n + 1)
            link(nc.vector.tensor_tensor(MTb, AT4, bc(C("level0"), 4), ALU.mult))
            nc.vector.tensor_tensor(MTb, bc(C("ident"), 4), MTb, ALU.subtract).then_inc(S("c_mt0"), 1)
            nc.vector.tensor_tensor(AKK, banks(5), bc(strict, 4), ALU.mult).then_inc(S("c_masked"), 1)
            for x in range(2):
                nc.vector.tensor_tensor(ARt[:, :, x, :], banks(6)[:, :, 64 * x:64 * x + 64], bc(incl, 4), ALU.mult)\
                  .then_inc(S("c_masked"), 1)
            dve.wait_ge(S("c_mturned"), n + 1)
            nc.vector.tensor_copy(Mb, banks(7)).then_inc(S("c_m0"), 1)
            for l in range(1, levels):
                if not sample and 2 <= l < 6:
                    spread_x(l - 2, n, 1)
                for s, qs in enumerate(STREAMS):
                    dve.wait_ge(S("c_mm"), 2 * (5 * n + l) + (s - 1))
                    nc.vector.tensor_tensor(MTb[:, qs], MTb[:, qs], stream(3 * s + 1, s), ALU.subtract).then_inc(S("c_inverse"), 1)
                    nc.vector.tensor_tensor(Mb[:, qs], Mb[:, qs], stream(3 * s + 2, s), ALU.subtract).then_inc(S("c_inverse"), 1)
            dve.wait_ge(S("c_w1mm"), n + 1)
            nc.vector.tensor_copy(Gb, banks(7)).then_inc(S("c_g"), 1)
            if sample:
                return
            dve.wait_ge(S("c_umm"), n + 1)
            nc.vector.tensor_scalar(Ub, banks(4), -1.0, None, ALU.mult).then_inc(S("c_u"), 1)
            dve.wait_ge(S("c_smm"), n + 1)
            link(nc.vector.tensor_tensor(Sb, Sb, banks(7), ALU.add))
            link(nc.vector.tensor_tensor(Sb, Sb, PC.unsqueeze(2).broadcast_to([P, 4, P]), ALU.mult))
            chunk_rest(n, 1)

        def sample_state_pe(pe):
            pe.wait_ge(S("c_g"), NRC + 1)
            pe.wait_ge(S("c_w1"), NRC + 1)
            for q in range(4):
                nc.tensor.matmul(ps[:, q, 0:P], MTb[:, q, :], Gb[:, q, :], start=True, stop=True)
                nc.tensor.matmul(ps[:, 4 + q, 0:64], TM[:, 3, q, :], ARt[:, q, 1, :], start=True, stop=True)
            with pe.Fori(0, NS) as b:
                pe.wait_ge(S("s_operands"), b * 2 + 2)
                for q in range(4):
                    nc.tensor.matmul(ps[:, q, 0:P], W1b[:, q, :], Sbb[:, q, :], start=False, stop=True,
                                     skip_group_check=True)
                    mm = nc.tensor.matmul(ps[:, 4 + q, ds(b * LS, LS)], Sbb[:, q, :], RDc[:, q, ds(b * LS, LS)],
                                          start=False, stop=True, skip_group_check=True)
                mm.then_inc(S("s_read"), 1)
            pe.wait_ge(S("c_u"), NRC + 1)
            for q in range(4):
                mm = nc.tensor.matmul(ps[:, 4 + q, 0:64], Ub[:, q, :], ARt[:, q, 0, :], start=False, stop=True,
                                      skip_group_check=True)
            mm.then_inc(S("s_ymm"), 1)
            with pe.Fori(0, NS) as b:
                pe.wait_ge(S("s_rows"), b * 2 + 2)
                for q in range(4):
                    nc.tensor.matmul(banks(0)[:, q, :], TM[:, 1, q, :], Ub2[:, q, :], start=True, stop=False)
                    mm = nc.tensor.matmul(banks(0)[:, q, :], TM[:, 2, q, :], Vb2[:, q, :], start=False, stop=True)
                mm.then_inc(S("s_smm"), 1)

        def sample_state_dve(dve, link):
            dve.wait_ge(S("c_w1"), NRC + 1)
            with dve.Fori(0, NS) as b:
                dve.wait_ge(S("s_read"), b + CREDIT)
                m = seq_cols[:, ds(b, 1), :].broadcast_to([P, 8, 64])
                nc.vector.tensor_tensor(W1b.rearrange("p q (h t) -> p (q h) t", h=2), W1.rearrange("p q (h t) -> p (q h) t", h=2),
                                        m, ALU.mult).then_inc(S("s_operands"), 1)
                spread(Sbb, S0[:, ds(b, 1), :, :].rearrange("p o q n -> p (o q) n")).then_inc(S("s_operands"), 1)
            dve.wait_ge(S("s_read"), NS + CREDIT)
            nc.vector.tensor_scalar(Ub, ps[:, 0:4, 0:P], -1.0, None, ALU.mult).then_inc(S("c_u"), 1)
            dve.wait_ge(S("c_u"), NRC + 1)
            dve.wait_ge(S("s_ymm"), 1)
            link(nc.vector.tensor_copy(KD[:, :, TP:T], ps[:, 4:8, 0:64]))
            with dve.Fori(0, NS) as b:
                link.enter(b, 2)
                dve.wait_ge(S("s_smm"), b + CREDIT)
                row = C("seq_rows")[:, ds(b, 1)]
                nc.vector.tensor_scalar(Ub2, Ub, row, None, ALU.mult).then_inc(S("s_rows"), 1)
                nc.vector.tensor_scalar(Vb2, TM[:, 3], row, None, ALU.mult).then_inc(S("s_rows"), 1)
                dve.wait_ge(S("s_smm"), b + 1 + CREDIT)
                sb_ = S0[:, ds(b, 1), :, :].rearrange("p o q n -> p (o q) n")
                for hh in range(2):
                    r = slice(64 * hh, 64 * hh + 64)
                    link(nc.vector.tensor_tensor(sb_[r], sb_[r], banks(0)[r, :, 64 * hh:64 * hh + 64], ALU.add))
                end = LC[:, :, ds(b * LS + (TP + LS - 1), 1)].broadcast_to([P, 4, 64])
                nc.vector.tensor_tensor(sb_, sb_, end, ALU.mult).then_inc(S("s_state"), 1)
            link.leave(NS)

        seq_cols = C("seq_cols").rearrange("p (b t) -> p b t", b=NS)

        def b_post_dve(dve, link):
            dve.wait_ge(S("b_products"), 5)
            flat = lambda v: v.rearrange("p k (a b) -> p (k a) b", a=2)
            link(nc.vector.scalar_tensor_tensor(flat(KD), all_banks, -1.0 / 64, flat(KD), ALU.mult, ALU.add))
            nc.vector.tensor_tensor(RD, KD, KD, ALU.mult).then_inc(S("b_ysq"), 1)
            dve.wait_ge(S("b_root"), 2)
            link(nc.vector.reciprocal(LC, LC))
            link(nc.vector.tensor_tensor(KD, KD, LC, ALU.mult))
            for k in range(4):
                link(nc.vector.tensor_scalar(KD[:, k, :], KD[:, k, :], G("gn_g", k), G("gn_b", k), ALU.mult, ALU.add))
            for k in range(4):
                nc.vector.scalar_tensor_tensor(LC[:, k, :], R[:, k, :], G("r_k", k), K[:, k, :], ALU.mult, ALU.mult)\
                  .then_inc(S("b_bonus"), 1)
            dve.wait_ge(S("b_products"), 7)
            link(nc.vector.tensor_tensor(flat(RD), all_banks, flat(V), ALU.mult))
            link(nc.vector.tensor_tensor(RD, RD, KD, ALU.add))
            nc.vector.tensor_tensor(RD, RD, GT, ALU.mult).then_inc(S("b_out"), 1)

        def b_post_pe(pe):
            pe.wait_ge(S("c_yout"), NRC + CREDIT)
            pe.wait_ge(S("s_state"), NS)
            head_sums(KD).then_inc(S("b_products"), 1)
            pe.wait_ge(S("b_ysq"), 1)
            head_sums(RD).then_inc(S("b_products"), 1)
            pe.wait_ge(S("b_root"), 2)
            pe.wait_ge(S("b_bonus"), 4)
            head_sums(LC).then_inc(S("b_products"), 1)

        def b_post_act(act):
            act.wait_ge(S("b_products"), 6)
            nc.scalar.activation(LC.rearrange("p k (a b) -> p (k a) b", a=2), all_banks, ACT.Sqrt, bias=eps[:, 1:2],
                                 scale=1.0 / 64).then_inc(S("b_root"), 1)

        MR = SC[:, 0:2048].rearrange("p (k m) -> p k m", k=KT)
        MSQ = SC[:, 2048:4096].rearrange("p (k m) -> p k m", k=KT)
        RM, RMI = SC[:, 4096:4352], SC[:, 4352:4608]
        MN = SC[:, 4608:6656].rearrange("p (k m) -> p k m", k=KT)
        MK = SC[:, 6656:8704].rearrange("p (k m) -> p k m", k=KT)
        MV = SC[:, 8704:10752].rearrange("p (j n) -> p j n", j=2)
        XQ = PJ[:, 0:8, :]
        SKt, SVt = PJt[:, 8 * T:8 * T + 4096], PMt[:, 0:4096]
        SKs = [SKt[:, 2048 * i:2048 * (i + 1)].rearrange("p (k m) -> p k m", k=KT) for i in range(2)]
        SVs = [SVt[:, 2048 * i:2048 * (i + 1)].rearrange("p (j n) -> p j n", j=2) for i in range(2)]
        XP = PMt[:, 4096:5120].rearrange("p (i m) -> p i m", i=4)
        XPT = PMt[:, 5120:6144].rearrange("p (j q) -> p j q", j=2)
        XQS = PMt[:, 6144:7168].rearrange("p (d q) -> p d q", d=2)
        XVS = PMt[:, 7168:7680].rearrange("p (j n) -> p j n", j=2)
        XST = PMt[:, 7680:7700]
        YQZ = [SC[:, 10752 + 256 * i:10752 + 256 * (i + 1)].rearrange("p (k c) -> p k c", k=KT) for i in range(2)]
        YP = [SC[0:32, 11264 + 256 * i:11264 + 256 * (i + 1)] for i in range(2)]
        YPT = [SC[:, 11776 + 64 * i:11776 + 64 * (i + 1)].rearrange("p (j c) -> p j c", j=2) for i in range(2)]
        YST = SC[0:32, 11904:11912]
        XSC = XHD ** -0.5

        def mem_act(act, l):
            act.wait_ge(S("mem_in"), 16 * (l + 1))
            nc.scalar.activation(MSQ, MR, ACT.Square).then_inc(S("m_square"), 1)
            act.wait_ge(S("m_sum"), l + 1)
            nc.scalar.activation(RM, ps[:, 6, 0:MEM], ACT.Sqrt, bias=eps[:, 0:1], scale=1.0 / D).then_inc(S("m_root"), 1)

        def mem_pe(pe, l):
            pe.wait_ge(S("m_square"), l + 1)
            for k in range(KT):
                mm = nc.tensor.matmul(ps[:, 6, 0:MEM], ones[:, :], MSQ[:, k, :], start=(k == 0), stop=(k == KT - 1))
            mm.then_inc(S("m_sum"), 1)

        def mem_dve(dve, l, link):
            dve.wait_ge(S("m_root"), l + 1)
            link(nc.vector.reciprocal(RMI, RM))
            for k in range(KT):
                nc.vector.scalar_tensor_tensor(MN[:, k, :], MR[:, k, :], G(f"mem{l}", k), RMI, ALU.mult, ALU.mult)\
                  .then_inc(S("m_normed"), 1)

        def memory_product(pe, g, keys):
            for at, k, reps in g.steps():
                def body(it):
                    for j in range(k):
                        b = g.g0 + at + j
                        o = g.o0 + at + j
                        pe.wait_ge(S(f"slot{b % SLOTS}"), it * 16 + 16 * (b // SLOTS + 1))
                        pe.wait_ge(S("out_taken"), it * SLOTS + (o - 1))
                        bank = ps[:, 2 * (o % 2), 0:MEM]
                        for half in range(1 if keys else 2):
                            for kt in range(KT):
                                w = ring[:, b % SLOTS, kt * P:(kt + 1) * P]
                                if keys:
                                    mm = nc.tensor.matmul(bank, w, MN[:, kt, :], start=(kt == 0), stop=(kt == KT - 1))
                                else:
                                    mm = nc.tensor.matmul(bank[:, half * P:(half + 1) * P], MN[:, kt, half * P:(half + 1) * P],
                                                          w, start=(kt == 0), stop=(kt == KT - 1))
                        mm.then_inc(S("block_done"), 1)
                assert k == SLOTS
                with pe.Fori(0, reps) as it:
                    body(it)

        def memory_take(dve, g, keys):
            for at, k, reps in g.steps():
                with dve.Fori(0, reps) as it:
                    for j in range(k):
                        b = g.g0 + at + j
                        dve.wait_ge(S("block_done"), it * SLOTS + (b + 1))
                        bank = ps[:, 2 * ((g.o0 + at + j) % 2), 0:MEM]
                        if keys:
                            d = MK[:, ds(it * SLOTS + (at + j), 1), :].rearrange("p o m -> p (o m)")
                            nc.vector.tensor_copy(d, bank).then_inc(S("out_taken"), 1)
                        else:
                            d = MV[:, :, ds(it * (SLOTS * P) + (at + j) * P, P)]
                            nc.vector.tensor_copy(d, bank.rearrange("p (j n) -> p j n", j=2)).then_inc(S("out_taken"), 1)

        def cross_pool(pool, l):
            for i in range(2):
                nc.gpsimd.memset(YQZ[i], 0.0).then_inc(S("zeroed"), 1)
            pool.wait_ge(S("zeroed"), 4 * l + 2)
            pool.wait_ge(S("out_taken"), layers[l]["q"].o1)
            with pool.Fori(0, XH) as h:
                n = h + 4 * l
                pool.wait_ge(S("x_logits"), n + CREDIT)
                nc.gpsimd.tensor_copy(XQS, XQ[:, ds(h * 2, 2), 0:TP]).then_inc(S("x_q"), 1)
                for i in range(2):
                    pool.wait_ge(S("y_logits"), h * 2 + max(8 * l + i - 1, 0) + CREDIT)
                    for hh in range(XH):
                        q = XQ[:, 2 * hh:2 * hh + 2, ds(h * (2 * LS) + (TP + i * LS), LS)]
                        nc.gpsimd.tensor_copy(YQZ[i][:, 2 * hh:2 * hh + 2, LS * hh:LS * hh + LS], q).then_inc(S("y_q"), 1)
                pool.wait_ge(S("x_outmm"), n + CREDIT)
                nc.gpsimd.tensor_copy(XVS, MV[:, :, ds(h * XHD, XHD)]).then_inc(S("x_v"), 1)

        def cross_pe(pe, l):
            def x_logits(h, k):
                n = h + (4 * l + k)
                pe.wait_ge(S("x_q"), n + 1)
                pe.wait_ge(S("x_p"), n * 4 + CREDIT)
                for i in range(4):
                    for d in range(2):
                        mm = nc.tensor.matmul(ps[:, i // 2, (i % 2) * MEM:(i % 2 + 1) * MEM], XQS[:, d, i * P:(i + 1) * P],
                                              MK[:, ds(h * 2 + (2 * k + d), 1), :].rearrange("p o m -> p (o m)"),
                                              start=(d == 0), stop=(d == 1))
                mm.then_inc(S("x_logits"), 1)

            def y_logits(h, i):
                m = h * 2 + (8 * l + i)
                pe.wait_ge(S("y_q"), m * 4 + 4)
                pe.wait_ge(S(f"sk{i}"), h * 16 + 16 * (4 * l + 1))
                pe.wait_ge(S("y_p"), m + CREDIT)
                pe.wait_ge(S("y_out"), h * 2 + 8 * l + CREDIT)
                for k in range(KT):
                    mm = nc.tensor.matmul(ps[0:32, 6, 0:MEM], YQZ[i][:, k, :], SKs[i][:, k, :],
                                          start=(k == 0), stop=(k == KT - 1))
                mm.then_inc(S("y_logits"), 1)

            def turn(h, last):
                n = h + 4 * l
                y_logits(h, 0)
                pe.wait_ge(S("x_pn"), n + 1)
                for j in range(2):
                    for i in range(4):
                        mm = nc.tensor.transpose(ps[:, 2 + j, i * P:(i + 1) * P], XP[:, i, j * P:(j + 1) * P], C("ident"))
                mm.then_inc(S("x_turned"), 1)
                if not last:
                    x_logits(h, 1)
                y_logits(h, 1)
                pe.wait_ge(S("x_v"), n + 1)
                pe.wait_ge(S("x_pt"), n + 1)
                pe.wait_ge(S("x_out"), n * 2 + CREDIT)
                for d in range(2):
                    for j in range(2):
                        mm = nc.tensor.matmul(ps[:, 4 + d, :], XVS[:, j, d * P:(d + 1) * P], XPT[:, j, :],
                                              start=(j == 0), stop=(j == 1))
                mm.then_inc(S("x_outmm"), 1)
                for i in range(2):
                    m = h * 2 + (8 * l + i)
                    pe.wait_ge(S("y_pn"), m + 1)
                    for j in range(2):
                        mm = nc.tensor.matmul(ps[:, 7, j * 32:(j + 1) * 32], YP[i][:, j * P:(j + 1) * P], C("ident")[0:32, 0:32],
                                              start=True, stop=True)
                    mm.then_inc(S("y_turned"), 1)
                    pe.wait_ge(S("y_pt"), m + 1)
                for i in range(2):
                    pe.wait_ge(S(f"sv{i}"), h * 16 + 16 * (4 * l + 1))
                    for d in range(KT):
                        for j in range(2):
                            mm = nc.tensor.matmul(ps[:, 7 - i, 256 + d * LS:256 + (d + 1) * LS],
                                                  SVs[i][:, j, d * P:(d + 1) * P],
                                                  YPT[i][:, j, (d // 2) * LS:(d // 2 + 1) * LS],
                                                  start=(j == 0), stop=(j == 1))
                    mm.then_inc(S("y_outmm"), 1)

            pe.wait_ge(S("out_taken"), layers[l]["q"].o1)
            x_logits(0, 0)
            with pe.Fori(0, XH - 1) as h:
                turn(h, False)
            turn(XH - 1, True)

        def cross_dve(dve, l, link):
            def x_maxima(n):
                dve.wait_ge(S("x_logits"), n + 1 + CREDIT)
                lg = ps[:, 0:2, :].rearrange("p a (c m) -> p (a c) m", c=2)
                link(nc.vector.tensor_reduce(XST[:, 0:4], lg, AX_X, ALU.max))
                nc.vector.tensor_scalar(XST[:, 4:8], XST[:, 0:4], -XSC, None, ALU.mult).then_inc(S("x_bias"), 1)

            def y_maxima(h, i):
                m = h * 2 + (8 * l + i)
                dve.wait_ge(S("y_logits"), m + 1 + CREDIT)
                link(nc.vector.tensor_reduce(YST[:, 4 * i:4 * i + 1], ps[0:32, 6, 0:MEM], AX_X, ALU.max))
                nc.vector.tensor_scalar(YST[:, 4 * i + 1:4 * i + 2], YST[:, 4 * i:4 * i + 1], -XSC, None, ALU.mult)\
                  .then_inc(S("y_bias"), 1)

            def turn(h, last):
                n = h + 4 * l
                dve.wait_ge(S("x_p"), n * 4 + 4 + CREDIT)
                link(nc.vector.reciprocal(XST[:, 12:16], XST[:, 8:12]))
                nc.vector.tensor_tensor(XP, XP, XST[:, 12:16].unsqueeze(2).broadcast_to([P, 4, MEM]), ALU.mult)\
                  .then_inc(S("x_pn"), 1)
                y_maxima(h, 0)
                dve.wait_ge(S("x_turned"), n + 1 + CREDIT)
                nc.vector.tensor_copy(XPT, ps[:, 2:4, :]).then_inc(S("x_pt"), 1)
                if not last:
                    x_maxima(n + 1)
                y_maxima(h, 1)
                for i in range(2):
                    m = h * 2 + (8 * l + i)
                    dve.wait_ge(S("y_p"), m + 1 + CREDIT)
                    link(nc.vector.reciprocal(YST[:, 4 * i + 3:4 * i + 4], YST[:, 4 * i + 2:4 * i + 3]))
                    nc.vector.tensor_scalar(YP[i], YP[i], YST[:, 4 * i + 3:4 * i + 4], None, ALU.mult).then_inc(S("y_pn"), 1)
                for i in range(2):
                    m = h * 2 + (8 * l + i)
                    dve.wait_ge(S("y_turned"), m + 1)
                    nc.vector.tensor_copy(YPT[i], ps[:, 7, 0:64].rearrange("p (j c) -> p j c", j=2)).then_inc(S("y_pt"), 1)
                for i in range(2):
                    m = h * 2 + (8 * l + i)
                    dve.wait_ge(S("y_outmm"), m + 1)
                    o = ps[:, 7 - i, 256:320].rearrange("p (k t) -> p k t", k=KT)
                    nc.vector.tensor_copy(H[:, :, ds(h * (2 * LS) + (TP + i * LS), LS)], o).then_inc(S("y_out"), 1)

            x_maxima(4 * l)
            with dve.Fori(0, XH - 1) as h:
                link.enter(h, 6)
                turn(h, False)
            link.leave(XH - 1)
            turn(XH - 1, True)

        def cross_act(act, l):
            def x_exp(h, k):
                n = h + (4 * l + k)
                act.wait_ge(S("x_bias"), n + 1)
                act.wait_ge(S("x_turned"), n + CREDIT)
                for i in range(4):
                    nc.scalar.activation(XP[:, i, :], ps[:, i // 2, (i % 2) * MEM:(i % 2 + 1) * MEM], ACT.Exp,
                                         bias=XST[:, 4 + i:5 + i], scale=XSC, accum_out=XST[:, 8 + i:9 + i])\
                      .then_inc(S("x_p"), 1)

            def y_exp(h, i):
                m = h * 2 + (8 * l + i)
                act.wait_ge(S("y_bias"), m + 1)
                nc.scalar.activation(YP[i], ps[0:32, 6, 0:MEM], ACT.Exp, bias=YST[:, 4 * i + 1:4 * i + 2], scale=XSC,
                                     accum_out=YST[:, 4 * i + 2:4 * i + 3]).then_inc(S("y_p"), 1)

            def turn(h, last):
                y_exp(h, 0)
                if not last:
                    x_exp(h, 1)
                y_exp(h, 1)
                act.wait_ge(S("x_outmm"), h + (4 * l + 1) + CREDIT)
                for d in range(2):
                    nc.scalar.activation(H[:, ds(h * 2 + d, 1), 0:TP].rearrange("p o t -> p (o t)"), ps[:, 4 + d, :], ACT.Copy)\
                      .then_inc(S("x_out"), 1)

            x_exp(0, 0)
            with act.Fori(0, XH - 1) as h:
                turn(h, False)
            turn(XH - 1, True)

        HG = PJ
        SGt = PMt[:, 0:2 * T].rearrange("p (j t) -> p j t", j=2)

        def gate_free(pe, l):
            g = layers[l]["gu"]

            def free(it, o):
                k = o - g.o0
                if k % 2 == 0:
                    pe.wait_ge(S("silu"), it * 2 + (FT * l + k // 2) + CREDIT)
                else:
                    pe.wait_ge(S("out_taken"), it * 4 + (o - 1))
            return free

        def silu_act(act, l):
            g = layers[l]["gu"]
            with act.Fori(0, FT // 2) as it:
                for j in range(2):
                    b = g.g0 + 2 * j
                    act.wait_ge(S("block_done"), it * 4 + (b + 1))
                    nc.scalar.activation(two(SGt[:, j, :]), pair(2 * ((g.o0 + 2 * j) % 2)), ACT.Silu).then_inc(S("silu"), 1)

        def hidden_dve(dve, l):
            g = layers[l]["gu"]
            with dve.Fori(0, FT // 2) as it:
                for j in range(2):
                    b = g.g0 + 2 * j + 1
                    dve.wait_ge(S("silu"), it * 2 + (FT * l + j + 1) + CREDIT)
                    dve.wait_ge(S("block_done"), it * 4 + (b + 1))
                    d = HG[:, ds(it * 2 + j, 1), :].rearrange("p o (a b) -> p (o a) b", a=2)
                    nc.vector.tensor_tensor(d, pair(2 * ((g.o0 + 2 * j + 1) % 2)), two(SGt[:, j, :]), ALU.mult)\
                      .then_inc(S("out_taken"), 2)

        Q1, K1, V1, QI, KW = PJ[:, 8:12, :], PJ[:, 12, :], PJ[:, 13, :], PJ[:, 14:16, :], PJ[:, 16, :]
        GP, XI = PJ[:, 0:4, :], PJ[:, 4:8, :]
        XC, GX, GA = PM[:, 0:4, :], PM[:, 4:8, :], PM[:, 8:12, :]
        CA = SC[:, 0:4 * T].rearrange("p (k t) -> p k t", k=4)
        WXA = SC[:, 2304:3328].rearrange("p (x k n) -> p x k n", x=2, k=4)
        LH0 = SC[:, 3328:3360].rearrange("p (k b) -> p k b", k=4)
        LCV = SC[:, 3360:3456].rearrange("p (k b j) -> p k b j", k=4, b=NS)
        LS8, LU, LR, LP = (SC[:, 3456 + 4 * i:3460 + 4 * i] for i in range(4))
        CO = SC[:, 3480:3480 + 4 * 27].rearrange("p (k n) -> p k n", k=4)
        HO = SC[:, 3600:3636].rearrange("p (k n) -> p k n", k=4)

        def c_dve(dve, link):
            taken(G_OIN)(dve)
            dve.wait_ge(S("lru_in"), 16 * 3)
            nc.vector.tensor_copy(CO[:, :, 0:3], XI[:, :, TP - 3:TP]).then_inc(S("l_conv_out"), 1)
            for b in range(NS):
                nc.vector.tensor_copy(CO[:, :, 3 + 3 * b:6 + 3 * b], XI[:, :, TP + LS * b + LS - 3:TP + LS * b + LS])\
                  .then_inc(S("l_conv_out"), 1)
            for k in range(4):
                w = lambda j: G("conv_w", 4 * j + k)
                link(nc.vector.tensor_scalar(XC[:, k, :], XI[:, k, :], w(3), G("conv_b", k), ALU.mult, ALU.add))
                xs = XC[:, k, TP:T].rearrange("p (b t) -> p b t", b=NS)
                xi = XI[:, k, TP:T].rearrange("p (b t) -> p b t", b=NS)
                for j in (2, 1, 0):
                    d = 3 - j
                    for o, i in ((XC[:, k, d:TP], XI[:, k, 0:TP - d]), (xs[:, :, d:LS], xi[:, :, 0:LS - d]),
                                 (xs[:, :, 0:d], LCV[:, k, :, j:3])):
                        nc.vector.scalar_tensor_tensor(o, i, w(j), o, ALU.mult, ALU.add).then_inc(S("l_tap"), 1)
                    dve.wait_ge(S("l_tap"), 9 * k + 3 * d)
            o, _ = PCOL["lam"]
            lam = par[:, o:o + 4]
            link(nc.vector.tensor_scalar(LU, lam, -1.0, None, ALU.mult))
            nc.vector.tensor_tensor(LU, LU, lam, ALU.max).then_inc(S("l_logs"), 1)
            dve.wait_ge(S("l_exp"), 1)
            link(nc.vector.tensor_scalar(LR, LU, 2.0, None, ALU.add))
            link(nc.vector.reciprocal(LR, LR))
            link(nc.vector.tensor_tensor(LU, LU, LR, ALU.mult))
            link(nc.vector.tensor_tensor(LR, LU, LU, ALU.mult))
            link(nc.vector.tensor_scalar(LP, LR, 1.0 / 17, 1.0 / 15, ALU.mult, ALU.add))
            for c in (13, 11, 9, 7, 5, 3, 1):
                link(nc.vector.tensor_tensor(LP, LP, LR, ALU.mult))
                link(nc.vector.tensor_scalar(LP, LP, 1.0 / c, None, ALU.add))
            link(nc.vector.scalar_tensor_tensor(LP, LP, 2.0, LU, ALU.mult, ALU.mult))
            link(nc.vector.tensor_scalar(LR, lam, 0.0, None, ALU.min))
            link(nc.vector.tensor_tensor(LP, LR, LP, ALU.subtract))
            nc.vector.tensor_scalar(LS8, LP, 8.0, None, ALU.mult).then_inc(S("l_logs"), 1)
            dve.wait_ge(S("l_tanh"), 4)
            TM1 = H[:, 0:4, :]
            link(nc.vector.tensor_scalar(TM1, GA, -1.0, 1.0, ALU.mult, ALU.add))
            link(nc.vector.reciprocal(TM1, TM1))
            nc.vector.scalar_tensor_tensor(GA, GA, -2.0, TM1, ALU.mult, ALU.mult).then_inc(S("l_logs"), 1)
            link(nc.vector.tensor_tensor(GX, GX, XC, ALU.mult))
            dve.wait_ge(S("l_mult"), 1)
            link(nc.vector.memset(GA[:, :, 0:1], 1.0))
            link(nc.vector.tensor_tensor(GX, GX, GA, ALU.mult))
            first = seqs(GX[:, :, TP:T])[:, :, :, 0]
            afirst = seqs(CA[:, :, TP:T])[:, :, :, 0]
            link(nc.vector.tensor_tensor(LH0, LH0, afirst, ALU.mult))
            link(nc.vector.tensor_tensor(first, first, LH0, ALU.add))
            link(nc.vector.memset(afirst, 0.0))
            for k in range(4):
                link(nc.vector.tensor_tensor_scan(XC[:, k, :], CA[:, k, :], GX[:, k, :], 0.0, ALU.mult, ALU.add))
            nc.vector.tensor_copy(HO[:, :, 0:1], XC[:, :, TP - 1:TP]).then_inc(S("l_h_out"), 1)
            nc.vector.tensor_copy(HO[:, :, 1:9], seqs(XC[:, :, TP:T])[:, :, :, LS - 1]).then_inc(S("l_h_out"), 1)
            dve.wait_ge(S("l_gelu"), 1)
            nc.vector.tensor_tensor(H[:, 0:4, :], XC, GP, ALU.mult).then_inc(S("l_out"), 1)

        def c_act(act):
            taken(G_OIN)(act)
            act.wait_ge(S("l_logs"), 1)
            nc.scalar.activation(LU, LU, ACT.Exp, scale=-1.0).then_inc(S("l_exp"), 1)
            for x, (dst, bias) in enumerate(((GX, "bx"), (GA, "ba"))):
                act.wait_ge(S("l_gates"), x + 1)
                for k in range(4):
                    nc.scalar.activation(two(dst[:, k, :]), pair(2 * k), ACT.Sigmoid, bias=G(bias, k)).then_inc(S("l_sig"), 1)
            act.wait_ge(S("l_logs"), 2)
            act.wait_ge(S("l_sig"), 8)
            for k in range(4):
                nc.scalar.activation(CA[:, k, :], GA[:, k, :], ACT.Exp, scale=LS8[:, k:k + 1]).then_inc(S("l_a"), 1)
            act.wait_ge(S("l_a"), 4)
            for k in range(4):
                nc.scalar.activation(GA[:, k, :], GA[:, k, :], ACT.Tanh, scale=LS8[:, k:k + 1]).then_inc(S("l_tanh"), 1)
            act.wait_ge(S("l_logs"), 3)
            nc.scalar.activation(GA, GA, ACT.Sqrt).then_inc(S("l_mult"), 1)
            nc.scalar.activation(GP, GP, ACT.Gelu_apprx_tanh).then_inc(S("l_gelu"), 1)

        def c_pe(pe):
            pe.wait_ge(S("l_tap"), 36)
            for x in range(2):
                if x:
                    pe.wait_ge(S("l_sig"), 4)
                for k in range(4):
                    for h in range(2):
                        mm = nc.tensor.matmul(ps[:, 2 * k + h, 0:HT], WXA[:, x, k, :], XC[:, k, h * HT:(h + 1) * HT],
                                              start=True, stop=True)
                mm.then_inc(S("l_gates"), 1)

        ROT = H[:, 4:8, :]
        RT = PJ[:, 17:21, :]
        KR = PJ[:, 21, :]
        at[0] = 0
        MB = carve(2048).rearrange("p (i n) -> p i n", i=4)
        RL = [carve(512) for _ in range(2)]
        VT = carve(512).rearrange("p (j d) -> p j d", j=4)
        VN = carve(1024)[0:LS].rearrange("p (b d) -> p b d", b=NS)
        WI = carve(32).rearrange("p (i h) -> p i h", i=4)
        T8 = carve(25)
        SS = carve(LK)[0:TS]
        WSA = carve(64)[0:TS]
        WSB = carve(512)[0:TS].rearrange("p (b t) -> p b t", b=NS)
        WSs = carve(128)[0:TS]
        QIS = carve(512)[0:32].rearrange("p (b h t) -> p b h t", b=NS, h=8)
        QIb = carve(64)[0:32]
        QB = carve(64)
        MRb = carve(64)[0:TS]
        VNb = carve(128)[0:LS]
        KNb = carve(LS)[0:32]
        ZR = carve(LK)
        ZS = ZR[0:TS]
        PTS = carve(17 * 64).rearrange("p (c n) -> p c n", c=17)
        ZP = ZR[:, 0:1024].rearrange("p (v n) -> p v n", v=2)
        PTP = ZR[:, 1024:2048].rearrange("p (v n) -> p v n", v=2)
        QG = carve(512)
        DST = carve(16)
        assert at[0] <= 13600, at
        KS = [PJt[:, 2048 * i:2048 * (i + 1)] for i in range(2)]
        VS = [PMt[:, 2048 * i:2048 * (i + 1)].rearrange("p (g d) -> p g d", g=NPG) for i in range(2)]
        flat = lambda v: v.rearrange("p k (a b) -> p (k a) b", a=2)

        def d_rope_pe(pe):
            pe.wait_ge(S("l_sig"), 8)
            for k in range(4):
                for h in range(2):
                    mm = nc.tensor.matmul(ps[:, 2 * k + h, 0:HT], C("rot64"), Q1[:, k, h * HT:(h + 1) * HT], start=True, stop=True)
            mm.then_inc(S("d_rot"), 1)
            pe.wait_ge(S("d_roped"), 1)
            for o, lhsT, src in ((0, C("rot64"), K1), (2, C("rot32"), QI[:, 0, :]), (4, C("rot32"), QI[:, 1, :]),
                                 (6, C("rep32")[0:32, :], KW[0:32, :])):
                for h in range(2):
                    mm = nc.tensor.matmul(ps[:, o + h, 0:HT], lhsT, src[:, h * HT:(h + 1) * HT], start=True, stop=True)
            mm.then_inc(S("d_rot"), 1)
            pe.wait_ge(S("d_roped"), 2)
            for h in range(2):
                mm = nc.tensor.matmul(ps[:, h, 0:HT], C("rotrep")[0:32, :], KW[0:32, h * HT:(h + 1) * HT], start=True, stop=True)
            mm.then_inc(S("d_rot"), 1)
            for j in range(4):
                nc.tensor.transpose(ps[:, 2, j * P:(j + 1) * P], V1[:, j * P:(j + 1) * P], C("ident"))
                nc.tensor.transpose(ps[:, 3, j * P:(j + 1) * P], KW[:, j * P:(j + 1) * P], C("ident"))
            for b in range(NS):
                nc.tensor.transpose(ps[0:LS, 4 + b // 4, (b % 4) * P:(b % 4 + 1) * P], V1[:, TP + b * LS:TP + (b + 1) * LS], C("ident"))
            nc.tensor.matmul(ps[0:TS, 6, 0:TS], C("spread")[32:40, :], KW[32:40, TP:T], start=True, stop=True)
            for h in range(8):
                mm = nc.tensor.matmul(ps[0:32, 7, h * TS:(h + 1) * TS], C("ident")[:, 32 * (h % 4):32 * (h % 4) + 32],
                                      QI[:, h // 4, TP:T], start=True, stop=True)
            mm.then_inc(S("d_rot"), 1)

        def d_rope_dve(dve, link):
            dve.wait_ge(S("rotary_in"), 16)
            dve.wait_ge(S("d_rot"), 1)
            for k in range(4):
                link(nc.vector.tensor_tensor(two(RT[:, k, :]), pair(2 * k), two(ROT[:, 1, :]), ALU.mult))
            link(nc.vector.tensor_tensor(Q1, Q1, bc(ROT[:, 0, :], 4), ALU.mult))
            nc.vector.tensor_tensor(Q1, Q1, RT, ALU.add).then_inc(S("d_roped"), 1)
            dve.wait_ge(S("d_roped"), 1)
            dve.wait_ge(S("d_rot"), 2)
            link(nc.vector.tensor_tensor(two(RT[:, 0, :]), pair(0), two(ROT[:, 1, :]), ALU.mult))
            link(nc.vector.tensor_tensor(K1, K1, ROT[:, 0, :], ALU.mult))
            link(nc.vector.tensor_tensor(K1, K1, RT[:, 0, :], ALU.add))
            for k in range(2):
                link(nc.vector.tensor_tensor(two(RT[:, 1 + k, :]), pair(2 + 2 * k), two(ROT[:, 3, :]), ALU.mult))
            link(nc.vector.tensor_tensor(QI, QI, bc(ROT[:, 2, :], 2), ALU.mult))
            link(nc.vector.tensor_tensor(QI, QI, RT[:, 1:3, :], ALU.add))
            nc.vector.tensor_tensor(two(KR), pair(6), two(ROT[:, 2, :]), ALU.mult).then_inc(S("d_roped"), 1)
            dve.wait_ge(S("d_roped"), 2)
            dve.wait_ge(S("d_rot"), 3)
            link(nc.vector.tensor_tensor(two(RT[:, 0, :]), pair(0), two(ROT[:, 3, :]), ALU.mult))
            link(nc.vector.tensor_tensor(KR, KR, RT[:, 0, :], ALU.add))
            dve.wait_ge(S("d_rot"), 4)
            iw = (8 ** -0.5) * (32 ** -0.5)
            dve.wait_ge(S("c_stored"), 32)
            t = S("d_ready")
            nc.vector.tensor_copy(VT, ps[:, 2, :].rearrange("p (j d) -> p j d", j=4)).then_inc(t, 1)
            nc.vector.tensor_scalar(WI, ps[:, 3, :].rearrange("p (i n) -> p i n", i=4)[:, :, 32:40], iw, None, ALU.mult).then_inc(t, 1)
            nc.vector.tensor_copy(VN, ps[0:LS, 4:6, :].rearrange("p a (b d) -> p (a b) d", b=4)).then_inc(t, 1)
            nc.vector.scalar_tensor_tensor(WSA, ps[0:TS, 6, 0:TS], iw, C("same_t")[0:TS], ALU.mult, ALU.mult).then_inc(t, 1)
            nc.vector.tensor_copy(QIS, ps[0:32, 7, :].rearrange("p (h b t) -> p b h t", h=8, b=NS)).then_inc(t, 1)
            dve.wait_ge(t, 5)
            nc.vector.tensor_tensor(WSB, bc(WSA, NS), seq_cols[0:TS], ALU.mult).then_inc(t, 1)
            dve.wait_ge(t, 6)

        blocks = [(i, h) for i in range(1, 4) for h in range(8)]

        def d_score_pe(pe):
            pe.wait_ge(S("d_ready"), 6)
            for n, (i, h) in enumerate(blocks):
                if n >= 2:
                    pe.wait_ge(S("i_relu"), n - 1)
                r = slice(32 * (h % 4), 32 * (h % 4) + 32)
                nc.tensor.matmul(ps[:, n % 2, 0:(i + 1) * P], QI[r, h // 4, i * P:(i + 1) * P], KR[r, 0:(i + 1) * P],
                                 start=True, stop=True).then_inc(S("i_dot"), 1)

        def d_score_act(act):
            for n, (i, h) in enumerate(blocks):
                act.wait_ge(S("i_dot"), n + 1)
                if n >= 2:
                    act.wait_ge(S("i_sum"), n - 1)
                nc.scalar.activation(RL[n % 2][:, 0:(i + 1) * P], ps[:, n % 2, 0:(i + 1) * P], ACT.Relu).then_inc(S("i_relu"), 1)

        def d_score_dve(dve, link):
            link(nc.vector.tensor_copy(MB[:, 0, 0:P], C("causal")))
            for n, (i, h) in enumerate(blocks):
                w = (i + 1) * P
                dve.wait_ge(S("i_relu"), n + 1)
                m = MB[:, i, 0:w]
                if h:
                    dve.wait_ge(S("i_sum"), n)
                    ins = nc.vector.scalar_tensor_tensor(m, RL[n % 2][:, 0:w], WI[:, i, h:h + 1], m, ALU.mult, ALU.add)
                else:
                    ins = nc.vector.tensor_scalar(m, RL[n % 2][:, 0:w], WI[:, i, h:h + 1], None, ALU.mult)
                ins.then_inc(S("i_sum"), 1)
                if h == 7:
                    dve.wait_ge(S("i_sum"), n + 1)
                    link(nc.vector.tensor_tensor(MB[:, i, i * P:w], MB[:, i, i * P:w], C("causal"), ALU.add))
            with dve.Fori(0, TOPK_P // 8) as r:
                for i in range(1, 4):
                    nc.vector.max(T8[:, 8 * i - 8:8 * i], MB[:, i, 0:(i + 1) * P]).then_inc(S("top"), 1)
                dve.wait_ge(S("top"), r * 3 + 3)
                nc.vector.memset(T8[:, 24:25], 0.0)
                for i in range(1, 4):
                    nc.vector.match_replace(MB[:, i, 0:(i + 1) * P], T8[:, 8 * i - 8:8 * i], MB[:, i, 0:(i + 1) * P], TAKEN)\
                      .then_inc(S("take"), 1)
                dve.wait_ge(S("take"), r * 3 + 3)
            for i in range(1, 4):
                m = MB[:, i, 0:(i + 1) * P]
                link(nc.vector.tensor_scalar(m, m, TAKEN, BIG, ALU.is_equal, ALU.mult))
                nc.vector.tensor_scalar(m, m, -BIG, None, ALU.add).then_inc(S("mask"), 1)
            dve.wait_ge(S("mask"), 3)

        def d_prompt_pool(pool):
            pool.wait_ge(S("d_ready"), 6)
            with pool.Fori(0, 4) as g:
                pool.wait_ge(S("p_logits"), g * 4 + CREDIT)
                nc.gpsimd.tensor_copy(QG, Q1[:, ds(g, 1), 0:TP].rearrange("p o t -> p (o t)")).then_inc(S("p_q"), 1)

        def d_prompt_pe(pe):
            def logits(g, i):
                w = (i + 1) * P
                if i == 0:
                    pe.wait_ge(S("p_q"), g + 1)
                pe.wait_ge(S("p_masked"), g * 4 + i + CREDIT)
                for v in range(2):
                    r = slice(64 * v, 64 * v + 64)
                    mm = nc.tensor.matmul(ps[:, v, 0:w], QG[r, i * P:w], K1[r, 0:w], start=True, stop=True)
                mm.then_inc(S("p_logits"), 1)

            def heads(g, last):
                for i in range(4):
                    if i < 3:
                        logits(g, i + 1)
                    elif not last:
                        logits(g + 1, 0)
                    pe.wait_ge(S("p_normed"), g * 4 + (i + 1))
                    pe.wait_ge(S("p_pt"), g * 4 + i + CREDIT)
                    for v in range(2):
                        for j in range(i + 1):
                            mm = nc.tensor.transpose(ps[:, 2 + v, j * P:(j + 1) * P], ZP[:, v, j * P:(j + 1) * P], C("ident"))
                    mm.then_inc(S("p_turned"), 1)
                    pe.wait_ge(S("p_pt"), g * 4 + (i + 1) + CREDIT)
                    pe.wait_ge(S("p_out"), g * 4 + i + CREDIT)
                    for v in range(2):
                        for j in range(i + 1):
                            mm = nc.tensor.matmul(ps[64 * v:64 * v + 64, 4, 0:P], VT[:, j, 64 * v:64 * v + 64],
                                                  PTP[:, v, j * P:(j + 1) * P], start=(j == 0), stop=(j == i))
                    mm.then_inc(S("p_outmm"), 1)

            pe.wait_ge(S("mask"), 3)
            pe.wait_ge(S("t_taken"), 2)
            logits(0, 0)
            with pe.Fori(0, 3) as g:
                heads(g, False)
            heads(3, True)

        def d_prompt_dve(dve, link):
            def round(r):
                nc.vector.max(T8[0:TS, 0:8], SS).then_inc(S("top"), 1)
                dve.wait_ge(S("top"), r + (3 * (TOPK_P // 8) + 1))
                nc.vector.memset(T8[:, 24:25], 0.0)
                nc.vector.match_replace(SS, T8[0:TS, 0:8], SS, TAKEN).then_inc(S("take"), 1)
                dve.wait_ge(S("take"), r + (3 * (TOPK_P // 8) + 1))

            assert TOPK_S // 8 == 32
            with dve.Fori(0, 4) as g:
                link.enter(g, 4 * 2)
                for i in range(4):
                    w = (i + 1) * P
                    dve.wait_ge(S("p_logits"), g * 4 + (i + 1) + CREDIT)
                    dve.wait_ge(S("p_turned"), g * 4 + i + CREDIT)
                    nc.vector.scalar_tensor_tensor(ZP[:, :, 0:w], ps[:, 0:2, 0:w], 0.125, bc(MB[:, i, 0:w], 2), ALU.mult, ALU.add)\
                      .then_inc(S("p_masked"), 1)
                    dve.wait_ge(S("p_masked"), g * 4 + (i + 1) + CREDIT)
                    link(nc.vector.tensor_reduce(DST[:, 0:2], ZP[:, :, 0:w], AX_X, ALU.max))
                    nc.vector.tensor_scalar(DST[:, 2:4], DST[:, 0:2], -1.0, None, ALU.mult).then_inc(S("p_bias"), 1)
                    round(g * 8 + 2 * i)
                    dve.wait_ge(S("p_exp"), g * 8 + (2 * i + 2))
                    link(nc.vector.reciprocal(DST[:, 6:8], DST[:, 4:6]))
                    nc.vector.tensor_tensor(ZP[:, :, 0:w], ZP[:, :, 0:w], DST[:, 6:8].unsqueeze(2).broadcast_to([P, 2, w]), ALU.mult)\
                      .then_inc(S("p_normed"), 1)
                    round(g * 8 + (2 * i + 1))
                    dve.wait_ge(S("p_outmm"), g * 4 + (i + 1) + CREDIT)
                    dst = H[:, ds(g + 4, 1), i * P:w].rearrange("p o t -> p (o t)")
                    nc.vector.tensor_copy(dst, ps[:, 4, 0:P]).then_inc(S("p_out"), 1)
            link.leave(4)
            link(nc.vector.tensor_scalar(SS, SS, TAKEN, BIG, ALU.is_equal, ALU.mult))
            nc.vector.tensor_scalar(SS, SS, -BIG, None, ALU.add).then_inc(S("mask"), 1)

        def d_prompt_act(act):
            with act.Fori(0, 4) as g:
                for i in range(4):
                    w = (i + 1) * P
                    act.wait_ge(S("p_bias"), g * 4 + (i + 1))
                    for v in range(2):
                        nc.scalar.activation(ZP[:, v, 0:w], ZP[:, v, 0:w], ACT.Exp, bias=DST[:, 2 + v:3 + v],
                                             accum_out=DST[:, 4 + v:5 + v]).then_inc(S("p_exp"), 1)
                    act.wait_ge(S("p_turned"), g * 4 + (i + 1) + CREDIT)
                    act.wait_ge(S("p_outmm"), g * 4 + i + CREDIT)
                    nc.scalar.activation(PTP[:, :, 0:w], ps[:, 2:4, 0:w], ACT.Copy).then_inc(S("p_pt"), 1)

        def pages_in(sp):
            sp.wait_ge(S("l_out"), 1)
            sp.wait_ge(S("b_in"), 80)

            def page(b, i, g):
                return sp.value_load(PT[0:1, ds(b * NPG + (i * NPG + g), 1)], min_val=0, max_val=a["pool_ki"].shape[0] - 1)

            def ki(b, i, again):
                if again:
                    sp.wait_ge(S("t_chunk"), b * 5 + (5 * i - 5))
                for g in range(NPG):
                    sp.dma_start(KS[i][0:32, g * PAGE:(g + 1) * PAGE],
                                 a["pool_ki"][ds(page(b, i, g), 1)].rearrange("o d n -> (o d) n")).then_inc(S(f"pages{i}"), 16)

            def kv(b, i, again):
                if again:
                    sp.wait_ge(S("u_logits"), b + (i - 1) + CREDIT)
                numbers = [page(b, i, g) for g in range(NPG)]
                for g, pg in enumerate(numbers):
                    sp.dma_start(KS[i][:, g * PAGE:(g + 1) * PAGE], a["pool_k"][ds(pg, 1)].rearrange("o d n -> (o d) n"))\
                      .then_inc(S(f"pages{i}"), 16)
                if again:
                    sp.wait_ge(S("u_outmm"), b + (i - 1) + CREDIT)
                for g, pg in enumerate(numbers):
                    sp.dma_start(VS[i][:, g, :], a["pool_v"][ds(pg, 1)].rearrange("o n d -> (o n) d")).then_inc(S(f"pv{i}"), 16)

            for i in range(2):
                ki(0, i, False)
            with sp.Fori(1, NS // 2) as b2:
                b = b2 * 2
                for i in range(2):
                    ki(b, i, True)
            sp.wait_ge(S("t_chunk"), 5 * NS)
            for i in range(2):
                kv(0, i, False)
            with sp.Fori(1, NS // 2) as b2:
                b = b2 * 2
                for i in range(2):
                    kv(b, i, True)

        def d_index_pool(pool):
            nc.gpsimd.memset(WSs, 0.0).then_inc(S("zeroed"), 1)
            pool.wait_ge(S("zeroed"), 3)
            with pool.Fori(0, NS) as b:
                pool.wait_ge(S("t_sum"), b * 5 + CREDIT)
                nc.gpsimd.tensor_copy(QIb.rearrange("p (h t) -> p h t", h=8), QIS[:, ds(b, 1)].rearrange("p o h t -> p (o h) t"))\
                  .then_inc(S("t_copy"), 1)
                nc.gpsimd.tensor_copy(KNb, KR[0:32, ds(b * LS + TP, LS)]).then_inc(S("t_copy"), 1)
                nc.gpsimd.tensor_copy(WSs[:, 0:TS], WSB[:, ds(b, 1), :].rearrange("p o t -> p (o t)")).then_inc(S("t_copy"), 1)

        def d_index_pe(pe):
            pe.wait_ge(S("i_relu"), len(blocks))

            def add(b, i, c, first):
                k = 5 * i + c
                pe.wait_ge(S("t_relu"), b * 5 + (k + 1))
                w = 512 if c < 4 else LS
                nc.tensor.matmul(ps[:, 2 + c, 0:w], WSs, RL[k % 2][0:TS, 0:w], start=first, stop=True,
                                 skip_group_check=True).then_inc(S("t_sum"), 1)

            def sequence(b, i, first):
                pe.wait_ge(S("t_copy"), b * 3 + (3 * i + 3))
                pe.wait_ge(S(f"pages{i}"), b * (8 * NPG) + 16 * NPG)
                for c in range(5):
                    k = 5 * i + c
                    if not first or c >= 2:
                        pe.wait_ge(S("t_relu"), b * 5 + (k - 1))
                    w = 512 if c < 4 else LS
                    rhs = KS[i][0:32, c * 512:(c + 1) * 512] if c < 4 else KNb
                    mm = nc.tensor.matmul(ps[0:TS, k % 2, 0:w], QIb, rhs, start=True, stop=True)
                    mm.then_inc(S("t_chunk"), 1)
                    if c:
                        add(b, i, c - 1, first)
                add(b, i, 4, first)

            sequence(0, 0, True)
            sequence(0, 1, False)
            with pe.Fori(1, NS // 2) as b2:
                b = b2 * 2
                for i in range(2):
                    sequence(b, i, False)

        def d_index_act(act):
            def chunk(b, i, c, first):
                k = 5 * i + c
                w = 512 if c < 4 else LS
                act.wait_ge(S("t_chunk"), b * 5 + (k + 1))
                if not first or c >= 2:
                    act.wait_ge(S("t_sum"), b * 5 + (k - 1) + CREDIT)
                nc.scalar.activation(RL[k % 2][0:TS, 0:w], ps[0:TS, k % 2, 0:w], ACT.Relu).then_inc(S("t_relu"), 1)

            act.wait_ge(S("i_sum"), len(blocks))
            for i in range(2):
                for c in range(5):
                    chunk(0, i, c, i == 0)
            with act.Fori(1, NS // 2) as b2:
                b = b2 * 2
                for i in range(2):
                    for c in range(5):
                        chunk(b, i, c, False)

        def d_index_dve(dve, link):
            dve.wait_ge(S("t_sum"), 5 * NS + CREDIT)
            nc.vector.tensor_copy(SS[:, 0:PAST].rearrange("p (c n) -> p c n", c=4), ps[0:TS, 2:6, :]).then_inc(S("t_taken"), 1)
            nc.vector.tensor_tensor(SS[:, PAST:LK], ps[0:TS, 6, 0:LS], C("causal_n")[0:TS], ALU.add).then_inc(S("t_taken"), 1)
            dve.wait_ge(S("t_taken"), 2)

        def d_sample_pool(pool):
            nc.gpsimd.memset(QB, 0.0).then_inc(S("zeroed"), 1)
            pool.wait_ge(S("zeroed"), 4)
            with pool.Fori(0, NS) as b:
                pool.wait_ge(S("u_logits"), b + CREDIT)
                for v in range(2):
                    r = slice(64 * v, 64 * v + 64)
                    nc.gpsimd.tensor_copy(QB[r, 32 * v:32 * v + 32].rearrange("p (g t) -> p g t", g=4),
                                          Q1[r, :, ds(b * LS + TP, LS)]).then_inc(S("u_copy"), 1)
                nc.gpsimd.tensor_copy(MRb, C("mask_rows")[0:TS, ds(b * 64, 64)]).then_inc(S("u_copy"), 1)
                pool.wait_ge(S("u_outmm"), b + CREDIT)
                nc.gpsimd.tensor_copy(VNb, VN[:, ds(b, 1), :].rearrange("p o d -> p (o d)")).then_inc(S("u_copy"), 1)

        def d_sample_pe(pe):
            def logits(b, i):
                pe.wait_ge(S("u_copy"), b * 4 + (4 * i + 3))
                pe.wait_ge(S(f"pages{i % 2}"), b * (8 * NPG) + 16 * NPG * (1 + i // 2 + NS // 2))
                pe.wait_ge(S("u_exp"), b * 2 + 2 * i + CREDIT)
                for c in range(5):
                    w = 512 if c < 4 else LS
                    rhs = KS[i % 2][:, c * 512:(c + 1) * 512] if c < 4 else K1[:, ds(b * LS + (i * LS + TP), LS)]
                    nc.tensor.matmul(ps[0:TS, c, 0:w], QB, rhs, start=True, stop=False)
                    mm = nc.tensor.matmul(ps[0:TS, c, 0:w], MRb, SS[:, c * 512:c * 512 + w], start=False, stop=True)
                mm.then_inc(S("u_logits"), 1)

            def outputs(b, i):
                pe.wait_ge(S("u_normed"), b + (i + 1))
                for c in range(NPG):
                    nc.tensor.matmul(ps[:, 5 + c // 8, (c % 8) * 64:(c % 8 + 1) * 64], ZS[:, c * P:(c + 1) * P], C("ident")[0:TS, 0:TS],
                                     start=True, stop=True)
                mm = nc.tensor.matmul(ps[0:LS, 7, 0:64], ZS[:, PAST:LK], C("ident")[0:TS, 0:TS], start=True, stop=True)
                mm.then_inc(S("u_turned"), 1)
                pe.wait_ge(S("u_copy"), b * 4 + (4 * i + 4))
                pe.wait_ge(S("u_pt"), b * 2 + (2 * i + 2))
                pe.wait_ge(S(f"pv{i}"), b * (8 * NPG) + 16 * NPG)
                pe.wait_ge(S("u_out"), b * 2 + 2 * i + CREDIT)
                for c in range(NPG):
                    nc.tensor.matmul(ps[:, 7, 64:128], VS[i][:, c, :], PTS[:, c, :], start=(c == 0), stop=False)
                mm = nc.tensor.matmul(ps[:, 7, 64:128], VNb, PTS[0:LS, 16, :], start=False, stop=True)
                mm.then_inc(S("u_outmm"), 1)

            pe.wait_ge(S("mask"), 4)
            logits(0, 0)
            with pe.Fori(0, NS // 2 - 1) as b2:
                b = b2 * 2
                for i in range(2):
                    logits(b, i + 1)
                    outputs(b, i)
            logits(NS - 2, 1)
            outputs(NS - 2, 0)
            outputs(NS - 2, 1)

        def d_sample_dve(dve, link):
            st = lambda j, n=1: DST[0:TS, j:j + n]

            def maxima(b, k):
                dve.wait_ge(S("u_logits"), b + (k + 1) + CREDIT)
                nc.vector.tensor_reduce(st(0), ps[0:TS, 0:4, :], mybir.AxisListType.XY, ALU.max).then_inc(S("u_max"), 1)
                nc.vector.tensor_reduce(st(1), ps[0:TS, 4, 0:LS], AX_X, ALU.max).then_inc(S("u_max"), 1)
                dve.wait_ge(S("u_max"), b * 2 + (2 * k + 2))
                link(nc.vector.tensor_tensor(st(2), st(0), st(1), ALU.max))
                nc.vector.tensor_scalar(st(3), st(2), -0.125, None, ALU.mult).then_inc(S("u_bias"), 1)

            def rest(b, last):
                dve.wait_ge(S("u_exp"), b * 2 + 2 + CREDIT)
                link(nc.vector.tensor_tensor(st(6), st(4), st(5), ALU.add))
                link(nc.vector.reciprocal(st(7), st(6)))
                nc.vector.tensor_scalar(ZS, ZS, st(7), None, ALU.mult).then_inc(S("u_normed"), 1)
                if not last:
                    maxima(b, 1)
                dve.wait_ge(S("u_turned"), b + 1 + CREDIT)
                nc.vector.tensor_copy(PTS[:, 0:16, :].rearrange("p (a c) n -> p a (c n)", a=2), ps[:, 5:7, :]).then_inc(S("u_pt"), 1)
                nc.vector.tensor_copy(PTS[0:LS, 16, :], ps[0:LS, 7, 0:64]).then_inc(S("u_pt"), 1)
                dve.wait_ge(S("u_outmm"), b + 1 + CREDIT)
                for v in range(2):
                    r = slice(64 * v, 64 * v + 64)
                    nc.vector.tensor_copy(H[r, 4:8, ds(b * LS + TP, LS)],
                                          ps[r, 7, 64 + 32 * v:96 + 32 * v].rearrange("p (g t) -> p g t", g=4)).then_inc(S("u_out"), 1)

            maxima(0, 0)
            with dve.Fori(0, NS - 1) as b:
                link.enter(b, 3)
                rest(b, False)
            link.leave(NS - 1)
            rest(NS - 1, True)

        def d_sample_act(act):
            with act.Fori(0, NS) as b:
                act.wait_ge(S("u_bias"), b + 1)
                act.wait_ge(S("u_turned"), b + CREDIT)
                nc.scalar.activation(ZS[:, 0:PAST].rearrange("p (c n) -> p c n", c=4), ps[0:TS, 0:4, :], ACT.Exp,
                                     bias=DST[0:TS, 3:4], scale=0.125, accum_out=DST[0:TS, 4:5]).then_inc(S("u_exp"), 1)
                nc.scalar.activation(ZS[:, PAST:LK], ps[0:TS, 4, 0:LS], ACT.Exp, bias=DST[0:TS, 3:4], scale=0.125,
                                     accum_out=DST[0:TS, 5:6]).then_inc(S("u_exp"), 1)

        PT = ctx.enter_context(nc.sbuf_tensor("PT", [1, NS * NPG], I32))
        LD = layers
        RES = [lambda e: e.wait_ge(S("x_in"), 16), taken(G_EOUT), taken(LD[0]["o"]), taken(LD[0]["d"]), taken(G_OOUT),
               taken(LD[1]["o"]), taken(LD[1]["d"])]
        GAINS = ["mix0", "x0", "ffn0", "mix1", "x1", "ffn1", "final"]

        block = ctx.enter_context(nc.Block())

        def normed(eng, n):
            eng.wait_ge(S("normed"), KT * (n + 1))

        @block.sync
        def _(sp):
            sp.dma_start(X, a["x"]).then_inc(S("x_in"), 16)
            sp.dma_start(par[:, :], a["par"]).then_inc(S("par_in"), 16)
            weights_in(sp, G_EIN)
            weights_in(sp, G_EOUT)

            def cache_in(l):
                taken([G_EOUT, G_OOUT][l])(sp)
                normed(sp, 1 + 3 * l)
                for i in range(2):
                    sp.dma_start(SKs[i], a["mk"][NS * l + i]).then_inc(S(f"sk{i}"), 16)
                    sp.dma_start(SVs[i], a["mv"][NS * l + i]).then_inc(S(f"sv{i}"), 16)
                for h in range(1, XH):
                    for i in range(2):
                        sp.wait_ge(S("y_logits"), h * 2 + (8 * l + i - 1) + CREDIT)
                        sp.dma_start(SKs[i], a["mk"][h * 2 + (NS * l + i)]).then_inc(S(f"sk{i}"), 16)
                    for i in range(2):
                        sp.wait_ge(S("y_outmm"), h * 2 + (8 * l + i - 1))
                        sp.dma_start(SVs[i], a["mv"][h * 2 + (NS * l + i)]).then_inc(S(f"sv{i}"), 16)

            for l in range(2):
                if l == 1:
                    weights_in(sp, G_OIN)
                    pages_in(sp)
                    weights_in(sp, G_OOUT)
                for k in ("k", "v", "q"):
                    weights_in(sp, LD[l][k])
                cache_in(l)
                for k in ("o", "gu", "d"):
                    weights_in(sp, LD[l][k])

        @block.gpsimd
        def _(pool):
            nc.gpsimd.memset(ones[:, :], 1.0).then_inc(S("consts_set"), 1)
            for name in CREDITED:
                pool.sem_inc(S(name), CREDIT)
            for j, v in enumerate((EPS, GN_EPS, 1e-12)):
                nc.gpsimd.memset(eps[:, j:j + 1], v).then_inc(S("consts_set"), 1)
            nc.gpsimd.memset(Sb, 0.0).then_inc(S("consts_set"), 1)
            pool.dma_start(cst[:, :], a["cst"]).then_inc(S("cst_in"), 16)
            for dst, name in ((WS, "ws"), (WSS, "wss"), (BS, "bs"), (BSS, "bss")):
                pool.dma_start(dst, a[name]).then_inc(S("a_in"), 16)
            for dst, name in ((LORA, "lora"), (SH0, "sh0"), (RESET, "reset"), (S0, "s0")):
                pool.dma_start(dst, a[name]).then_inc(S("b_in"), 16)
            pool.dma_start(PT[:, :], a["table"]).then_inc(S("b_in"), 16)
            pool.wait_ge(S("cst_in"), 16)
            pool.wait_ge(S("a_normed"), 1)
            pool.dma_start(out["cv"], A_V[:, :, TP:T]).then_inc(S("cv_stored"), 16)
            with pool.Fori(0, NRC) as n:
                chunk_pool(pool, n, LEVELS, False)
            chunk_pool(pool, NRC, 3, True)
            pool.wait_ge(S("b_shift"), LS + 2)
            pool.dma_start(out["sh"], SHO).then_inc(S("b_stored"), 16)
            pool.wait_ge(S("s_state"), NS)
            pool.dma_start(out["rs"], S0).then_inc(S("b_stored"), 16)
            for hh in range(2):
                r = slice(64 * hh, 64 * hh + 64)
                pool.dma_start(out["rp"][hh], Sb[r, :, r]).then_inc(S("b_stored"), 16)
            pool.wait_ge(S("b_stored"), 64)
            for l in range(2):
                pool.dma_start(MR, a["mem"]).then_inc(S("mem_in"), 16)
                cross_pool(pool, l)
                pool.dma_start(out["mk"][l], MK).then_inc(S("m_stored"), 16)
                pool.dma_start(out["mv"][l], MV).then_inc(S("m_stored"), 16)
                pool.wait_ge(S("m_stored"), 32 * (l + 1))
                if l == 1:
                    break
                taken(LD[0]["o"])(pool)
                for dst, name in ((WXA, "wxa"), (LH0, "lh0"), (LCV, "lcv")):
                    pool.dma_start(dst, a[name]).then_inc(S("lru_in"), 16)
                taken(G_OIN)(pool)
                pool.dma_start(ROT, a["rot"]).then_inc(S("rotary_in"), 16)
                pool.wait_ge(S("l_conv_out"), 1 + NS)
                pool.dma_start(out["conv"], CO).then_inc(S("c_stored"), 16)
                pool.dma_start(out["v"], V1).then_inc(S("d_stored"), 16)
                pool.wait_ge(S("l_h_out"), 2)
                pool.dma_start(out["h"], HO).then_inc(S("c_stored"), 16)
                pool.wait_ge(S("d_ready"), 6)
                pool.dma_start(out["k"], K1).then_inc(S("d_stored"), 16)
                pool.dma_start(out["ki"], KR[0:32]).then_inc(S("d_stored"), 16)
                d_index_pool(pool)
                d_prompt_pool(pool)
                d_sample_pool(pool)
                pool.wait_ge(S("c_stored"), 32)
                pool.wait_ge(S("d_stored"), 48)
                pool.wait_ge(S("u_out"), 2 * NS + CREDIT)
            normed(pool, 6)
            pool.dma_start(out["y"], H).then_inc(S("y_stored"), 16)
            pool.wait_ge(S("y_stored"), 16)
            pool.wait_ge(S("cv_stored"), 16)

        @block.tensor
        def _(pe):
            pe.wait_ge(S("consts_set"), 5)
            norm_pe(pe, 0)
            product(pe, G_EIN, H, norm=0)
            pe.wait_ge(S("cst_in"), 16)
            a_pe(pe)
            b_pre_pe(pe)
            turn_pe(pe, 0, 0)
            with pe.Fori(0, NRC) as n:
                chunk_pe(pe, n, LEVELS, False)
            chunk_pe(pe, NRC, 3, True)
            sample_state_pe(pe)
            b_post_pe(pe)
            pe.wait_ge(S("b_out"), 1)
            product(pe, G_EOUT, H)
            for l in range(2):
                if l == 1:
                    norm_pe(pe, 3)
                    product(pe, G_OIN, H, norm=3)
                    c_pe(pe)
                    d_rope_pe(pe)
                    d_score_pe(pe)
                    d_index_pe(pe)
                    d_prompt_pe(pe)
                    d_sample_pe(pe)
                    pe.wait_ge(S("u_out"), 2 * NS + CREDIT)
                    product(pe, G_OOUT, H)
                mem_pe(pe, l)
                norm_pe(pe, 1 + 3 * l)
                pe.wait_ge(S("m_normed"), KT * (l + 1))
                memory_product(pe, LD[l]["k"], True)
                memory_product(pe, LD[l]["v"], False)
                product(pe, LD[l]["q"], H, norm=1 + 3 * l)
                cross_pe(pe, l)
                pe.wait_ge(S("x_out"), 8 * (l + 1) + CREDIT)
                pe.wait_ge(S("y_out"), NS * (l + 1) + CREDIT)
                product(pe, LD[l]["o"], H)
                norm_pe(pe, 2 + 3 * l)
                product(pe, LD[l]["gu"], H, gate_free(pe, l), norm=2 + 3 * l)
                taken(LD[l]["gu"])(pe)
                product(pe, LD[l]["d"], HG)
            norm_pe(pe, 6)

        @block.scalar
        def _(act):
            act.wait_ge(S("consts_set"), 5)
            norm_act(act, 0, RES[0])
            act.wait_ge(S("par_in"), 16)
            a_act(act)
            b_pre_act(act)
            with act.Fori(0, NRC) as n:
                chunk_act(act, n, LEVELS, False)
            chunk_act(act, NRC, 3, True)
            b_post_act(act)
            for l in range(2):
                if l == 1:
                    norm_act(act, 3, RES[3])
                    c_act(act)
                    d_score_act(act)
                    d_index_act(act)
                    d_prompt_act(act)
                    d_sample_act(act)
                mem_act(act, l)
                norm_act(act, 1 + 3 * l, RES[1 + 3 * l])
                cross_act(act, l)
                norm_act(act, 2 + 3 * l, RES[2 + 3 * l])
                silu_act(act, l)
            norm_act(act, 6, RES[6])

        @block.vector
        def _(dve):
            link = Chain(dve, S("vector_chain"))
            dve.wait_ge(S("par_in"), 16)
            norm_dve(dve, 0, RES[0], GAINS[0], link)
            take(dve, G_EIN, PJ, False)
            dve.wait_ge(S("cst_in"), 16)
            dve.wait_ge(S("consts_set"), 5)
            a_dve(dve, link)
            b_pre_dve(dve, link)
            for x in range(4):
                spread_x(x, 0, 0)
            chunk_rest(0, 0)
            with dve.Fori(0, NRC) as n:
                link.enter(n, 1 + 2)
                chunk_dve(dve, n, LEVELS, False, link)
            link.leave(NRC)
            chunk_dve(dve, NRC, 3, True, link)
            sample_state_dve(dve, link)
            b_post_dve(dve, link)
            take(dve, G_EOUT, X, True)
            for l in range(2):
                if l == 1:
                    norm_dve(dve, 3, RES[3], GAINS[3], link)
                    take(dve, G_OIN, PJ, False)
                    c_dve(dve, link)
                    d_rope_dve(dve, link)
                    d_score_dve(dve, link)
                    d_index_dve(dve, link)
                    d_prompt_dve(dve, link)
                    d_sample_dve(dve, link)
                    take(dve, G_OOUT, X, True)
                mem_dve(dve, l, link)
                norm_dve(dve, 1 + 3 * l, RES[1 + 3 * l], GAINS[1 + 3 * l], link)
                memory_take(dve, LD[l]["k"], True)
                memory_take(dve, LD[l]["v"], False)
                take(dve, LD[l]["q"], XQ, False)
                cross_dve(dve, l, link)
                take(dve, LD[l]["o"], X, True)
                norm_dve(dve, 2 + 3 * l, RES[2 + 3 * l], GAINS[2 + 3 * l], link)
                hidden_dve(dve, l)
                take(dve, LD[l]["d"], X, True)
            norm_dve(dve, 6, RES[6], GAINS[6], link)


def tiles(v):
    v = np.asarray(v)
    return np.ascontiguousarray(v.reshape(v.shape[0] // P, P, *v.shape[1:]).swapaxes(0, 1))


def blocks_of(w, kt):
    k, n = w.shape
    b = w.reshape(k // (kt * P), kt, P, n // P, P).transpose(3, 0, 2, 1, 4)
    return np.ascontiguousarray(b).reshape(-1, P, kt * P)


B_COLS = np.concatenate([np.arange(0, 512), np.arange(576, 1600), np.arange(512, 576), np.arange(1600, 1792)])
HEADS = np.concatenate([np.r_[64 * j:64 * j + 64, 64 * (4 + j):64 * (4 + j) + 64] for j in range(4)])


def kernel(**i):
    import concourse.bacc as bacc
    from concourse.bass_utils import run_bass_kernel_spmd

    i = {k: np.asarray(v) for k, v in i.items()}
    f = np.float32
    n = {}
    x = np.concatenate([i["x_prompt"][0], i["x_sample"].reshape(TS, D)], 0)
    n["x"] = tiles(x.T)
    n["mem"] = tiles(i["mem_prompt"][0].T)
    vecs = []
    for l in range(2):
        vecs.append(("mix%d" % l, i["norm_mix"][l]))
        vecs.append(("x%d" % l, i["norm_x"][l]))
        vecs.append(("mem%d" % l, i["norm_mem"][l]))
        vecs.append(("ffn%d" % l, i["norm_ffn"][l]))
    vecs += [("final", i["norm_final"]), ("ln_g", i["a_ln_g"][0]), ("ln_b", i["a_ln_b"][0]), ("mu", i["b_mu"][0][B_COLS]),
             ("w0", i["b_w0"][0]), ("a0", i["b_a0"][0]), ("k_k", i["b_kk"][0]), ("k_a", i["b_ka"][0]),
             ("r_k", i["b_rk"][0].reshape(-1)), ("gn_g", i["b_gn_g"][0]), ("gn_b", i["b_gn_b"][0]),
             ("conv_w", i["c_conv_w"][0].reshape(-1)), ("conv_b", i["c_conv_b"][0]), ("bx", i["c_bx"][0]),
             ("ba", i["c_ba"][0]), ("lam", i["c_lambda"][0])]
    n["par"] = np.zeros((P, NPAR), f)
    for name, v in vecs:
        o, w = PCOL[name]
        n["par"][:, o:o + w] = tiles(v)
    n["cst"] = np.concatenate([CONST[k] for k in CCOL], 1)
    c64, s64 = rotary(64)
    c32, s32 = rotary(32)
    n["rot"] = np.ascontiguousarray(np.stack([c64, s64, c32, s32], 1))
    reset = np.ones((P, T), f)
    reset[:, 0:TP:RC] = 0
    reset[:, TP::LS] = 0
    n["reset"] = reset
    wt = i["a_ws"][0].transpose(2, 0, 1)
    n["ws"] = np.ascontiguousarray(wt)
    wss = np.zeros((TS, A_G, TS), f)
    bss = np.zeros((1, A_G, NS, LS), f)
    for b in range(NS):
        wss[b * LS:(b + 1) * LS, :, b * LS:(b + 1) * LS] = wt[:LS, :, :LS]
        bss[0, :, b] = i["a_bs"][0][:, :LS]
    n["wss"] = wss
    n["bs"] = i["a_bs"][0].reshape(1, -1)
    n["bss"] = bss.reshape(1, -1)
    n["lora"] = np.concatenate([np.concatenate([i["b_wB"][0], i["b_aB"][0]], 0), i["b_gB"][0]], 1)
    n["sh0"] = tiles(i["state_rwkv_shift"][0][:, B_COLS].T)
    s0 = i["state_rwkv"][0].reshape(NS, 4, 2, 64, 64)
    n["s0"] = np.ascontiguousarray(s0.transpose(2, 4, 0, 1, 3)).reshape(P, NS, 4, 64)
    n["table"] = i["page_table"].reshape(1, -1)
    n["mk"] = np.ascontiguousarray(i["cache_mem_k"].reshape(2 * NS, MEM, KT, P).transpose(0, 3, 2, 1))
    n["mv"] = np.ascontiguousarray(i["cache_mem_v"].reshape(2 * NS, 2, P, D).transpose(0, 2, 1, 3))
    wxa = np.zeros((P, 2, 4, P), f)
    for g, w in enumerate((i["c_wx"][0], i["c_wa"][0])):
        for k in range(8):
            r = slice(64 * (k % 2), 64 * (k % 2) + 64)
            wxa[r, g, k // 2, r] = w[k]
    n["wxa"] = wxa
    n["lh0"] = tiles(i["state_lru_h"][0].T)
    n["lcv"] = tiles(i["state_lru_conv"][0].transpose(2, 0, 1))
    n["pool_k"] = np.ascontiguousarray(i["cache_attn_k"][0].reshape(-1, PAGE, P).transpose(0, 2, 1))
    n["pool_v"] = i["cache_attn_v"][0].reshape(-1, PAGE, P)
    n["pool_ki"] = np.ascontiguousarray(i["cache_attn_kidx"][0].transpose(0, 2, 1))
    ein = i["e_w_in"][0]
    n["w_ein"] = blocks_of(np.concatenate([ein[:, :1024], ein[:, 1024:][:, B_COLS]], 1), KT)
    n["w_eout"] = blocks_of(i["e_w_out"][0], KT)
    oin = i["o_w_in"][0]
    oin = np.concatenate([oin[:, :1024], oin[:, 1024:1536][:, HEADS], oin[:, 1536:],
                          np.zeros((D, OW_T * P - oin.shape[1]), f)], 1)
    n["w_oin"] = blocks_of(oin, KT)
    oo = i["o_w_out"][0]
    n["w_oout"] = blocks_of(np.concatenate([oo[:512], oo[512:][HEADS]], 0), KT)
    for l in range(2):
        n[f"w_xk{l}"], n[f"w_xv{l}"] = blocks_of(i["w_xk"][l], KT), blocks_of(i["w_xv"][l], KT)
        n[f"w_xq{l}"], n[f"w_xo{l}"] = blocks_of(i["w_xq"][l], KT), blocks_of(i["w_xo"][l], KT)
        n[f"w_gu{l}"] = np.stack([blocks_of(i["w_ff_gate"][l], KT), blocks_of(i["w_ff_up"][l], KT)], 1).reshape(2 * FT, P, D)
        n[f"w_d{l}"] = blocks_of(i["w_ff_down"][l], FT // 2)
    shapes = dict(y=(P, KT, T), cv=(P, 4, TS), rp=(2, 64, 4, 64), rs=(P, NS, 4, 64), sh=(P, 14, 9), conv=(P, 4, 27),
                  h=(P, 4, 9), k=(P, T), v=(P, T), ki=(32, T), mk=(2, P, KT, MEM), mv=(2, P, 2, D))
    nc = bacc.Bacc("TRN2", target_bir_lowering=False, num_devices=1)
    arrays = {f"in_{k}": np.ascontiguousarray(v) for k, v in n.items()}
    a = {k: nc.dram_tensor(f"in_{k}", list(v.shape), mybir.dt.from_np(v.dtype), kind="ExternalInput").ap() for k, v in n.items()}
    o = {k: nc.dram_tensor(f"out_{k}", list(s), F32, kind="ExternalOutput").ap() for k, s in shapes.items()}
    build(nc, a, o)
    r = run_bass_kernel_spmd(nc, [arrays], core_ids=[0]).results[0]
    r = {k: np.asarray(r[f"out_{k}"]) for k in shapes}

    rows = lambda v: v.swapaxes(0, 1).reshape(-1, *v.shape[2:])
    y = rows(r["y"]).T
    sh = np.empty((9, 1792), f)
    sh[:, B_COLS] = rows(r["sh"]).T
    state = lambda s: s.reshape(2, 64, -1, 4, 64).transpose(2, 3, 0, 4, 1).reshape(1, -1, 8, 64, 64)
    rp = r["rp"].reshape(P, 1, 4, 64)
    conv = rows(r["conv"]).reshape(512, 9, 3).transpose(1, 2, 0)
    h = rows(r["h"]).T
    k, v, ki = r["k"].T, r["v"].T, r["ki"].T
    mk = r["mk"].transpose(0, 3, 2, 1).reshape(2, 1, MEM, XH, XHD)
    mv = r["mv"].transpose(0, 2, 1, 3).reshape(2, 1, MEM, XH, XHD)
    return (y[None, :TP], y[TP:].reshape(NS, LS, D),
            state(rp), sh[None, :1], h[None, :1], conv[None, :1],
            k[:TP].reshape(1, 1, TP, 2, 64), v[:TP].reshape(1, 1, TP, 2, 64), ki[:TP].reshape(1, 1, TP, 32), mk, mv,
            rows(r["cv"]).T.reshape(1, NS, LS, AW), state(r["rs"]), sh[None, 1:], h[None, 1:], conv[None, 1:],
            k[TP:].reshape(1, NS, LS, 2, 64), v[TP:].reshape(1, NS, LS, 2, 64), ki[TP:].reshape(1, NS, LS, 32))
```

```python
from contextlib import ExitStack

import numpy as np

import concourse.bass as bass
from concourse import mybir

ALU = mybir.AluOpType
ACT = mybir.ActivationFunctionType
F32 = mybir.dt.float32
I32 = mybir.dt.int32
F32R = mybir.dt.float32r
AX_X = mybir.AxisListType.X
ds = bass.ds

P = 128
D = 1024
KT = D // P
TP, NS, LS = 512, 8, 8
TS = NS * LS
T = TP + TS
HT = T // 2
EPS = 1e-6
GN_EPS = 64e-5
PAST, PAGE, NPG = 2048, 128, 16
MEM = 256
XH, XHD = 4, 256
DFF = 2816
FT = DFF // P
AW = 512
WT = AW // P
A_G = 4
NCH, CH = 4, 128
RC = 64
NRC = TP // RC
LEVELS = 6
SLOTS = 4
SLOT = 1408
DECAY = float(np.exp(-0.5))
TOPK_P, TOPK_S = 128, 256
LK = PAST + LS
BIG = 1e30
TAKEN = -3e38
EW_T, OW_T = 22, 17

CREDIT = 1
CREDITED = ("c_yout", "x_outmm", "y_logits", "x_p", "y_p",
            "y_out", "x_out", "x_turned", "silu", "p_logits", "p_masked", "p_pt", "p_out",
            "p_turned", "p_outmm", "t_sum", "u_outmm", "u_exp", "u_out", "u_turned", "u_logits", "x_logits")

PCOL = {}
_n = 0
for _name, _w in (("mix0", 8), ("mix1", 8), ("x0", 8), ("x1", 8), ("mem0", 8), ("mem1", 8), ("ffn0", 8), ("ffn1", 8),
                  ("final", 8), ("ln_g", 4), ("ln_b", 4), ("mu", 14), ("w0", 4), ("a0", 4), ("k_k", 4), ("k_a", 4),
                  ("r_k", 4), ("gn_g", 4), ("gn_b", 4), ("conv_w", 16), ("conv_b", 4), ("bx", 4), ("ba", 4),
                  ("lam", 4)):
    PCOL[_name] = (_n, _w)
    _n += _w
NPAR = _n


def shape_constants():
    c = {}
    i = np.arange(P)
    f = lambda m: np.ascontiguousarray(m, np.float32)
    head = i // 64
    same = head[:, None] == head[None, :]
    c["ident"] = f(np.eye(P))
    c["heads"] = f(same)
    c["upper"] = f(i[:, None] <= i[None, :])
    s, t = i[:, None] % 64, i[None, :] % 64
    c["strict"] = f(same & (s < t))
    c["incl"] = f((s <= t)[:, :64])
    seq = same & (s // LS == t // LS)
    c["strict_s"] = f(seq & (s < t))
    c["incl_s"] = f(((s // LS == t // LS) & (s <= t))[:, :64])
    for l in range(LEVELS):
        b = 2 ** l
        c[f"level{l}"] = f(same & (s // (2 * b) == t // (2 * b)) & (s // b % 2 == 0) & (t // b % 2 == 1))
    c["causal"] = f(np.where(i[None, :] <= i[:, None], 0.0, -BIG))
    r64, r32 = np.zeros((P, P)), np.zeros((P, P))
    for o in range(P):
        d = o % 64
        if d < 8:
            r64[o + 8, o] = -1
        elif d < 16:
            r64[o - 8, o] = 1
        d = o % 32
        if d < 4:
            r32[o + 4, o] = -1
        elif d < 8:
            r32[o - 4, o] = 1
    c["rot64"], c["rot32"] = f(r64), f(r32)
    c["rep32"] = f(np.vstack([np.tile(np.eye(32), (1, 4)), np.zeros((96, P))]))
    c["rotrep"] = f(np.vstack([np.tile(r32[:32, :32], (1, 4)), np.zeros((96, P))]))
    e = np.zeros((P, 64))
    for h in range(8):
        e[32 + h, 8 * h:8 * h + 8] = 1
    c["spread"] = f(e)
    c["same_t"] = f(np.pad((i[:64, None] % 8 == i[None, :64] % 8), ((0, 64), (0, 0))))
    cn = np.zeros((P, LS))
    cn[:64] = np.where(np.arange(LS)[None, :] <= (i[:64] % LS)[:, None], 0.0, -BIG)
    c["causal_n"] = f(cn)
    eb = np.zeros((P, NS, 64))
    for b in range(NS):
        for r in range(64):
            eb[8 * b + r % 8, b, r] = 1
    c["mask_rows"] = f(eb.reshape(P, -1))
    c["seq_cols"] = f(np.broadcast_to((np.arange(64)[None, :] // LS == np.arange(NS)[:, None]).reshape(1, -1),
                                      (P, NS * 64)))
    c["seq_rows"] = f((i[:, None] % 64) // LS == np.arange(NS)[None, :])
    return c


def rotary(head, theta=500000.0):
    rot = head // 4
    half = rot // 2
    inv = (np.float32(theta) ** (-np.arange(half, dtype=np.float32) * np.float32(2.0) / np.float32(rot))).astype(np.float32)
    pos = np.concatenate([np.arange(TP), np.tile(PAST + np.arange(LS), NS)]).astype(np.float32)
    ang = (pos[:, None] * inv[None, :]).astype(np.float32)
    cos, sin = np.ones((P, T), np.float32), np.zeros((P, T), np.float32)
    for p in range(P):
        if p % head < rot:
            cos[p] = np.cos(ang[:, p % head % half])
            sin[p] = np.sin(ang[:, p % head % half])
    return cos, sin


CONST = shape_constants()
CCOL = {}
_n = 0
for _name, _a in CONST.items():
    CCOL[_name] = (_n, _a.shape[1])
    _n += _a.shape[1]
NCONST = _n


class Chain:

    def __init__(self, eng, sem):
        self.eng, self.sem, self.n, self.k = eng, sem, 0, 0

    def __call__(self, ins):
        ins.then_inc(self.sem, 1)
        self.n = self.n + 1
        self.k += 1
        self.eng.wait_ge(self.sem, self.n)

    def enter(self, i, per):
        self.base, self.per, self.k = self.n, per, 0
        self.n = i * per + self.base

    def leave(self, count):
        assert self.k == self.per, (self.k, self.per)
        self.n = self.base + count * self.per


class Gemm:

    blocks = 0
    outs = 0

    def __init__(self, src, n_out, kt, per_out=1):
        self.src, self.n_out, self.kt, self.per_out = src, n_out, kt, per_out
        self.g0, self.o0 = Gemm.blocks, Gemm.outs
        self.n = n_out * per_out
        Gemm.blocks += self.n
        Gemm.outs += n_out
        self.g1, self.o1 = Gemm.blocks, Gemm.outs

    def steps(self):
        at, left = 0, self.n
        if self.g0 == 0:
            yield 0, SLOTS, 1
            at, left = SLOTS, left - SLOTS
        if left // SLOTS:
            yield at, SLOTS, left // SLOTS
        at += left // SLOTS * SLOTS
        if left % SLOTS:
            yield at, left % SLOTS, 1


def build(nc, a, out):
    Gemm.blocks = Gemm.outs = 0
    ctx = ExitStack()
    sems = {}

    def S(name):
        if name not in sems:
            sems[name] = ctx.enter_context(nc.semaphore(name))
        return sems[name]

    with ctx:
        def sb(name, width):
            return ctx.enter_context(nc.sbuf_tensor(name, [P, width], F32))

        X = sb("X", KT * T)[:, :].rearrange("p (k t) -> p k t", k=KT)
        with nc.sbuf_tensor("PJ", [P, EW_T * T], F32) as PJt:
            pass
        HGH = ctx.enter_context(nc.sbuf_tensor("hidden_high", [P, FT * T], F32R))[:, :].rearrange("p (k t) -> p k t", k=FT)
        PJ = PJt[:, :].rearrange("p (k t) -> p k t", k=EW_T)
        with ExitStack() as other_stages:
            def for_other_stages(name, width):
                return other_stages.enter_context(nc.sbuf_tensor(name, [P, width], F32))
            PMt = for_other_stages("PM", 14 * T)
            Ht = for_other_stages("H", KT * T)
            cst = for_other_stages("cst", NCONST)
        for_gates = sb("for_gates", 2 * T)
        HGL = ctx.enter_context(nc.sbuf_tensor("hidden_low", [P, FT * T], F32R))[:, :].rearrange("p (k t) -> p k t", k=FT)
        for_constants = sb("for_constants", 14 * T + KT * T + NCONST - (2 + FT) * T)
        PM = PMt[:, :].rearrange("p (k t) -> p k t", k=14)
        H = Ht[:, :].rearrange("p (k t) -> p k t", k=KT)
        ring = sb("ring", SLOTS * SLOT)[:, :].rearrange("p (s n) -> p s n", s=SLOTS)
        par = sb("par", NPAR)
        ones = sb("ones", P)
        eps = sb("eps", 4)
        PT = ctx.enter_context(nc.sbuf_tensor("PT", [1, NS * NPG], I32))
        with nc.sbuf_tensor("SC", [P, 13720], F32) as SC:
            pass
        SPt = ctx.enter_context(nc.sbuf_tensor("split", [P, 2 * KT * T + 4 * D], F32R))
        HH = SPt[:, 0:KT * T].rearrange("p (k t) -> p k t", k=KT)
        HL = SPt[:, KT * T:2 * KT * T].rearrange("p (k t) -> p k t", k=KT)
        DW = FT // 2 * P
        DWH, DWL = (SPt[:, 2 * DW * x:2 * DW * (x + 1)].rearrange("p (s n) -> p s n", s=2) for x in range(2))
        WH, WL = (SPt[:, 2 * KT * T + 2 * D * x:2 * KT * T + 2 * D * (x + 1)].rearrange("p (s n) -> p s n", s=2) for x in range(2))
        ps = ctx.enter_context(nc.psum_tensor("ps", [P, 8, 512], F32))

        def C(name):
            o, w = CCOL[name]
            return cst[:, o:o + w]

        def G(name, k=0):
            o, _ = PCOL[name]
            return par[:, o + k:o + k + 1]

        def two(ap):
            return ap.rearrange("p (a b) -> p a b", a=2)

        def pair(b):
            return ps[:, b:b + 2, 0:HT]

        G_EIN = Gemm("w_ein", EW_T, KT)
        G_EOUT = Gemm("w_eout", KT, KT)
        layers = []
        for l in range(2):
            if l == 1:
                G_OIN = Gemm("w_oin", OW_T, KT)
            g = dict(k=Gemm(f"w_xk{l}", KT, KT), v=Gemm(f"w_xv{l}", KT, KT))
            if l == 1:
                G_OOUT = Gemm("w_oout", KT, KT)
            g |= dict(q=Gemm(f"w_xq{l}", KT, KT), o=Gemm(f"w_xo{l}", KT, KT), gu=Gemm(f"w_gu{l}", 2 * FT, KT),
                      d=Gemm(f"w_d{l}", KT, FT // 2, 2))
            layers.append(g)
        blocks_split = tiles_split = 0
        for g in (G_EIN, G_EOUT, layers[0]["o"], layers[0]["gu"], layers[0]["d"],
                  G_OIN, G_OOUT, layers[1]["o"], layers[1]["gu"], layers[1]["d"]):
            g.s0, g.h0 = blocks_split, tiles_split
            g.w_parts = (DWH, DWL) if g.per_out == 2 else (WH, WL)
            blocks_split += g.n
            tiles_split += g.kt * g.per_out

        LD = layers

        def weights_in(sp, g):
            src = a[g.src]
            w = g.kt * P
            for at, k, reps in g.steps():
                def body(it):
                    for j in range(k):
                        b = g.g0 + at + j
                        if b >= SLOTS or reps > 1:
                            sp.wait_ge(S("block_done"), it * SLOTS + (b - SLOTS + 1))
                        sp.dma_start(ring[:, b % SLOTS, 0:w], src[it * SLOTS + (at + j)]).then_inc(S(f"slot{b % SLOTS}"), 16)
                if reps == 1:
                    body(0)
                else:
                    with sp.Fori(0, reps) as it:
                        body(it)

        def weights_round(sp, g, r):
            for c in range(4 * r, 4 * r + 4):
                b = g.g0 + c
                sp.wait_ge(S("block_done"), b - SLOTS + 1)
                sp.dma_start(ring[:, b % SLOTS, 0:g.kt * P], a[g.src][c]).then_inc(S(f"slot{b % SLOTS}"), 16)

        def product(pe, g, rhs, norm=None):
            for at, k, reps in g.steps():
                def body(it):
                    for j in range(k):
                        b = g.g0 + at + j
                        o = g.o0 + (at + j) // g.per_out
                        sub = (at + j) % g.per_out
                        outs = SLOTS // g.per_out
                        pe.wait_ge(S(f"slot{b % SLOTS}"), it * 16 + 16 * (b // SLOTS + 1))
                        if sub == 0 and (o >= 2 or reps > 1):
                            pe.wait_ge(S("out_taken"), it * outs + (o - 1))
                        for kt in range(g.kt):
                            if norm is not None and at == 0 and j == 0:
                                pe.wait_ge(S("normed"), KT * norm + kt + 1)
                            for h in range(2):
                                mm = nc.tensor.matmul(ps[:, 2 * (o % 2) + h, 0:HT], ring[:, b % SLOTS, kt * P:(kt + 1) * P],
                                                      rhs[:, sub * g.kt + kt, h * HT:(h + 1) * HT],
                                                      start=(sub == 0 and kt == 0),
                                                      stop=(sub == g.per_out - 1 and kt == g.kt - 1))
                        mm.then_inc(S("block_done"), 1)
                if reps == 1:
                    body(0)
                else:
                    with pe.Fori(0, reps) as it:
                        body(it)

        def take(dve, g, dst, add):
            for at, k, reps in g.steps():
                def body(it):
                    for j in range(k):
                        if (at + j) % g.per_out != g.per_out - 1:
                            continue
                        b = g.g0 + at + j
                        o = (at + j) // g.per_out
                        bank = 2 * ((g.o0 + o) % 2)
                        dve.wait_ge(S("block_done"), it * SLOTS + (b + 1))
                        d = dst[:, ds(it * (SLOTS // g.per_out) + o, 1), :].rearrange("p o (a b) -> p (o a) b", a=2)
                        if add:
                            nc.vector.tensor_tensor(d, pair(bank), d, ALU.add).then_inc(S("out_taken"), 1)
                        else:
                            nc.vector.tensor_copy(d, pair(bank)).then_inc(S("out_taken"), 1)
                if reps == 1:
                    body(0)
                else:
                    with dve.Fori(0, reps) as it:
                        body(it)

        def rounds(eng, g, body):
            at = 0
            if g.g0 == 0:
                for c in range(4):
                    body(0, c)
                at = 4
            reps = (g.n - 2 - at) // 4
            with eng.Fori(0, reps) as it:
                for c in range(at, at + 4):
                    body(it, c)
            for c in range(at + 4 * reps, g.n):
                body(0, c)

        def split_product(pe, g, free=None):
            def body(it, c):
                o = g.o0 + c
                pe.wait_ge(S("w_low"), it * 4 + (g.s0 + c + 1))
                if free:
                    free(it, c)
                elif o >= 2:
                    pe.wait_ge(S("out_taken"), it * 4 + (o - 1))
                for kt in range(KT):
                    if c == 0:
                        pe.wait_ge(S("h_low"), g.h0 + kt + 1)
                    w = slice(kt * P, (kt + 1) * P)
                    for n, (lhsT, rhs) in enumerate(((WL, HH), (WH, HL), (WH, HH))):
                        for h in range(2):
                            mm = nc.tensor.matmul(ps[:, 2 * (o % 2) + h, 0:HT], lhsT[:, c % 2, w], rhs[:, kt, h * HT:(h + 1) * HT],
                                                  start=(kt == 0 and n == 0), stop=(kt == KT - 1 and n == 2))
                mm.then_inc(S("block_done"), 1)
            rounds(pe, g, body)

        def high(act, g, it, c):
            b = g.g0 + c
            act.wait_ge(S(f"slot{b % SLOTS}"), it * 16 + 16 * (b // SLOTS + 1))
            if b >= 2:
                act.wait_ge(S("block_done"), it * 4 + (b - 1))
            nc.scalar.activation(g.w_parts[0][:, c % 2, :], ring[:, b % SLOTS, 0:g.kt * P], ACT.Copy).then_inc(S("w_high"), 1)

        def low(dve, g, it, c):
            dve.wait_ge(S("w_high"), it * 4 + (g.s0 + c + 1))
            wh, wl = g.w_parts
            nc.vector.tensor_tensor(wl[:, c % 2, :], ring[:, (g.g0 + c) % SLOTS, 0:g.kt * P], wh[:, c % 2, :], ALU.subtract)\
              .then_inc(S("w_low"), 1)

        def split_high(act, g, ready=None, step=None, after=None):
            for c in range(2):
                high(act, g, 0, c)
            for k in range(KT):
                if ready:
                    ready(k)
                nc.scalar.activation(HH[:, k, :], H[:, k, :], ACT.Copy).then_inc(S("h_high"), 1)

            def body(it, c):
                act.wait_ge(S("block_done"), it * 4 + (g.g0 + c + 1))
                if step:
                    step(it, c)
                if not (isinstance(it, int) and c + 2 >= g.n):
                    high(act, g, it, c + 2)
                if after:
                    after(it, c)
            rounds(act, g, body)

        def low_tile(dve, g, k):
            dve.wait_ge(S("h_high"), g.h0 + k + 1)
            nc.vector.tensor_tensor(HL[:, k, :], H[:, k, :], HH[:, k, :], ALU.subtract).then_inc(S("h_low"), 1)

        def split_low(dve, g):
            low(dve, g, 0, 0)
            for k in range(KT):
                low_tile(dve, g, k)
            low(dve, g, 0, 1)

        def split_take(dve, g, dst=None, add=False, step=None, after=None):
            def take_one(it, c):
                bank = 2 * ((g.o0 + c) % 2)
                dve.wait_ge(S("block_done"), it * 4 + (g.g0 + c + 1))
                d = dst[:, ds(it * 4 + c, 1), :].rearrange("p o (a b) -> p (o a) b", a=2)
                if add:
                    nc.vector.tensor_tensor(d, pair(bank), d, ALU.add).then_inc(S("out_taken"), 1)
                else:
                    nc.vector.tensor_copy(d, pair(bank)).then_inc(S("out_taken"), 1)

            def body(it, c):
                (step or take_one)(it, c)
                if not (isinstance(it, int) and c + 2 >= g.n):
                    low(dve, g, it, c + 2)
                if after:
                    after(it, c)
            rounds(dve, g, body)

        def normed_tiles(act, n):
            return lambda k: act.wait_ge(S("normed"), KT * n + k + 1)

        SQ = PM[:, 0:KT, :]
        RMS = PM[:, KT, :]
        RINV = PM[:, KT + 1, :]

        def norm_act(act, n, x_ready):
            x_ready(act)
            for k in range(0, KT, 2):
                nc.scalar.activation(SQ[:, k, :], X[:, k, :], ACT.Square).then_inc(S("square_even"), 1)
            act.wait_ge(S("norm_sum"), n + 1)
            nc.scalar.activation(two(RMS), pair(4), ACT.Sqrt, bias=eps[:, 0:1], scale=1.0 / D).then_inc(S("norm_root"), 1)

        def norm_pe(pe, n):
            for k in range(KT):
                pe.wait_ge(S("square_odd" if k % 2 else "square_even"), 4 * n + k // 2 + 1)
                for h in range(2):
                    mm = nc.tensor.matmul(ps[:, 4 + h, 0:HT], ones[:, :], SQ[:, k, h * HT:(h + 1) * HT],
                                          start=(k == 0), stop=(k == KT - 1))
            mm.then_inc(S("norm_sum"), 1)

        def norm_dve(dve, n, x_ready, gain, link, g=None):
            x_ready(dve)
            for k in range(1, KT, 2):
                nc.vector.tensor_tensor(SQ[:, k, :], X[:, k, :], X[:, k, :], ALU.mult).then_inc(S("square_odd"), 1)
            dve.wait_ge(S("norm_root"), n + 1)
            link(nc.vector.reciprocal(RINV, RMS))
            if g:
                low(dve, g, 0, 0)
            for k in range(KT + 1):
                if k < KT:
                    nc.vector.scalar_tensor_tensor(H[:, k, :], X[:, k, :], G(gain, k), RINV, ALU.mult, ALU.mult)\
                      .then_inc(S("normed"), 1)
                if g and k:
                    low_tile(dve, g, k - 1)
            if g:
                low(dve, g, 0, 1)

        def taken(g):
            return lambda eng: eng.wait_ge(S("out_taken"), g.o1)

        A_V = PJ[:, 4:8, :]
        A_U = PJ[:, 0:4, :]
        A_SQ = PM[:, 0:4, :]
        A_MU = PM[:, 4, :]
        A_VT = PMt[:, 5 * T:5 * T + 5 * 512].rearrange("p (c n) -> p c n", c=5)
        WS = SC[:, 0:512].rearrange("p (g t) -> p g t", g=4)
        WSS = SC[0:TS, 512:768].rearrange("p (g t) -> p g t", g=4)
        BS = SC[0:1, 768:1280]
        BSS = SC[0:1, 1280:1536]

        def bc(ap, n):
            return ap.unsqueeze(1).broadcast_to([ap.shape[0], n, ap.shape[1]])

        def a_act(act):
            taken(G_EIN)(act)
            nc.scalar.activation(A_V, A_V, ACT.Gelu_apprx_tanh).then_inc(S("a_gelu"), 1)
            nc.scalar.activation(A_U, A_U, ACT.Gelu_apprx_tanh).then_inc(S("a_gelu"), 1)
            act.wait_ge(S("a_products"), 2)
            nc.scalar.activation(two(A_MU), pair(6), ACT.Sqrt, bias=eps[:, 0:1], scale=1.0 / AW).then_inc(S("a_root"), 1)

        def column_sums(pe, src, bank, lhsT, n=4):
            for k in range(n):
                for h in range(2):
                    mm = nc.tensor.matmul(ps[:, bank + h, 0:HT], lhsT, src[:, k, h * HT:(h + 1) * HT],
                                          start=(k == 0), stop=(k == n - 1))
            return mm

        def a_pe(pe):
            pe.wait_ge(S("a_gelu"), 1)
            column_sums(pe, A_V, 4, ones[:, :]).then_inc(S("a_products"), 1)
            pe.wait_ge(S("a_squares"), 1)
            column_sums(pe, A_SQ, 6, ones[:, :]).then_inc(S("a_products"), 1)
            pe.wait_ge(S("a_normed"), 1)
            for c in range(5):
                n = CH if c < NCH else TS
                for g in range(4):
                    mm = nc.tensor.transpose(ps[0:n, c, g * P:(g + 1) * P], A_V[:, g, c * CH:c * CH + n], C("ident"))
            mm.then_inc(S("a_products"), 1)
            pe.wait_ge(S("a_rows"), 2)
            for g in range(4):
                for c in range(NCH):
                    o = ps[:, g, c * CH:(c + 1) * CH]
                    nc.tensor.matmul(o, A_VT[:, c, g * P:(g + 1) * P], WS[:, g, :], start=True, stop=False)
                    nc.tensor.matmul(o, ones[0:1, :], BS[:, g * CH:(g + 1) * CH], start=False, stop=True)
                o = ps[:, 4, g * TS:(g + 1) * TS]
                nc.tensor.matmul(o, A_VT[0:TS, 4, g * P:(g + 1) * P], WSS[:, g, :], start=True, stop=False)
                mm = nc.tensor.matmul(o, ones[0:1, :], BSS[:, g * TS:(g + 1) * TS], start=False, stop=True)
            mm.then_inc(S("a_products"), 1)

        def a_dve(dve, link):
            dve.wait_ge(S("a_products"), 1)
            link(nc.vector.tensor_scalar(two(A_MU), pair(4), 1.0 / AW, None, ALU.mult))
            dve.wait_ge(S("a_gelu"), 1)
            link(nc.vector.tensor_tensor(A_V, A_V, bc(A_MU, 4), ALU.subtract))
            nc.vector.tensor_tensor(A_SQ, A_V, A_V, ALU.mult).then_inc(S("a_squares"), 1)
            dve.wait_ge(S("a_root"), 1)
            link(nc.vector.reciprocal(A_MU, A_MU))
            link(nc.vector.tensor_tensor(A_V, A_V, bc(A_MU, 4), ALU.mult))
            for k in range(4):
                ins = nc.vector.tensor_scalar(A_V[:, k, :], A_V[:, k, :], G("ln_g", k), G("ln_b", k), ALU.mult, ALU.add)
                if k < 3:
                    link(ins)
            ins.then_inc(S("a_normed"), 1)
            dve.wait_ge(S("a_in"), 64)
            link(nc.vector.tensor_tensor(WS, WS, bc(C("upper"), 4), ALU.mult))
            link(nc.vector.tensor_tensor(WSS, WSS, bc(C("upper")[0:TS, 0:TS], 4), ALU.mult))
            dve.wait_ge(S("a_products"), 3)
            nc.vector.tensor_copy(A_VT[:, 0:4, :], ps[:, 0:4, :]).then_inc(S("a_rows"), 1)
            nc.vector.tensor_copy(A_VT[0:TS, 4, :], ps[0:TS, 4, :]).then_inc(S("a_rows"), 1)
            dve.wait_ge(S("a_products"), 4)
            dve.wait_ge(S("a_gelu"), 2)
            nc.vector.tensor_tensor(H[:, 0:4, 0:TP], A_U[:, :, 0:TP], ps[:, 0:4, :], ALU.mult).then_inc(S("a_out"), 1)
            nc.vector.tensor_tensor(H[:, 0:4, TP:T], A_U[:, :, TP:T],
                                    ps[:, 4, 0:4 * TS].rearrange("p (g t) -> p g t", g=4), ALU.mult).then_inc(S("a_out"), 1)

        PB = PJ[:, 8:22, :]
        R, K, V = PM[:, 0:4, :], PM[:, 4:8, :], PM[:, 8:12, :]
        WA, GL = PM[:, 12, :], PM[:, 13, :]
        KI, LC = PJ[:, 0:4, :], PJ[:, 4:8, :]
        KD, BI, GT = PJ[:, 8:12, :], PJ[:, 12:16, :], PJ[:, 16:20, :]
        RD = H[:, 4:8, :]
        LORA = SC[:, 1536:1536 + 1024]
        SH0 = SC[:, 2560:2560 + 14 * NS].rearrange("p (k b) -> p k b", k=14)
        RESET = SC[:, 2700:2700 + T]
        AK = SC[:, 0:4 * T].rearrange("p (k t) -> p k t", k=4)
        SHO = SC[:, 13584:13584 + 14 * 9].rearrange("p (k b) -> p k b", k=14)
        at = [0]

        def carve(n):
            v = SC[:, at[0]:at[0] + n]
            at[0] += n
            return v
        f4 = lambda ap: ap.rearrange("p (q n) -> p q n", q=4)
        XBt = carve(2048)
        XB = XBt.rearrange("p (x q n) -> p x q n", x=4, q=4)
        TM = carve(2048).rearrange("p (x q n) -> p x q n", x=4, q=4)
        ALt = carve(2560)
        AL = ALt.rearrange("p (l q n) -> p l q n", l=5, q=4)
        MTb, Mb, Yb, Gb, W1, Ub, Sb, AKK = (f4(carve(512)) for _ in range(8))
        ARt = carve(512).rearrange("p (q x n) -> p q x n", q=4, x=2)
        RDc = f4(carve(256))
        PC = carve(4)
        S0 = carve(NS * 256).rearrange("p (b q n) -> p b q n", b=NS, q=4)
        assert at[0] <= 13584, at
        W1b, Ub2, Vb2, Sbb = (f4(ALt[:, n * 512:(n + 1) * 512]) for n in range(4))

        def seqs(ap):
            return ap.rearrange("p k (b t) -> p k b t", b=NS)

        def b_pre_dve(dve, link):
            taken(G_EIN)(dve)
            dve.wait_ge(S("a_products"), 4)
            dve.wait_ge(S("b_in"), 80)
            PMa = PM[:, :, :]
            link(nc.vector.tensor_tensor(PMa[:, :, 1:TP], PB[:, :, 0:TP - 1], PB[:, :, 1:TP], ALU.subtract))
            link(nc.vector.tensor_scalar(PMa[:, :, 0:1], PB[:, :, 0:1], -1.0, None, ALU.mult))
            s, d = PB[:, :, TP:T], PMa[:, :, TP:T]
            for t in range(1, LS):
                nc.vector.tensor_tensor(seqs(d)[:, :, :, t], seqs(s)[:, :, :, t - 1], seqs(s)[:, :, :, t], ALU.subtract)\
                  .then_inc(S("b_shift"), 1)
            nc.vector.tensor_tensor(seqs(d)[:, :, :, 0], SH0, seqs(s)[:, :, :, 0], ALU.subtract).then_inc(S("b_shift"), 1)
            dve.wait_ge(S("b_shift"), LS)
            for k in (12, 13, 0, 1, 2, 3, 4, 5, 6, 7, 8, 9, 10, 11):
                nc.vector.scalar_tensor_tensor(PM[:, k, :], PM[:, k, :], G("mu", k), PB[:, k, :], ALU.mult, ALU.add)\
                  .then_inc(S("b_mixed"), 1)
            nc.vector.tensor_copy(SHO[:, :, 0:1], PB[:, :, TP - 1:TP]).then_inc(S("b_shift"), 1)
            nc.vector.tensor_copy(SHO[:, :, 1:9], seqs(PB[:, :, TP:T])[:, :, :, LS - 1]).then_inc(S("b_shift"), 1)
            dve.wait_ge(S("b_shift"), LS + 2)
            dve.wait_ge(S("b_mixed"), 14)
            dve.wait_ge(S("cv_stored"), 16)
            dve.wait_ge(S("b_sig"), 6)
            link(nc.vector.tensor_scalar(KD, KD, -DECAY, None, ALU.mult))
            for k in range(4):
                nc.vector.tensor_tensor_scan(LC[:, k, :], RESET, KD[:, k, :], 0.0, ALU.mult, ALU.add).then_inc(S("b_scan"), 1)
            dve.wait_ge(S("b_sig"), 10)
            dve.wait_ge(S("b_products"), 3)
            nc.vector.tensor_copy(GT, all_banks).then_inc(S("b_gate"), 1)
            for k in range(4):
                nc.vector.tensor_scalar(KI[:, k, :], K[:, k, :], G("k_k", k), None, ALU.mult).then_inc(S("b_kk"), 1)
            dve.wait_ge(S("b_kk"), 4)
            nc.vector.tensor_tensor(RD, KI, KI, ALU.mult).then_inc(S("b_kk"), 1)
            dve.wait_ge(S("b_scan"), 4)
            nc.vector.tensor_tensor(KD, LC, KD, ALU.subtract).then_inc(S("b_before"), 1)
            for k in range(4):
                link(nc.vector.tensor_scalar(AK[:, k, :], BI[:, k, :], -1.0, G("k_a", k), ALU.add, ALU.mult))
                link(nc.vector.scalar_tensor_tensor(K[:, k, :], AK[:, k, :], 1.0, K[:, k, :], ALU.add, ALU.mult))
            dve.wait_ge(S("b_root"), 1)
            link(nc.vector.reciprocal(RD, RD))
            link(nc.vector.tensor_tensor(KI, KI, RD, ALU.mult))
            nc.vector.tensor_tensor(BI, BI, KI, ALU.mult).then_inc(S("b_before"), 1)
            dve.wait_ge(S("b_decay"), 1)
            link(nc.vector.tensor_tensor(KD, KD, KI, ALU.mult))
            dve.wait_ge(S("b_decay"), 2)
            link(nc.vector.tensor_tensor(BI, BI, RD, ALU.mult))
            link(nc.vector.tensor_tensor(KI, K, RD, ALU.mult))
            dve.wait_ge(S("b_decay"), 3)
            link(nc.vector.tensor_tensor(RD, R, LC, ALU.mult))

        all_banks = ps[:, :, 0:HT]

        def b_pre_act(act):
            act.wait_ge(S("b_mixed"), 2)
            nc.scalar.activation(WA[0:64, :], WA[0:64, :], ACT.Tanh).then_inc(S("b_sig"), 1)
            nc.scalar.activation(GL, GL, ACT.Sigmoid).then_inc(S("b_sig"), 1)
            act.wait_ge(S("b_products"), 1)
            act.wait_ge(S("b_shift"), LS + 2)
            act.wait_ge(S("b_mixed"), 14)
            for k in range(4):
                nc.scalar.activation(two(KD[:, k, :]), pair(2 * k), ACT.Sigmoid, bias=G("w0", k)).then_inc(S("b_sig"), 1)
            act.wait_ge(S("b_products"), 2)
            for k in range(4):
                nc.scalar.activation(two(BI[:, k, :]), pair(2 * k), ACT.Sigmoid, bias=G("a0", k)).then_inc(S("b_sig"), 1)
            act.wait_ge(S("b_products"), 4)
            nc.scalar.activation(RD.rearrange("p k (a b) -> p (k a) b", a=2), all_banks, ACT.Sqrt, bias=eps[:, 2:3])\
              .then_inc(S("b_root"), 1)
            act.wait_ge(S("b_before"), 1)
            nc.scalar.activation(KD, KD, ACT.Exp).then_inc(S("b_decay"), 1)
            act.wait_ge(S("b_before"), 2)
            nc.scalar.activation(RD, LC, ACT.Exp, scale=-1.0).then_inc(S("b_decay"), 1)
            act.wait_ge(S("b_decay"), 2)
            nc.scalar.activation(LC, LC, ACT.Exp).then_inc(S("b_decay"), 1)

        def b_pre_pe(pe):
            def lora(lhs_rows, cols, rhs):
                for k in range(4):
                    for h in range(2):
                        mm = nc.tensor.matmul(ps[:, 2 * k + h, 0:HT], LORA[lhs_rows, cols + k * P:cols + (k + 1) * P],
                                              rhs[:, h * HT:(h + 1) * HT], start=True, stop=True)
                mm.then_inc(S("b_products"), 1)

            pe.wait_ge(S("a_out"), 2)
            pe.wait_ge(S("b_sig"), 1)
            pe.wait_ge(S("b_mixed"), 2)
            lora(slice(0, 64), 0, WA[0:64, :])
            pe.wait_ge(S("b_sig"), 6)
            lora(slice(64, 128), 0, WA[64:128, :])
            pe.wait_ge(S("b_sig"), 10)
            lora(slice(0, 128), 512, GL)
            pe.wait_ge(S("b_kk"), 5)
            pe.wait_ge(S("b_gate"), 1)
            head_sums(RD).then_inc(S("b_products"), 1)

        def head_sums(src):
            for k in range(4):
                for h in range(2):
                    mm = nc.tensor.matmul(ps[:, 2 * k + h, 0:HT], C("heads"), src[:, k, h * HT:(h + 1) * HT],
                                          start=True, stop=True)
            return mm

        heads3 = C("heads").rearrange("p (h t) -> p h t", h=2)

        def banks(b):
            return f4(ps[:, b, :])

        def spread(dst, src, mask=None):
            d = dst.rearrange("p q (h t) -> p q h t", h=2)
            s = src.unsqueeze(2).broadcast_to([P, 4, 2, 64])
            m = heads3.unsqueeze(1).broadcast_to([P, 4, 2, 64]) if mask is None else mask
            return nc.vector.tensor_tensor(d, s, m, ALU.mult)

        def mm4(bank, lhsT, rhs, start=True, stop=True):
            for q in range(4):
                mm = nc.tensor.matmul(banks(bank)[:, q, :], lhsT[:, q, :], rhs[:, q, :], start=start, stop=stop)
            return mm

        STREAMS = [slice(0, 2), slice(2, 4)]

        def stream(b, s):
            return banks(b)[:, 0:2, :]

        def turn_pe(pe, n, k):
            pe.wait_ge(S("c_spread"), 6 * n + (6 * k + 4))
            for x in range(4):
                for q in range(4):
                    mm = nc.tensor.transpose(banks(x)[:, q, :], XB[:, x, q, :], C("ident"))
            mm.then_inc(S("c_turned"), 1)

        def chunk_pe(pe, n, levels, sample):
            W = lambda sem, v: pe.wait_ge(S(sem), v)
            mm4(4, XB[:, 1], XB[:, 0])
            W("c_yout", n + CREDIT)
            mm4(5, XB[:, 2], XB[:, 0])
            W("c_spread", 6 * n + 6)
            for q in range(4):
                o = ps[:, 6, q * P:(q + 1) * P]
                nc.tensor.matmul(o[:, 0:64], XB[:, 1, q, :], RDc[:, q, :], start=True, stop=True)
                mm = nc.tensor.matmul(o[:, 64:128], XB[:, 2, q, :], RDc[:, q, :], start=True, stop=True)
            mm.then_inc(S("c_products"), 1)
            W("c_mt0", n + 1)
            for q in range(4):
                mm = nc.tensor.transpose(banks(7)[:, q, :], MTb[:, q, :], C("ident"))
            mm.then_inc(S("c_mturned"), 1)
            W("c_m0", n + 1)
            W("c_tm", n + 1)
            W("c_masked", 3 * n + 3)
            for l in range(1, levels):
                k = 5 * n + l
                W("c_level", k)
                for s, qs in enumerate(STREAMS):
                    if l > 1:
                        W("c_inverse", 4 * k + (2 * s - 6))
                    for j, q in enumerate(range(4)[qs]):
                        mm = nc.tensor.matmul(stream(3 * s, s)[:, j, :], AL[:, l - 1, q, :], Mb[:, q, :], start=True, stop=True)
                    mm.then_inc(S("c_ymm"), 1)
                for s, qs in enumerate(STREAMS):
                    W("c_y", 2 * k + (s - 1))
                    for j, q in enumerate(range(4)[qs]):
                        nc.tensor.matmul(stream(3 * s + 1, s)[:, j, :], Yb[:, q, :], MTb[:, q, :], start=True, stop=True)
                    for j, q in enumerate(range(4)[qs]):
                        mm = nc.tensor.matmul(stream(3 * s + 2, s)[:, j, :], MTb[:, q, :], Yb[:, q, :], start=True, stop=True)
                    mm.then_inc(S("c_mm"), 1)
            W("c_inverse", 4 * (5 * n + levels - 1))
            mm4(6, TM[:, 0], MTb)
            mm4(7, AKK, TM[:, 3]).then_inc(S("c_w1mm"), 1)
            if sample:
                return
            W("c_g", n + 1)
            W("c_w1", n + 1)
            for q in range(4):
                nc.tensor.matmul(banks(4)[:, q, :], W1[:, q, :], Sb[:, q, :], start=True, stop=False)
                mm = nc.tensor.matmul(banks(4)[:, q, :], MTb[:, q, :], Gb[:, q, :], start=False, stop=True)
            mm.then_inc(S("c_umm"), 1)
            turn_pe(pe, n, 1)
            W("c_u", n + 1)
            for q in range(4):
                o = ps[:, 5, q * 64:(q + 1) * 64]
                nc.tensor.matmul(o, Sb[:, q, :], RDc[:, q, :], start=True, stop=False)
                nc.tensor.matmul(o, Ub[:, q, :], ARt[:, q, 0, :], start=False, stop=False)
                mm = nc.tensor.matmul(o, TM[:, 3, q, :], ARt[:, q, 1, :], start=False, stop=True)
            for q in range(4):
                nc.tensor.matmul(banks(7)[:, q, :], TM[:, 1, q, :], Ub[:, q, :], start=True, stop=False)
                mm = nc.tensor.matmul(banks(7)[:, q, :], TM[:, 2, q, :], TM[:, 3, q, :], start=False, stop=True)
            mm.then_inc(S("c_smm"), 1)

        def chunk_act(act, n, levels, sample):
            act.wait_ge(S("c_turned"), n + 1)
            nc.scalar.activation(TM.rearrange("p x q n -> p x (q n)"), ps[:, 0:4, :], ACT.Copy).then_inc(S("c_tm"), 1)
            for l in range(1, levels):
                for s, qs in enumerate(STREAMS):
                    act.wait_ge(S("c_ymm"), 2 * (5 * n + l) + (s - 1))
                    nc.scalar.activation(Yb[:, qs], stream(3 * s, s), ACT.Copy).then_inc(S("c_y"), 1)
            act.wait_ge(S("c_w1mm"), n + 1)
            nc.scalar.activation(W1, banks(6), ACT.Copy).then_inc(S("c_w1"), 1)
            if sample:
                return
            act.wait_ge(S("c_smm"), n + 1)
            nc.scalar.activation(KD[:, :, ds(n * 64, 64)], ps[:, 5, 0:256].rearrange("p (q t) -> p q t", q=4),
                                 ACT.Copy).then_inc(S("c_yout"), 1)

        def chunk_pool(pool, n, levels, sample):
            pool.wait_ge(S("c_at"), n + 1)
            for l in range(1, levels):
                nc.gpsimd.tensor_tensor(AL[:, l - 1], AT4, bc(C(f"level{l}"), 4), ALU.mult).then_inc(S("c_level"), 1)

        AT4 = Ub

        def spread_x(x, n, k):
            spread(XB[:, x], (KD, BI, KI, V)[x][:, :, ds(n * 64 + 64 * k, 64)]).then_inc(S("c_spread"), 1)

        def chunk_rest(n, k):
            nc.vector.tensor_copy(RDc, RD[:, :, ds(n * 64 + 64 * k, 64)]).then_inc(S("c_spread"), 1)
            nc.vector.tensor_copy(PC, LC[:, :, ds(n * 64 + (64 * k + 63), 1)].rearrange("p q o -> p (q o)"))\
              .then_inc(S("c_spread"), 1)

        def chunk_dve(dve, n, levels, sample, link):
            strict, incl = (C("strict_s"), C("incl_s")) if sample else (C("strict"), C("incl"))
            dve.wait_ge(S("c_products"), n + 1)
            nc.vector.tensor_tensor(AT4, banks(4), bc(strict, 4), ALU.mult).then_inc(S("c_at"), 1)
            dve.wait_ge(S("c_at"), n + 1)
            link(nc.vector.tensor_tensor(MTb, AT4, bc(C("level0"), 4), ALU.mult))
            nc.vector.tensor_tensor(MTb, bc(C("ident"), 4), MTb, ALU.subtract).then_inc(S("c_mt0"), 1)
            nc.vector.tensor_tensor(AKK, banks(5), bc(strict, 4), ALU.mult).then_inc(S("c_masked"), 1)
            for x in range(2):
                nc.vector.tensor_tensor(ARt[:, :, x, :], banks(6)[:, :, 64 * x:64 * x + 64], bc(incl, 4), ALU.mult)\
                  .then_inc(S("c_masked"), 1)
            dve.wait_ge(S("c_mturned"), n + 1)
            nc.vector.tensor_copy(Mb, banks(7)).then_inc(S("c_m0"), 1)
            for l in range(1, levels):
                if not sample and 2 <= l < 6:
                    spread_x(l - 2, n, 1)
                for s, qs in enumerate(STREAMS):
                    dve.wait_ge(S("c_mm"), 2 * (5 * n + l) + (s - 1))
                    nc.vector.tensor_tensor(MTb[:, qs], MTb[:, qs], stream(3 * s + 1, s), ALU.subtract).then_inc(S("c_inverse"), 1)
                    nc.vector.tensor_tensor(Mb[:, qs], Mb[:, qs], stream(3 * s + 2, s), ALU.subtract).then_inc(S("c_inverse"), 1)
            dve.wait_ge(S("c_w1mm"), n + 1)
            nc.vector.tensor_copy(Gb, banks(7)).then_inc(S("c_g"), 1)
            if sample:
                return
            dve.wait_ge(S("c_umm"), n + 1)
            nc.vector.tensor_scalar(Ub, banks(4), -1.0, None, ALU.mult).then_inc(S("c_u"), 1)
            dve.wait_ge(S("c_smm"), n + 1)
            link(nc.vector.tensor_tensor(Sb, Sb, banks(7), ALU.add))
            link(nc.vector.tensor_tensor(Sb, Sb, PC.unsqueeze(2).broadcast_to([P, 4, P]), ALU.mult))
            chunk_rest(n, 1)

        def sample_state_pe(pe):
            pe.wait_ge(S("c_g"), NRC + 1)
            pe.wait_ge(S("c_w1"), NRC + 1)
            for q in range(4):
                nc.tensor.matmul(ps[:, q, 0:P], MTb[:, q, :], Gb[:, q, :], start=True, stop=True)
                nc.tensor.matmul(ps[:, 4 + q, 0:64], TM[:, 3, q, :], ARt[:, q, 1, :], start=True, stop=True)
            with pe.Fori(0, NS // 2) as b2:
                for i, (w, st) in enumerate(READ):
                    b = b2 * 2
                    pe.wait_ge(S("s_operands"), b * 2 + (2 * i + 2))
                    for q in range(4):
                        nc.tensor.matmul(ps[:, q, 0:P], w[:, q, :], st[:, q, :], start=False, stop=True,
                                         skip_group_check=True)
                        mm = nc.tensor.matmul(ps[:, 4 + q, ds(b * LS + i * LS, LS)], st[:, q, :], RDc[:, q, ds(b * LS + i * LS, LS)],
                                              start=False, stop=True, skip_group_check=True)
                    mm.then_inc(S("s_read"), 1)
            pe.wait_ge(S("c_u"), NRC + 1)
            for q in range(4):
                mm = nc.tensor.matmul(ps[:, 4 + q, 0:64], Ub[:, q, :], ARt[:, q, 0, :], start=False, stop=True,
                                      skip_group_check=True)
            mm.then_inc(S("s_ymm"), 1)
            with pe.Fori(0, NS // 2) as b2:
                for i, (u, v) in enumerate(WRITE):
                    pe.wait_ge(S("s_rows"), b2 * 4 + (2 * i + 2))
                    for q in range(4):
                        nc.tensor.matmul(banks(i)[:, q, :], TM[:, 1, q, :], u[:, q, :], start=True, stop=False)
                        mm = nc.tensor.matmul(banks(i)[:, q, :], TM[:, 2, q, :], v[:, q, :], start=False, stop=True)
                    mm.then_inc(S("s_smm"), 1)

        READ = [(W1b, Sbb), (Ub2, Vb2)]
        WRITE = [(Ub2, Vb2), (W1b, Sbb)]

        def sample_state_dve(dve, link):
            def operands(b, i):
                w, st = READ[i]
                m = seq_cols[:, ds(b + i, 1), :].broadcast_to([P, 8, 64])
                nc.vector.tensor_tensor(w.rearrange("p q (h t) -> p (q h) t", h=2), W1.rearrange("p q (h t) -> p (q h) t", h=2),
                                        m, ALU.mult).then_inc(S("s_operands"), 1)
                spread(st, S0[:, ds(b + i, 1), :, :].rearrange("p o q n -> p (o q) n")).then_inc(S("s_operands"), 1)

            def rows(b, i):
                row = C("seq_rows")[:, ds(b + i, 1)]
                for dst, src in zip(WRITE[i % 2], (Ub, TM[:, 3])):
                    nc.vector.tensor_scalar(dst, src, row, None, ALU.mult).then_inc(S("s_rows"), 1)

            def state(b, i):
                dve.wait_ge(S("s_smm"), b + (i + 1))
                sb_ = S0[:, ds(b + i, 1), :, :].rearrange("p o q n -> p (o q) n")
                for hh in range(2):
                    r = slice(64 * hh, 64 * hh + 64)
                    link(nc.vector.tensor_tensor(sb_[r], sb_[r], banks(i)[r, :, 64 * hh:64 * hh + 64], ALU.add))
                end = LC[:, :, ds(b * LS + (TP + LS - 1 + i * LS), 1)].broadcast_to([P, 4, 64])
                nc.vector.tensor_tensor(sb_, sb_, end, ALU.mult).then_inc(S("s_state"), 1)

            dve.wait_ge(S("c_w1"), NRC + 1)
            for i in range(2):
                operands(0, i)
            with dve.Fori(1, NS // 2) as b2:
                for i in range(2):
                    dve.wait_ge(S("s_read"), b2 * 2 + (i - 1))
                    operands(b2 * 2, i)
            dve.wait_ge(S("s_read"), NS)
            nc.vector.tensor_scalar(Ub, ps[:, 0:4, 0:P], -1.0, None, ALU.mult).then_inc(S("c_u"), 1)
            dve.wait_ge(S("c_u"), NRC + 1)
            rows(0, 0)
            dve.wait_ge(S("s_ymm"), 1)
            link(nc.vector.tensor_copy(KD[:, :, TP:T], ps[:, 4:8, 0:64]))
            with dve.Fori(0, NS // 2 - 1) as b2:
                link.enter(b2, 4)
                for i in range(2):
                    rows(b2 * 2, i + 1)
                    state(b2 * 2, i)
            link.leave(NS // 2 - 1)
            rows(NS - 2, 1)
            state(NS - 2, 0)
            state(NS - 2, 1)

        seq_cols = C("seq_cols").rearrange("p (b t) -> p b t", b=NS)

        def b_post_dve(dve, link):
            dve.wait_ge(S("b_products"), 5)
            flat = lambda v: v.rearrange("p k (a b) -> p (k a) b", a=2)
            link(nc.vector.scalar_tensor_tensor(flat(KD), all_banks, -1.0 / 64, flat(KD), ALU.mult, ALU.add))
            nc.vector.tensor_tensor(RD, KD, KD, ALU.mult).then_inc(S("b_ysq"), 1)
            for k in range(4):
                nc.vector.scalar_tensor_tensor(KI[:, k, :], R[:, k, :], G("r_k", k), K[:, k, :], ALU.mult, ALU.mult)\
                  .then_inc(S("b_bonus"), 1)
            dve.wait_ge(S("b_root"), 2)
            link(nc.vector.reciprocal(LC, LC))
            link(nc.vector.tensor_tensor(KD, KD, LC, ALU.mult))
            for k in range(4):
                link(nc.vector.tensor_scalar(KD[:, k, :], KD[:, k, :], G("gn_g", k), G("gn_b", k), ALU.mult, ALU.add))
            dve.wait_ge(S("b_products"), 7)
            link(nc.vector.tensor_tensor(flat(RD), all_banks, flat(V), ALU.mult))
            link(nc.vector.tensor_tensor(RD, RD, KD, ALU.add))
            nc.vector.tensor_tensor(RD, RD, GT, ALU.mult).then_inc(S("b_out"), 1)

        def b_post_pe(pe):
            pe.wait_ge(S("c_yout"), NRC + CREDIT)
            pe.wait_ge(S("s_state"), NS)
            head_sums(KD).then_inc(S("b_products"), 1)
            pe.wait_ge(S("b_ysq"), 1)
            head_sums(RD).then_inc(S("b_products"), 1)
            pe.wait_ge(S("b_root"), 2)
            pe.wait_ge(S("b_bonus"), 4)
            head_sums(KI).then_inc(S("b_products"), 1)

        def b_post_act(act):
            act.wait_ge(S("b_products"), 6)
            nc.scalar.activation(LC.rearrange("p k (a b) -> p (k a) b", a=2), all_banks, ACT.Sqrt, bias=eps[:, 1:2],
                                 scale=1.0 / 64).then_inc(S("b_root"), 1)

        MR = PMt[:, 10 * T:10 * T + 2048].rearrange("p (k m) -> p k m", k=KT)
        MSQs = [PJt[:, o:o + 2048].rearrange("p (k m) -> p k m", k=KT) for o in (0, 17 * T)]
        RMs = [(PJt[:, 2048:2304], PJt[:, 2304:2560]), (PMt[:, 4096:4352], PMt[:, 4352:4608])]
        MST = PMt[:, 4608:5120].rearrange("p (s n) -> p s n", s=2)
        MNs = [SC[:, 4608:6656].rearrange("p (k m) -> p k m", k=KT), MSQs[1]]
        MN = MNs[0]
        MK = SC[:, 6656:8704].rearrange("p (k m) -> p k m", k=KT)
        MV = SC[:, 8704:10752].rearrange("p (j n) -> p j n", j=2)
        XQ = PJ[:, 0:8, :]
        SKt, SVt = PJt[:, 8 * T:8 * T + 4096], PMt[:, 0:4096]
        SKs = [SKt[:, 2048 * i:2048 * (i + 1)].rearrange("p (k m) -> p k m", k=KT) for i in range(2)]
        SVs = [SVt[:, 2048 * i:2048 * (i + 1)].rearrange("p (j n) -> p j n", j=2) for i in range(2)]
        XP = PMt[:, 4096:5120].rearrange("p (i m) -> p i m", i=4)
        XPT = PMt[:, 5120:6144].rearrange("p (j q) -> p j q", j=2)
        XQS = PMt[:, 6144:7168].rearrange("p (d q) -> p d q", d=2)
        XVS = PMt[:, 7168:7680].rearrange("p (j n) -> p j n", j=2)
        XST = PMt[:, 7680:7700]
        YQZ = [SC[:, 10752 + 256 * i:10752 + 256 * (i + 1)].rearrange("p (k c) -> p k c", k=KT) for i in range(2)]
        YP = [SC[0:32, 11264 + 256 * i:11264 + 256 * (i + 1)] for i in range(2)]
        YPT = [SC[:, 11776 + 64 * i:11776 + 64 * (i + 1)].rearrange("p (j c) -> p j c", j=2) for i in range(2)]
        YST = SC[0:32, 11904:11912]
        XSC = XHD ** -0.5

        def mem_act(act, l):
            act.wait_ge(S("mem_in"), 16 * (l + 1))
            nc.scalar.activation(MSQs[l], MR, ACT.Square).then_inc(S("m_square"), 1)
            act.wait_ge(S("m_sum"), l + 1)
            nc.scalar.activation(RMs[l][0], ps[:, 7, 0:MEM], ACT.Sqrt, bias=eps[:, 0:1], scale=1.0 / D).then_inc(S("m_root"), 1)

        def mem_pe(pe, l):
            pe.wait_ge(S("m_square"), l + 1)
            for k in range(KT):
                mm = nc.tensor.matmul(ps[:, 7, 0:MEM], ones[:, :], MSQs[l][:, k, :], start=(k == 0), stop=(k == KT - 1))
            mm.then_inc(S("m_sum"), 1)

        def mem_dve(dve, l, link):
            dve.wait_ge(S("m_root"), l + 1)
            link(nc.vector.reciprocal(RMs[l][1], RMs[l][0]))
            for k in range(KT):
                nc.vector.scalar_tensor_tensor(MNs[l][:, k, :], MR[:, k, :], G(f"mem{l}", k), RMs[l][1], ALU.mult, ALU.mult)\
                  .then_inc(S("m_normed"), 1)

        def memory_product(pe, g, keys):
            for at, k, reps in g.steps():
                def body(it):
                    for j in range(k):
                        b = g.g0 + at + j
                        o = g.o0 + at + j
                        pe.wait_ge(S(f"slot{b % SLOTS}"), it * 16 + 16 * (b // SLOTS + 1))
                        pe.wait_ge(S("out_taken"), it * SLOTS + (o - 1))
                        bank = ps[:, 2 * (o % 2), 0:MEM]
                        for half in range(1 if keys else 2):
                            for kt in range(KT):
                                w = ring[:, b % SLOTS, kt * P:(kt + 1) * P]
                                if keys:
                                    mm = nc.tensor.matmul(bank, w, MN[:, kt, :], start=(kt == 0), stop=(kt == KT - 1))
                                else:
                                    mm = nc.tensor.matmul(bank[:, half * P:(half + 1) * P], MN[:, kt, half * P:(half + 1) * P],
                                                          w, start=(kt == 0), stop=(kt == KT - 1))
                        mm.then_inc(S("block_done"), 1)
                assert k == SLOTS
                with pe.Fori(0, reps) as it:
                    body(it)

        def memory_take(dve, g, keys):
            for at, k, reps in g.steps():
                with dve.Fori(0, reps) as it:
                    for j in range(k):
                        b = g.g0 + at + j
                        dve.wait_ge(S("block_done"), it * SLOTS + (b + 1))
                        bank = ps[:, 2 * ((g.o0 + at + j) % 2), 0:MEM]
                        if keys:
                            d = MK[:, ds(it * SLOTS + (at + j), 1), :].rearrange("p o m -> p (o m)")
                            nc.vector.tensor_copy(d, bank).then_inc(S("out_taken"), 1)
                        else:
                            d = MV[:, :, ds(it * (SLOTS * P) + (at + j) * P, P)]
                            nc.vector.tensor_copy(d, bank.rearrange("p (j n) -> p j n", j=2)).then_inc(S("out_taken"), 1)

        def cross_pool(pool, l):
            taken([G_EOUT, G_OOUT][l])(pool)
            for i in range(2):
                nc.gpsimd.memset(YQZ[i], 0.0).then_inc(S("zeroed"), 1)
            pool.wait_ge(S("zeroed"), 4 * l + 2)
            pool.wait_ge(S("out_taken"), layers[l]["q"].o1)
            if l == 1:
                pool.wait_ge(S("mem_in"), 64)
            with pool.Fori(0, XH) as h:
                n = h + 4 * l
                pool.wait_ge(S("x_logits"), n + CREDIT)
                nc.gpsimd.tensor_copy(XQS, XQ[:, ds(h * 2, 2), 0:TP]).then_inc(S("x_q"), 1)
                for i in range(2):
                    pool.wait_ge(S("y_logits"), h * 2 + max(8 * l + i - 1, 0) + CREDIT)
                    for hh in range(XH):
                        q = XQ[:, 2 * hh:2 * hh + 2, ds(h * (2 * LS) + (TP + i * LS), LS)]
                        nc.gpsimd.tensor_copy(YQZ[i][:, 2 * hh:2 * hh + 2, LS * hh:LS * hh + LS], q).then_inc(S("y_q"), 1)
                pool.wait_ge(S("x_outmm"), n + CREDIT)
                nc.gpsimd.tensor_copy(XVS, MV[:, :, ds(h * XHD, XHD)]).then_inc(S("x_v"), 1)

        def cross_pe(pe, l):
            def x_logits(h, k):
                n = h + (4 * l + k)
                pe.wait_ge(S("x_q"), n + 1)
                pe.wait_ge(S("x_p"), n * 4 + CREDIT)
                for i in range(4):
                    for d in range(2):
                        mm = nc.tensor.matmul(ps[:, i // 2, (i % 2) * MEM:(i % 2 + 1) * MEM], XQS[:, d, i * P:(i + 1) * P],
                                              MK[:, ds(h * 2 + (2 * k + d), 1), :].rearrange("p o m -> p (o m)"),
                                              start=(d == 0), stop=(d == 1))
                mm.then_inc(S("x_logits"), 1)

            def y_logits(h, i):
                m = h * 2 + (8 * l + i)
                pe.wait_ge(S("y_q"), m * 4 + 4)
                pe.wait_ge(S(f"sk{i}"), h * 16 + 16 * (4 * l + 1))
                pe.wait_ge(S("y_p"), m + CREDIT)
                pe.wait_ge(S("y_out"), h * 2 + 8 * l + CREDIT)
                for k in range(KT):
                    mm = nc.tensor.matmul(ps[0:32, 6, 0:MEM], YQZ[i][:, k, :], SKs[i][:, k, :],
                                          start=(k == 0), stop=(k == KT - 1))
                mm.then_inc(S("y_logits"), 1)

            def turn(h, last):
                n = h + 4 * l
                y_logits(h, 0)
                pe.wait_ge(S("x_pn"), n + 1)
                for j in range(2):
                    for i in range(4):
                        mm = nc.tensor.transpose(ps[:, 2 + j, i * P:(i + 1) * P], XP[:, i, j * P:(j + 1) * P], C("ident"))
                mm.then_inc(S("x_turned"), 1)
                if not last:
                    x_logits(h, 1)
                y_logits(h, 1)
                pe.wait_ge(S("x_v"), n + 1)
                pe.wait_ge(S("x_pt"), n + 1)
                pe.wait_ge(S("x_out"), n * 2 + CREDIT)
                for d in range(2):
                    for j in range(2):
                        mm = nc.tensor.matmul(ps[:, 4 + d, :], XVS[:, j, d * P:(d + 1) * P], XPT[:, j, :],
                                              start=(j == 0), stop=(j == 1))
                mm.then_inc(S("x_outmm"), 1)
                for i in range(2):
                    m = h * 2 + (8 * l + i)
                    pe.wait_ge(S("y_pn"), m + 1)
                    for j in range(2):
                        mm = nc.tensor.matmul(ps[:, 7, j * 32:(j + 1) * 32], YP[i][:, j * P:(j + 1) * P], C("ident")[0:32, 0:32],
                                              start=True, stop=True)
                    mm.then_inc(S("y_turned"), 1)
                    pe.wait_ge(S("y_pt"), m + 1)
                for i in range(2):
                    pe.wait_ge(S(f"sv{i}"), h * 16 + 16 * (4 * l + 1))
                    for d in range(KT):
                        for j in range(2):
                            mm = nc.tensor.matmul(ps[:, 7 - i, 256 + d * LS:256 + (d + 1) * LS],
                                                  SVs[i][:, j, d * P:(d + 1) * P],
                                                  YPT[i][:, j, (d // 2) * LS:(d // 2 + 1) * LS],
                                                  start=(j == 0), stop=(j == 1))
                    mm.then_inc(S("y_outmm"), 1)

            pe.wait_ge(S("out_taken"), layers[l]["q"].o1)
            if l == 1:
                pe.wait_ge(S("mem_in"), 64)
            x_logits(0, 0)
            with pe.Fori(0, XH - 1) as h:
                turn(h, False)
            turn(XH - 1, True)

        def cross_dve(dve, l, link):
            def x_maxima(n):
                dve.wait_ge(S("x_logits"), n + 1 + CREDIT)
                lg = ps[:, 0:2, :].rearrange("p a (c m) -> p (a c) m", c=2)
                link(nc.vector.tensor_reduce(XST[:, 0:4], lg, AX_X, ALU.max))
                nc.vector.tensor_scalar(XST[:, 4:8], XST[:, 0:4], -XSC, None, ALU.mult).then_inc(S("x_bias"), 1)

            def y_maxima(h, i):
                m = h * 2 + (8 * l + i)
                dve.wait_ge(S("y_logits"), m + 1 + CREDIT)
                link(nc.vector.tensor_reduce(YST[:, 4 * i:4 * i + 1], ps[0:32, 6, 0:MEM], AX_X, ALU.max))
                nc.vector.tensor_scalar(YST[:, 4 * i + 1:4 * i + 2], YST[:, 4 * i:4 * i + 1], -XSC, None, ALU.mult)\
                  .then_inc(S("y_bias"), 1)

            def turn(h, last):
                n = h + 4 * l
                dve.wait_ge(S("x_p"), n * 4 + 4 + CREDIT)
                link(nc.vector.reciprocal(XST[:, 12:16], XST[:, 8:12]))
                nc.vector.tensor_tensor(XP, XP, XST[:, 12:16].unsqueeze(2).broadcast_to([P, 4, MEM]), ALU.mult)\
                  .then_inc(S("x_pn"), 1)
                y_maxima(h, 0)
                dve.wait_ge(S("x_turned"), n + 1 + CREDIT)
                nc.vector.tensor_copy(XPT, ps[:, 2:4, :]).then_inc(S("x_pt"), 1)
                if not last:
                    x_maxima(n + 1)
                y_maxima(h, 1)
                for i in range(2):
                    m = h * 2 + (8 * l + i)
                    dve.wait_ge(S("y_p"), m + 1 + CREDIT)
                    link(nc.vector.reciprocal(YST[:, 4 * i + 3:4 * i + 4], YST[:, 4 * i + 2:4 * i + 3]))
                    nc.vector.tensor_scalar(YP[i], YP[i], YST[:, 4 * i + 3:4 * i + 4], None, ALU.mult).then_inc(S("y_pn"), 1)
                for i in range(2):
                    m = h * 2 + (8 * l + i)
                    dve.wait_ge(S("y_turned"), m + 1)
                    nc.vector.tensor_copy(YPT[i], ps[:, 7, 0:64].rearrange("p (j c) -> p j c", j=2)).then_inc(S("y_pt"), 1)
                for i in range(2):
                    m = h * 2 + (8 * l + i)
                    dve.wait_ge(S("y_outmm"), m + 1)
                    o = ps[:, 7 - i, 256:320].rearrange("p (k t) -> p k t", k=KT)
                    nc.vector.tensor_copy(H[:, :, ds(h * (2 * LS) + (TP + i * LS), LS)], o).then_inc(S("y_out"), 1)

            x_maxima(4 * l)
            with dve.Fori(0, XH - 1) as h:
                link.enter(h, 6)
                turn(h, False)
            link.leave(XH - 1)
            turn(XH - 1, True)

        def cross_act(act, l):
            def x_exp(h, k):
                n = h + (4 * l + k)
                act.wait_ge(S("x_bias"), n + 1)
                act.wait_ge(S("x_turned"), n + CREDIT)
                for i in range(4):
                    nc.scalar.activation(XP[:, i, :], ps[:, i // 2, (i % 2) * MEM:(i % 2 + 1) * MEM], ACT.Exp,
                                         bias=XST[:, 4 + i:5 + i], scale=XSC, accum_out=XST[:, 8 + i:9 + i])\
                      .then_inc(S("x_p"), 1)

            def y_exp(h, i):
                m = h * 2 + (8 * l + i)
                act.wait_ge(S("y_bias"), m + 1)
                nc.scalar.activation(YP[i], ps[0:32, 6, 0:MEM], ACT.Exp, bias=YST[:, 4 * i + 1:4 * i + 2], scale=XSC,
                                     accum_out=YST[:, 4 * i + 2:4 * i + 3]).then_inc(S("y_p"), 1)

            def turn(h, last):
                y_exp(h, 0)
                if not last:
                    x_exp(h, 1)
                y_exp(h, 1)
                act.wait_ge(S("x_outmm"), h + (4 * l + 1) + CREDIT)
                for d in range(2):
                    nc.scalar.activation(H[:, ds(h * 2 + d, 1), 0:TP].rearrange("p o t -> p (o t)"), ps[:, 4 + d, :], ACT.Copy)\
                      .then_inc(S("x_out"), 1)

            x_exp(0, 0)
            with act.Fori(0, XH - 1) as h:
                turn(h, False)
            turn(XH - 1, True)

        SGt = PMt[:, 0:2 * T].rearrange("p (j t) -> p j t", j=2)

        def hidden(parts, it, c):
            return parts[:, ds(it * 2 + c // 2, 1), :].rearrange("p o t -> p (o t)")

        def gate_act(act, l):
            g, d = LD[l]["gu"], LD[l]["d"]

            def silu(it, c):
                if c % 2 == 0:
                    act.wait_ge(S("h_low"), it * 2 + (d.h0 + c // 2 - 1))
                    nc.scalar.activation(two(SGt[:, c // 2 % 2, :]), pair(2 * ((g.o0 + c) % 2)), ACT.Silu).then_inc(S("silu"), 1)

            def high_part(it, c):
                if c % 2:
                    act.wait_ge(S("out_taken"), it * 4 + (g.o0 + c + 1))
                    nc.scalar.activation(hidden(HGH, it, c), SGt[:, c // 2 % 2, :], ACT.Copy).then_inc(S("h_high"), 1)
            split_high(act, g, normed_tiles(act, 2 + 3 * l), silu, high_part)

        def gate_dve(dve, l):
            g, d = LD[l]["gu"], LD[l]["d"]

            def times_up(it, c):
                if c % 2:
                    dve.wait_ge(S("silu"), it * 2 + (FT * l + c // 2 + 1) + CREDIT)
                    dve.wait_ge(S("block_done"), it * 4 + (g.g0 + c + 1))
                    gate = two(SGt[:, c // 2 % 2, :])
                    nc.vector.tensor_tensor(gate, pair(2 * ((g.o0 + c) % 2)), gate, ALU.mult).then_inc(S("out_taken"), 2)

            def low_part(it, c):
                if c % 2:
                    dve.wait_ge(S("h_high"), it * 2 + (d.h0 + c // 2 + 1))
                    nc.vector.tensor_tensor(hidden(HGL, it, c), SGt[:, c // 2 % 2, :], hidden(HGH, it, c), ALU.subtract)\
                      .then_inc(S("h_low"), 1)
            split_take(dve, g, step=times_up, after=low_part)

        def down_pe(pe, l):
            g = LD[l]["d"]
            pe.wait_ge(S("h_low"), g.h0 + FT)

            def body(it, c):
                o, sub = g.o0 + c // 2, c % 2
                pe.wait_ge(S("w_low"), it * 4 + (g.s0 + c + 1))
                if sub == 0:
                    pe.wait_ge(S("out_taken"), it * 2 + (o - 1))
                for k in range(g.kt):
                    t, w = sub * g.kt + k, slice(k * P, (k + 1) * P)
                    for n, (lhsT, rhs) in enumerate(((DWL, HGH), (DWH, HGL), (DWH, HGH))):
                        for h in range(2):
                            mm = nc.tensor.matmul(ps[:, 2 * (o % 2) + h, 0:HT], lhsT[:, c % 2, w], rhs[:, t, h * HT:(h + 1) * HT],
                                                  start=(t == 0 and n == 0), stop=(t == FT - 1 and n == 2))
                mm.then_inc(S("block_done"), 1)
            rounds(pe, g, body)

        def down_act(act, l):
            g = LD[l]["d"]
            act.wait_ge(S("block_done"), g.g0)
            for c in range(2):
                high(act, g, 0, c)

            def body(it, c):
                if not (isinstance(it, int) and c + 2 >= g.n):
                    high(act, g, it, c + 2)
            rounds(act, g, body)

        def down_dve(dve, l):
            g = LD[l]["d"]
            for c in range(2):
                low(dve, g, 0, c)

            def body(it, c):
                if c % 2:
                    dve.wait_ge(S("block_done"), it * 4 + (g.g0 + c + 1))
                    d = X[:, ds(it * 2 + c // 2, 1), :].rearrange("p o (a b) -> p (o a) b", a=2)
                    nc.vector.tensor_tensor(d, pair(2 * ((g.o0 + c // 2) % 2)), d, ALU.add).then_inc(S("out_taken"), 1)
                if not (isinstance(it, int) and c + 2 >= g.n):
                    low(dve, g, it, c + 2)
            rounds(dve, g, body)

        def gate_free(pe, g, l):
            def free(it, c):
                if c % 2 == 0:
                    pe.wait_ge(S("silu"), it * 2 + (FT * l + c // 2) + CREDIT)
                else:
                    pe.wait_ge(S("out_taken"), it * 4 + (g.o0 + c - 1))
            return free

        Q1, K1, V1, QI, KW = PJ[:, 8:12, :], PJ[:, 12, :], PJ[:, 13, :], PJ[:, 14:16, :], PJ[:, 16, :]
        GP, XI = PJ[:, 0:4, :], PJ[:, 4:8, :]
        XC, GX, GA = PM[:, 0:4, :], PM[:, 4:8, :], PM[:, 8:12, :]
        CA = SC[:, 0:4 * T].rearrange("p (k t) -> p k t", k=4)
        WXA = SC[:, 2304:3328].rearrange("p (x k n) -> p x k n", x=2, k=4)
        LH0 = SC[:, 3328:3360].rearrange("p (k b) -> p k b", k=4)
        LCV = SC[:, 3360:3456].rearrange("p (k b j) -> p k b j", k=4, b=NS)
        LS8, LU, LR, LP = (SC[:, 3456 + 4 * i:3460 + 4 * i] for i in range(4))
        CO = SC[:, 3480:3480 + 4 * 27].rearrange("p (k n) -> p k n", k=4)
        HO = SC[:, 3600:3636].rearrange("p (k n) -> p k n", k=4)

        def c_dve(dve, link):
            taken(G_OIN)(dve)
            dve.wait_ge(S("lru_in"), 16 * 3)
            nc.vector.tensor_copy(CO[:, :, 0:3], XI[:, :, TP - 3:TP]).then_inc(S("l_conv_out"), 1)
            for b in range(NS):
                nc.vector.tensor_copy(CO[:, :, 3 + 3 * b:6 + 3 * b], XI[:, :, TP + LS * b + LS - 3:TP + LS * b + LS])\
                  .then_inc(S("l_conv_out"), 1)
            for k in range(4):
                w = lambda j: G("conv_w", 4 * j + k)
                link(nc.vector.tensor_scalar(XC[:, k, :], XI[:, k, :], w(3), G("conv_b", k), ALU.mult, ALU.add))
                xs = XC[:, k, TP:T].rearrange("p (b t) -> p b t", b=NS)
                xi = XI[:, k, TP:T].rearrange("p (b t) -> p b t", b=NS)
                for j in (2, 1, 0):
                    d = 3 - j
                    for o, i in ((XC[:, k, d:TP], XI[:, k, 0:TP - d]), (xs[:, :, d:LS], xi[:, :, 0:LS - d]),
                                 (xs[:, :, 0:d], LCV[:, k, :, j:3])):
                        nc.vector.scalar_tensor_tensor(o, i, w(j), o, ALU.mult, ALU.add).then_inc(S("l_tap"), 1)
                    dve.wait_ge(S("l_tap"), 9 * k + 3 * d)
            o, _ = PCOL["lam"]
            lam = par[:, o:o + 4]
            link(nc.vector.tensor_scalar(LU, lam, -1.0, None, ALU.mult))
            nc.vector.tensor_tensor(LU, LU, lam, ALU.max).then_inc(S("l_logs"), 1)
            dve.wait_ge(S("l_exp"), 1)
            link(nc.vector.tensor_scalar(LR, LU, 2.0, None, ALU.add))
            link(nc.vector.reciprocal(LR, LR))
            link(nc.vector.tensor_tensor(LU, LU, LR, ALU.mult))
            link(nc.vector.tensor_tensor(LR, LU, LU, ALU.mult))
            link(nc.vector.tensor_scalar(LP, LR, 1.0 / 17, 1.0 / 15, ALU.mult, ALU.add))
            for c in (13, 11, 9, 7, 5, 3, 1):
                link(nc.vector.tensor_tensor(LP, LP, LR, ALU.mult))
                link(nc.vector.tensor_scalar(LP, LP, 1.0 / c, None, ALU.add))
            link(nc.vector.scalar_tensor_tensor(LP, LP, 2.0, LU, ALU.mult, ALU.mult))
            link(nc.vector.tensor_scalar(LR, lam, 0.0, None, ALU.min))
            link(nc.vector.tensor_tensor(LP, LR, LP, ALU.subtract))
            nc.vector.tensor_scalar(LS8, LP, 8.0, None, ALU.mult).then_inc(S("l_logs"), 1)
            dve.wait_ge(S("l_decay"), 8)
            TM1 = H[:, 0:4, :]
            link(nc.vector.tensor_scalar(TM1, GA, -1.0, 1.0, ALU.mult, ALU.add))
            link(nc.vector.reciprocal(TM1, TM1))
            nc.vector.scalar_tensor_tensor(GA, GA, -2.0, TM1, ALU.mult, ALU.mult).then_inc(S("l_logs"), 1)
            link(nc.vector.tensor_tensor(GX, GX, XC, ALU.mult))
            dve.wait_ge(S("l_decay"), 9)
            link(nc.vector.memset(GA[:, :, 0:1], 1.0))
            link(nc.vector.tensor_tensor(GX, GX, GA, ALU.mult))
            first = seqs(GX[:, :, TP:T])[:, :, :, 0]
            afirst = seqs(CA[:, :, TP:T])[:, :, :, 0]
            link(nc.vector.tensor_tensor(LH0, LH0, afirst, ALU.mult))
            link(nc.vector.tensor_tensor(first, first, LH0, ALU.add))
            link(nc.vector.memset(afirst, 0.0))
            for k in range(4):
                link(nc.vector.tensor_tensor_scan(XC[:, k, :], CA[:, k, :], GX[:, k, :], 0.0, ALU.mult, ALU.add))
            nc.vector.tensor_copy(HO[:, :, 0:1], XC[:, :, TP - 1:TP]).then_inc(S("l_h_out"), 1)
            nc.vector.tensor_copy(HO[:, :, 1:9], seqs(XC[:, :, TP:T])[:, :, :, LS - 1]).then_inc(S("l_h_out"), 1)
            dve.wait_ge(S("l_decay"), 10)
            nc.vector.tensor_tensor(H[:, 0:4, :], XC, GP, ALU.mult).then_inc(S("l_out"), 1)

        def c_act(act):
            taken(G_OIN)(act)
            act.wait_ge(S("l_logs"), 1)
            nc.scalar.activation(LU, LU, ACT.Exp, scale=-1.0).then_inc(S("l_exp"), 1)
            for x, (dst, bias) in enumerate(((GX, "bx"), (GA, "ba"))):
                act.wait_ge(S("l_gates"), x + 1)
                for k in range(4):
                    nc.scalar.activation(two(dst[:, k, :]), pair(2 * k), ACT.Sigmoid, bias=G(bias, k)).then_inc(S("l_sig"), 1)
            act.wait_ge(S("l_logs"), 2)
            act.wait_ge(S("l_sig"), 8)
            for k in range(4):
                nc.scalar.activation(CA[:, k, :], GA[:, k, :], ACT.Exp, scale=LS8[:, k:k + 1]).then_inc(S("l_decay"), 1)
            act.wait_ge(S("l_decay"), 4)
            for k in range(4):
                nc.scalar.activation(GA[:, k, :], GA[:, k, :], ACT.Tanh, scale=LS8[:, k:k + 1]).then_inc(S("l_decay"), 1)
            act.wait_ge(S("d_rot"), 1)
            nc.scalar.activation(flat(RT), all_banks, ACT.Copy).then_inc(S("q_roped"), 1)
            act.wait_ge(S("l_logs"), 3)
            nc.scalar.activation(GA, GA, ACT.Sqrt).then_inc(S("l_decay"), 1)
            nc.scalar.activation(GP, GP, ACT.Gelu_apprx_tanh).then_inc(S("l_decay"), 1)

        def c_pe(pe):
            pe.wait_ge(S("l_tap"), 36)
            for x in range(2):
                if x:
                    pe.wait_ge(S("l_sig"), 4)
                for k in range(4):
                    for h in range(2):
                        mm = nc.tensor.matmul(ps[:, 2 * k + h, 0:HT], WXA[:, x, k, :], XC[:, k, h * HT:(h + 1) * HT],
                                              start=True, stop=True)
                mm.then_inc(S("l_gates"), 1)

        ROT = H[:, 4:8, :]
        RT = PJ[:, 17:21, :]
        KR = PJ[:, 21, :]
        at[0] = 0
        MB = carve(2048).rearrange("p (i n) -> p i n", i=4)
        RL = [carve(512) for _ in range(2)]
        VT = carve(512).rearrange("p (j d) -> p j d", j=4)
        VN = carve(1024)[0:LS].rearrange("p (b d) -> p b d", b=NS)
        WI = carve(32).rearrange("p (i h) -> p i h", i=4)
        T8 = carve(25)
        SS = carve(LK)[0:TS]
        WSA = carve(64)[0:TS]
        WSB = carve(512)[0:TS].rearrange("p (b t) -> p b t", b=NS)
        WSs = carve(128)[0:TS]
        QIS = carve(512)[0:32].rearrange("p (b h t) -> p b h t", b=NS, h=8)
        QIb = carve(64)[0:32]
        QB = carve(64)
        MRb = carve(64)[0:TS]
        VNb = carve(128)[0:LS]
        KNb = carve(LS)[0:32]
        ZR = carve(LK)
        ZS = ZR[0:TS]
        PTS = carve(17 * 64).rearrange("p (c n) -> p c n", c=17)
        ZP = ZR[:, 0:1024].rearrange("p (v n) -> p v n", v=2)
        PTP = ZR[:, 1024:2048].rearrange("p (v n) -> p v n", v=2)
        QG = carve(512)
        DST = carve(16)
        assert at[0] <= 13600, at
        KS = [PJt[:, 2048 * i:2048 * (i + 1)] for i in range(2)]
        VS = [PMt[:, 2048 * i:2048 * (i + 1)].rearrange("p (g d) -> p g d", g=NPG) for i in range(2)]
        flat = lambda v: v.rearrange("p k (a b) -> p (k a) b", a=2)

        def d_rope_pe(pe):
            pe.wait_ge(S("l_sig"), 8)
            for k in range(4):
                for h in range(2):
                    mm = nc.tensor.matmul(ps[:, 2 * k + h, 0:HT], C("rot64"), Q1[:, k, h * HT:(h + 1) * HT], start=True, stop=True)
            mm.then_inc(S("d_rot"), 1)
            pe.wait_ge(S("q_roped"), 1)
            for o, lhsT, src in ((0, C("rot64"), K1), (2, C("rot32"), QI[:, 0, :]), (4, C("rot32"), QI[:, 1, :]),
                                 (6, C("rep32")[0:32, :], KW[0:32, :])):
                for h in range(2):
                    mm = nc.tensor.matmul(ps[:, o + h, 0:HT], lhsT, src[:, h * HT:(h + 1) * HT], start=True, stop=True)
            mm.then_inc(S("d_rot"), 1)
            pe.wait_ge(S("d_roped"), 2)
            for h in range(2):
                mm = nc.tensor.matmul(ps[:, h, 0:HT], C("rotrep")[0:32, :], KW[0:32, h * HT:(h + 1) * HT], start=True, stop=True)
            mm.then_inc(S("d_rot"), 1)
            for j in range(4):
                nc.tensor.transpose(ps[:, 2, j * P:(j + 1) * P], V1[:, j * P:(j + 1) * P], C("ident"))
                nc.tensor.transpose(ps[:, 3, j * P:(j + 1) * P], KW[:, j * P:(j + 1) * P], C("ident"))
            for b in range(NS):
                nc.tensor.transpose(ps[0:LS, 4 + b // 4, (b % 4) * P:(b % 4 + 1) * P], V1[:, TP + b * LS:TP + (b + 1) * LS], C("ident"))
            nc.tensor.matmul(ps[0:TS, 6, 0:TS], C("spread")[32:40, :], KW[32:40, TP:T], start=True, stop=True)
            for h in range(8):
                mm = nc.tensor.matmul(ps[0:32, 7, h * TS:(h + 1) * TS], C("ident")[:, 32 * (h % 4):32 * (h % 4) + 32],
                                      QI[:, h // 4, TP:T], start=True, stop=True)
            mm.then_inc(S("d_rot"), 1)

        def d_rope_pool(pool):
            pool.wait_ge(S("rotary_in"), 16)
            pool.wait_ge(S("q_roped"), 1)
            nc.gpsimd.tensor_tensor(Q1, Q1, bc(ROT[:, 0, :], 4), ALU.mult).then_inc(S("q_roped"), 1)
            nc.gpsimd.tensor_tensor(RT, RT, bc(ROT[:, 1, :], 4), ALU.mult).then_inc(S("q_roped"), 1)
            pool.wait_ge(S("q_roped"), 3)
            nc.gpsimd.tensor_tensor(Q1, Q1, RT, ALU.add).then_inc(S("d_roped"), 1)

        def d_rope_dve(dve, link):
            dve.wait_ge(S("rotary_in"), 16)
            dve.wait_ge(S("d_roped"), 1)
            dve.wait_ge(S("d_rot"), 2)
            link(nc.vector.tensor_tensor(two(RT[:, 0, :]), pair(0), two(ROT[:, 1, :]), ALU.mult))
            link(nc.vector.tensor_tensor(K1, K1, ROT[:, 0, :], ALU.mult))
            link(nc.vector.tensor_tensor(K1, K1, RT[:, 0, :], ALU.add))
            for k in range(2):
                link(nc.vector.tensor_tensor(two(RT[:, 1 + k, :]), pair(2 + 2 * k), two(ROT[:, 3, :]), ALU.mult))
            link(nc.vector.tensor_tensor(QI, QI, bc(ROT[:, 2, :], 2), ALU.mult))
            link(nc.vector.tensor_tensor(QI, QI, RT[:, 1:3, :], ALU.add))
            nc.vector.tensor_tensor(two(KR), pair(6), two(ROT[:, 2, :]), ALU.mult).then_inc(S("d_roped"), 1)
            dve.wait_ge(S("d_roped"), 2)
            dve.wait_ge(S("d_rot"), 3)
            link(nc.vector.tensor_tensor(two(RT[:, 0, :]), pair(0), two(ROT[:, 3, :]), ALU.mult))
            link(nc.vector.tensor_tensor(KR, KR, RT[:, 0, :], ALU.add))
            dve.wait_ge(S("d_rot"), 4)
            iw = (8 ** -0.5) * (32 ** -0.5)
            dve.wait_ge(S("c_stored"), 32)
            t = S("d_ready")
            nc.vector.tensor_copy(VT, ps[:, 2, :].rearrange("p (j d) -> p j d", j=4)).then_inc(t, 1)
            nc.vector.tensor_scalar(WI, ps[:, 3, :].rearrange("p (i n) -> p i n", i=4)[:, :, 32:40], iw, None, ALU.mult).then_inc(t, 1)
            nc.vector.tensor_copy(VN, ps[0:LS, 4:6, :].rearrange("p a (b d) -> p (a b) d", b=4)).then_inc(t, 1)
            nc.vector.scalar_tensor_tensor(WSA, ps[0:TS, 6, 0:TS], iw, C("same_t")[0:TS], ALU.mult, ALU.mult).then_inc(t, 1)
            nc.vector.tensor_copy(QIS, ps[0:32, 7, :].rearrange("p (h b t) -> p b h t", h=8, b=NS)).then_inc(t, 1)
            dve.wait_ge(t, 5)
            nc.vector.tensor_tensor(WSB, bc(WSA, NS), seq_cols[0:TS], ALU.mult).then_inc(t, 1)
            dve.wait_ge(t, 6)

        blocks = [(i, h) for i in range(1, 4) for h in range(8)]

        def d_score_pe(pe):
            pe.wait_ge(S("d_ready"), 6)
            for n, (i, h) in enumerate(blocks):
                if n >= 2:
                    pe.wait_ge(S("i_relu"), n - 1)
                r = slice(32 * (h % 4), 32 * (h % 4) + 32)
                nc.tensor.matmul(ps[:, n % 2, 0:(i + 1) * P], QI[r, h // 4, i * P:(i + 1) * P], KR[r, 0:(i + 1) * P],
                                 start=True, stop=True).then_inc(S("i_dot"), 1)

        def d_score_act(act):
            for n, (i, h) in enumerate(blocks):
                act.wait_ge(S("i_dot"), n + 1)
                if n >= 2:
                    act.wait_ge(S("i_sum"), n - 1)
                nc.scalar.activation(RL[n % 2][:, 0:(i + 1) * P], ps[:, n % 2, 0:(i + 1) * P], ACT.Relu).then_inc(S("i_relu"), 1)

        def d_score_dve(dve, link):
            link(nc.vector.tensor_copy(MB[:, 0, 0:P], C("causal")))
            for n, (i, h) in enumerate(blocks):
                w = (i + 1) * P
                dve.wait_ge(S("i_relu"), n + 1)
                m = MB[:, i, 0:w]
                if h:
                    dve.wait_ge(S("i_sum"), n)
                    ins = nc.vector.scalar_tensor_tensor(m, RL[n % 2][:, 0:w], WI[:, i, h:h + 1], m, ALU.mult, ALU.add)
                else:
                    ins = nc.vector.tensor_scalar(m, RL[n % 2][:, 0:w], WI[:, i, h:h + 1], None, ALU.mult)
                ins.then_inc(S("i_sum"), 1)
                if h == 7:
                    dve.wait_ge(S("i_sum"), n + 1)
                    link(nc.vector.tensor_tensor(MB[:, i, i * P:w], MB[:, i, i * P:w], C("causal"), ALU.add))
            with dve.Fori(0, TOPK_P // 8) as r:
                for i in range(1, 4):
                    nc.vector.max(T8[:, 8 * i - 8:8 * i], MB[:, i, 0:(i + 1) * P]).then_inc(S("top"), 1)
                dve.wait_ge(S("top"), r * 3 + 3)
                nc.vector.memset(T8[:, 24:25], 0.0)
                for i in range(1, 4):
                    nc.vector.match_replace(MB[:, i, 0:(i + 1) * P], T8[:, 8 * i - 8:8 * i], MB[:, i, 0:(i + 1) * P], TAKEN)\
                      .then_inc(S("take"), 1)
                dve.wait_ge(S("take"), r * 3 + 3)
            for i in range(1, 4):
                m = MB[:, i, 0:(i + 1) * P]
                link(nc.vector.tensor_scalar(m, m, TAKEN, BIG, ALU.is_equal, ALU.mult))
                nc.vector.tensor_scalar(m, m, -BIG, None, ALU.add).then_inc(S("mask"), 1)
            dve.wait_ge(S("mask"), 3)

        def d_prompt_pool(pool):
            pool.wait_ge(S("d_ready"), 6)
            with pool.Fori(0, 4) as g:
                pool.wait_ge(S("p_logits"), g * 4 + CREDIT)
                nc.gpsimd.tensor_copy(QG, Q1[:, ds(g, 1), 0:TP].rearrange("p o t -> p (o t)")).then_inc(S("p_q"), 1)

        def d_prompt_pe(pe):
            def logits(g, i):
                w = (i + 1) * P
                if i == 0:
                    pe.wait_ge(S("p_q"), g + 1)
                pe.wait_ge(S("p_masked"), g * 4 + i + CREDIT)
                for v in range(2):
                    r = slice(64 * v, 64 * v + 64)
                    mm = nc.tensor.matmul(ps[:, v, 0:w], QG[r, i * P:w], K1[r, 0:w], start=True, stop=True)
                mm.then_inc(S("p_logits"), 1)

            def memory_block(g, i, keys):
                m = LD[1]["k"]
                b = m.g0 + i
                pe.wait_ge(S(f"slot{b % SLOTS}"), g * 16 + 16 * (b // SLOTS + 1))
                pe.wait_ge(S("out_taken"), g * 4 + (m.o0 + i - 1))
                bank = ps[:, 5 + i % 2, 0:MEM]
                for half in range(1 if keys else 2):
                    for kt in range(KT):
                        w = ring[:, b % SLOTS, kt * P:(kt + 1) * P]
                        if keys:
                            mm = nc.tensor.matmul(bank, w, MNs[1][:, kt, :], start=(kt == 0), stop=(kt == KT - 1))
                        else:
                            mm = nc.tensor.matmul(bank[:, half * P:(half + 1) * P], MNs[1][:, kt, half * P:(half + 1) * P],
                                                  w, start=(kt == 0), stop=(kt == KT - 1))
                mm.then_inc(S("block_done"), 1)

            def heads(g, keys, last=False):
                for i in range(4):
                    if i < 3:
                        logits(g, i + 1)
                    elif not last:
                        logits(g + 1, 0)
                    memory_block(g, i, keys)
                    pe.wait_ge(S("p_normed"), g * 4 + (i + 1))
                    pe.wait_ge(S("p_pt"), g * 4 + i + CREDIT)
                    for v in range(2):
                        for j in range(i + 1):
                            mm = nc.tensor.transpose(ps[:, 2 + v, j * P:(j + 1) * P], ZP[:, v, j * P:(j + 1) * P], C("ident"))
                    mm.then_inc(S("p_turned"), 1)
                    pe.wait_ge(S("p_pt"), g * 4 + (i + 1) + CREDIT)
                    pe.wait_ge(S("p_out"), g * 4 + i + CREDIT)
                    for v in range(2):
                        for j in range(i + 1):
                            mm = nc.tensor.matmul(ps[64 * v:64 * v + 64, 4, 0:P], VT[:, j, 64 * v:64 * v + 64],
                                                  PTP[:, v, j * P:(j + 1) * P], start=(j == 0), stop=(j == i))
                    mm.then_inc(S("p_outmm"), 1)

            pe.wait_ge(S("mask"), 3)
            pe.wait_ge(S("d_ready"), 8)
            logits(0, 0)
            pe.wait_ge(S("m_normed"), 2 * KT)
            with pe.Fori(0, 2) as g:
                heads(g, True)
            heads(2, False)
            heads(3, False, last=True)
            pe.wait_ge(S("out_taken"), LD[1]["v"].o1)

        def d_prompt_dve(dve, link):
            def round(r):
                nc.vector.max(T8[0:TS, 0:8], SS).then_inc(S("top"), 1)
                dve.wait_ge(S("top"), r + (3 * (TOPK_P // 8) + 1))
                nc.vector.memset(T8[:, 24:25], 0.0)
                nc.vector.match_replace(SS, T8[0:TS, 0:8], SS, TAKEN).then_inc(S("take"), 1)
                dve.wait_ge(S("take"), r + (3 * (TOPK_P // 8) + 1))

            assert TOPK_S // 8 == 32
            with dve.Fori(0, 4) as g:
                link.enter(g, 4 * 2)
                for i in range(4):
                    w = (i + 1) * P
                    dve.wait_ge(S("p_logits"), g * 4 + (i + 1) + CREDIT)
                    dve.wait_ge(S("p_turned"), g * 4 + i + CREDIT)
                    nc.vector.scalar_tensor_tensor(ZP[:, :, 0:w], ps[:, 0:2, 0:w], 0.125, bc(MB[:, i, 0:w], 2), ALU.mult, ALU.add)\
                      .then_inc(S("p_masked"), 1)
                    dve.wait_ge(S("p_masked"), g * 4 + (i + 1) + CREDIT)
                    link(nc.vector.tensor_reduce(DST[:, 0:2], ZP[:, :, 0:w], AX_X, ALU.max))
                    nc.vector.tensor_scalar(DST[:, 2:4], DST[:, 0:2], -1.0, None, ALU.mult).then_inc(S("p_bias"), 1)
                    round(g * 8 + 2 * i)
                    dve.wait_ge(S("p_exp"), g * 8 + (2 * i + 2))
                    link(nc.vector.reciprocal(DST[:, 6:8], DST[:, 4:6]))
                    nc.vector.tensor_tensor(ZP[:, :, 0:w], ZP[:, :, 0:w], DST[:, 6:8].unsqueeze(2).broadcast_to([P, 2, w]), ALU.mult)\
                      .then_inc(S("p_normed"), 1)
                    round(g * 8 + (2 * i + 1))
                    dve.wait_ge(S("p_outmm"), g * 4 + (i + 1) + CREDIT)
                    dst = H[:, ds(g + 4, 1), i * P:w].rearrange("p o t -> p (o t)")
                    nc.vector.tensor_copy(dst, ps[:, 4, 0:P]).then_inc(S("p_out"), 1)
            link.leave(4)
            link(nc.vector.tensor_scalar(SS, SS, TAKEN, BIG, ALU.is_equal, ALU.mult))
            nc.vector.tensor_scalar(SS, SS, -BIG, None, ALU.add).then_inc(S("mask"), 1)

        def d_prompt_act(act):
            m = LD[1]["k"]

            def heads(g, keys):
                for i in range(4):
                    w = (i + 1) * P
                    act.wait_ge(S("p_bias"), g * 4 + (i + 1))
                    for v in range(2):
                        nc.scalar.activation(ZP[:, v, 0:w], ZP[:, v, 0:w], ACT.Exp, bias=DST[:, 2 + v:3 + v],
                                             accum_out=DST[:, 4 + v:5 + v]).then_inc(S("p_exp"), 1)
                    act.wait_ge(S("block_done"), g * 4 + (m.g0 + i + 1))
                    nc.scalar.activation(MST[:, i % 2, :], ps[:, 5 + i % 2, 0:MEM], ACT.Copy).then_inc(S("out_taken"), 1)
                    act.wait_ge(S("out_taken"), g * 4 + (m.o0 + i + 1))
                    if keys:
                        act.dma_start(out["mk"][1][:, ds(g * 4 + i, 1), :].rearrange("p o m -> p (o m)"), MST[:, i % 2, :])\
                          .then_inc(S("m1_stored"), 16)
                    else:
                        n = (4 * (g - 2) + i) * P
                        act.dma_start(out["mv"][1][:, :, n:n + P], MST[:, i % 2, :].rearrange("p (j n) -> p j n", j=2))\
                          .then_inc(S("m1_stored"), 16)
                    act.wait_ge(S("p_turned"), g * 4 + (i + 1) + CREDIT)
                    act.wait_ge(S("p_outmm"), g * 4 + i + CREDIT)
                    nc.scalar.activation(PTP[:, :, 0:w], ps[:, 2:4, 0:w], ACT.Copy).then_inc(S("p_pt"), 1)
                    act.wait_ge(S("m1_stored"), g * 64 + (16 * i + 16))

            with act.Fori(0, 2) as g:
                heads(g, True)
            for g in (2, 3):
                heads(g, False)

        def pages_in(sp):
            sp.wait_ge(S("l_out"), 1)
            sp.wait_ge(S("b_in"), 80)

            def page(b, i, g):
                return sp.value_load(PT[0:1, ds(b * NPG + (i * NPG + g), 1)], min_val=0, max_val=a["pool_ki"].shape[0] - 1)

            def ki(b, i, again):
                if again:
                    sp.wait_ge(S("t_chunk"), b * 5 + (5 * i - 5))
                for g in range(NPG):
                    sp.dma_start(KS[i][0:32, g * PAGE:(g + 1) * PAGE],
                                 a["pool_ki"][ds(page(b, i, g), 1)].rearrange("o d n -> (o d) n")).then_inc(S(f"pages{i}"), 16)

            def kv(b, i, again):
                if again:
                    sp.wait_ge(S("u_logits"), b + (i - 1) + CREDIT)
                numbers = [page(b, i, g) for g in range(NPG)]
                for g, pg in enumerate(numbers):
                    sp.dma_start(KS[i][:, g * PAGE:(g + 1) * PAGE], a["pool_k"][ds(pg, 1)].rearrange("o d n -> (o d) n"))\
                      .then_inc(S(f"pages{i}"), 16)
                if again:
                    sp.wait_ge(S("u_outmm"), b + (i - 1) + CREDIT)
                for g, pg in enumerate(numbers):
                    sp.dma_start(VS[i][:, g, :], a["pool_v"][ds(pg, 1)].rearrange("o n d -> (o n) d")).then_inc(S(f"pv{i}"), 16)

            for i in range(2):
                ki(0, i, False)
            with sp.Fori(1, NS // 2) as b2:
                b = b2 * 2
                for i in range(2):
                    ki(b, i, True)
            weights_round(sp, LD[1]["k"], 0)
            sp.wait_ge(S("t_chunk"), 5 * NS)
            kv(0, 0, False)
            weights_round(sp, LD[1]["k"], 1)
            kv(0, 1, False)
            weights_in(sp, LD[1]["v"])
            with sp.Fori(1, NS // 2) as b2:
                b = b2 * 2
                for i in range(2):
                    kv(b, i, True)

        def d_index_pool(pool):
            nc.gpsimd.memset(WSs, 0.0).then_inc(S("zeroed"), 1)
            pool.wait_ge(S("zeroed"), 3)
            with pool.Fori(0, NS) as b:
                pool.wait_ge(S("t_sum"), b * 5 + CREDIT)
                nc.gpsimd.tensor_copy(QIb.rearrange("p (h t) -> p h t", h=8), QIS[:, ds(b, 1)].rearrange("p o h t -> p (o h) t"))\
                  .then_inc(S("t_copy"), 1)
                nc.gpsimd.tensor_copy(KNb, KR[0:32, ds(b * LS + TP, LS)]).then_inc(S("t_copy"), 1)
                nc.gpsimd.tensor_copy(WSs[:, 0:TS], WSB[:, ds(b, 1), :].rearrange("p o t -> p (o t)")).then_inc(S("t_copy"), 1)

        def d_index_pe(pe):
            pe.wait_ge(S("i_relu"), len(blocks))

            def add(b, i, c, first):
                k = 5 * i + c
                pe.wait_ge(S("t_relu"), b * 5 + (k + 1))
                w = 512 if c < 4 else LS
                nc.tensor.matmul(ps[:, 2 + c, 0:w], WSs, RL[k % 2][0:TS, 0:w], start=first, stop=True,
                                 skip_group_check=True).then_inc(S("t_sum"), 1)

            def sequence(b, i, first):
                pe.wait_ge(S("t_copy"), b * 3 + (3 * i + 3))
                pe.wait_ge(S(f"pages{i}"), b * (8 * NPG) + 16 * NPG)
                for c in range(5):
                    k = 5 * i + c
                    if not first or c >= 2:
                        pe.wait_ge(S("t_relu"), b * 5 + (k - 1))
                    w = 512 if c < 4 else LS
                    rhs = KS[i][0:32, c * 512:(c + 1) * 512] if c < 4 else KNb
                    mm = nc.tensor.matmul(ps[0:TS, k % 2, 0:w], QIb, rhs, start=True, stop=True)
                    mm.then_inc(S("t_chunk"), 1)
                    if c:
                        add(b, i, c - 1, first)
                add(b, i, 4, first)

            sequence(0, 0, True)
            sequence(0, 1, False)
            with pe.Fori(1, NS // 2) as b2:
                b = b2 * 2
                for i in range(2):
                    sequence(b, i, False)

        def d_index_act(act):
            def chunk(b, i, c, first):
                k = 5 * i + c
                w = 512 if c < 4 else LS
                act.wait_ge(S("t_chunk"), b * 5 + (k + 1))
                if not first or c >= 2:
                    act.wait_ge(S("t_sum"), b * 5 + (k - 1) + CREDIT)
                nc.scalar.activation(RL[k % 2][0:TS, 0:w], ps[0:TS, k % 2, 0:w], ACT.Relu).then_inc(S("t_relu"), 1)

            act.wait_ge(S("i_sum"), len(blocks))
            for i in range(2):
                for c in range(5):
                    chunk(0, i, c, i == 0)
            with act.Fori(1, NS // 2) as b2:
                b = b2 * 2
                for i in range(2):
                    for c in range(5):
                        chunk(b, i, c, False)

        def d_index_dve(dve, link):
            dve.wait_ge(S("t_sum"), 5 * NS + CREDIT)
            nc.vector.tensor_copy(SS[:, 0:PAST].rearrange("p (c n) -> p c n", c=4), ps[0:TS, 2:6, :]).then_inc(S("d_ready"), 1)
            nc.vector.tensor_tensor(SS[:, PAST:LK], ps[0:TS, 6, 0:LS], C("causal_n")[0:TS], ALU.add).then_inc(S("d_ready"), 1)
            dve.wait_ge(S("d_ready"), 8)

        def d_sample_pool(pool):
            nc.gpsimd.memset(QB, 0.0).then_inc(S("zeroed"), 1)
            pool.wait_ge(S("zeroed"), 4)
            with pool.Fori(0, NS) as b:
                pool.wait_ge(S("u_logits"), b + CREDIT)
                for v in range(2):
                    r = slice(64 * v, 64 * v + 64)
                    nc.gpsimd.tensor_copy(QB[r, 32 * v:32 * v + 32].rearrange("p (g t) -> p g t", g=4),
                                          Q1[r, :, ds(b * LS + TP, LS)]).then_inc(S("u_copy"), 1)
                nc.gpsimd.tensor_copy(MRb, C("mask_rows")[0:TS, ds(b * 64, 64)]).then_inc(S("u_copy"), 1)
                pool.wait_ge(S("u_outmm"), b + CREDIT)
                nc.gpsimd.tensor_copy(VNb, VN[:, ds(b, 1), :].rearrange("p o d -> p (o d)")).then_inc(S("u_copy"), 1)

        def d_sample_pe(pe):
            def logits(b, i):
                pe.wait_ge(S("u_copy"), b * 4 + (4 * i + 3))
                pe.wait_ge(S(f"pages{i % 2}"), b * (8 * NPG) + 16 * NPG * (1 + i // 2 + NS // 2))
                pe.wait_ge(S("u_exp"), b * 2 + 2 * i + CREDIT)
                for c in range(5):
                    w = 512 if c < 4 else LS
                    rhs = KS[i % 2][:, c * 512:(c + 1) * 512] if c < 4 else K1[:, ds(b * LS + (i * LS + TP), LS)]
                    nc.tensor.matmul(ps[0:TS, c, 0:w], QB, rhs, start=True, stop=False)
                    mm = nc.tensor.matmul(ps[0:TS, c, 0:w], MRb, SS[:, c * 512:c * 512 + w], start=False, stop=True)
                mm.then_inc(S("u_logits"), 1)

            def outputs(b, i):
                pe.wait_ge(S("u_normed"), b + (i + 1))
                for c in range(NPG):
                    nc.tensor.matmul(ps[:, 5 + c // 8, (c % 8) * 64:(c % 8 + 1) * 64], ZS[:, c * P:(c + 1) * P], C("ident")[0:TS, 0:TS],
                                     start=True, stop=True)
                mm = nc.tensor.matmul(ps[0:LS, 7, 0:64], ZS[:, PAST:LK], C("ident")[0:TS, 0:TS], start=True, stop=True)
                mm.then_inc(S("u_turned"), 1)
                pe.wait_ge(S("u_copy"), b * 4 + (4 * i + 4))
                pe.wait_ge(S("u_pt"), b * 2 + (2 * i + 2))
                pe.wait_ge(S(f"pv{i}"), b * (8 * NPG) + 16 * NPG)
                pe.wait_ge(S("u_out"), b * 2 + 2 * i + CREDIT)
                for c in range(NPG):
                    nc.tensor.matmul(ps[:, 7, 64:128], VS[i][:, c, :], PTS[:, c, :], start=(c == 0), stop=False)
                mm = nc.tensor.matmul(ps[:, 7, 64:128], VNb, PTS[0:LS, 16, :], start=False, stop=True)
                mm.then_inc(S("u_outmm"), 1)

            pe.wait_ge(S("mask"), 4)
            logits(0, 0)
            with pe.Fori(0, NS // 2 - 1) as b2:
                b = b2 * 2
                for i in range(2):
                    logits(b, i + 1)
                    outputs(b, i)
            logits(NS - 2, 1)
            outputs(NS - 2, 0)
            outputs(NS - 2, 1)

        def d_sample_dve(dve, link):
            st = lambda j, n=1: DST[0:TS, j:j + n]

            def maxima(b, k):
                dve.wait_ge(S("u_logits"), b + (k + 1) + CREDIT)
                nc.vector.tensor_reduce(st(0), ps[0:TS, 0:4, :], mybir.AxisListType.XY, ALU.max).then_inc(S("u_max"), 1)
                nc.vector.tensor_reduce(st(1), ps[0:TS, 4, 0:LS], AX_X, ALU.max).then_inc(S("u_max"), 1)
                dve.wait_ge(S("u_max"), b * 2 + (2 * k + 2))
                link(nc.vector.tensor_tensor(st(2), st(0), st(1), ALU.max))
                nc.vector.tensor_scalar(st(3), st(2), -0.125, None, ALU.mult).then_inc(S("u_bias"), 1)

            def rest(b, last):
                dve.wait_ge(S("u_exp"), b * 2 + 2 + CREDIT)
                link(nc.vector.tensor_tensor(st(6), st(4), st(5), ALU.add))
                link(nc.vector.reciprocal(st(7), st(6)))
                nc.vector.tensor_scalar(ZS, ZS, st(7), None, ALU.mult).then_inc(S("u_normed"), 1)
                if not last:
                    maxima(b, 1)
                dve.wait_ge(S("u_turned"), b + 1 + CREDIT)
                nc.vector.tensor_copy(PTS[:, 0:16, :].rearrange("p (a c) n -> p a (c n)", a=2), ps[:, 5:7, :]).then_inc(S("u_pt"), 1)
                nc.vector.tensor_copy(PTS[0:LS, 16, :], ps[0:LS, 7, 0:64]).then_inc(S("u_pt"), 1)
                dve.wait_ge(S("u_outmm"), b + 1 + CREDIT)
                for v in range(2):
                    r = slice(64 * v, 64 * v + 64)
                    nc.vector.tensor_copy(H[r, 4:8, ds(b * LS + TP, LS)],
                                          ps[r, 7, 64 + 32 * v:96 + 32 * v].rearrange("p (g t) -> p g t", g=4)).then_inc(S("u_out"), 1)

            maxima(0, 0)
            with dve.Fori(0, NS - 1) as b:
                link.enter(b, 3)
                rest(b, False)
            link.leave(NS - 1)
            rest(NS - 1, True)

        def d_sample_act(act):
            with act.Fori(0, NS) as b:
                act.wait_ge(S("u_bias"), b + 1)
                act.wait_ge(S("u_turned"), b + CREDIT)
                nc.scalar.activation(ZS[:, 0:PAST].rearrange("p (c n) -> p c n", c=4), ps[0:TS, 0:4, :], ACT.Exp,
                                     bias=DST[0:TS, 3:4], scale=0.125, accum_out=DST[0:TS, 4:5]).then_inc(S("u_exp"), 1)
                nc.scalar.activation(ZS[:, PAST:LK], ps[0:TS, 4, 0:LS], ACT.Exp, bias=DST[0:TS, 3:4], scale=0.125,
                                     accum_out=DST[0:TS, 5:6]).then_inc(S("u_exp"), 1)

        RES = [lambda e: e.wait_ge(S("x_in"), 16), taken(G_EOUT), taken(LD[0]["o"]), taken(LD[0]["d"]), taken(G_OOUT),
               taken(LD[1]["o"]), taken(LD[1]["d"])]
        GAINS = ["mix0", "x0", "ffn0", "mix1", "x1", "ffn1", "final"]

        block = ctx.enter_context(nc.Block())

        def normed(eng, n):
            eng.wait_ge(S("normed"), KT * (n + 1))

        @block.sync
        def _(sp):
            sp.dma_start(X, a["x"]).then_inc(S("x_in"), 16)
            sp.dma_start(par[:, :], a["par"]).then_inc(S("par_in"), 16)
            weights_in(sp, G_EIN)
            weights_in(sp, G_EOUT)

            def cache_in(l):
                taken([G_EOUT, G_OOUT][l])(sp)
                normed(sp, 1 + 3 * l)
                if l == 1:
                    sp.wait_ge(S("d_stored"), 48)
                for i in range(2):
                    sp.dma_start(SKs[i], a["mk"][NS * l + i]).then_inc(S(f"sk{i}"), 16)
                    sp.dma_start(SVs[i], a["mv"][NS * l + i]).then_inc(S(f"sv{i}"), 16)
                for h in range(1, XH):
                    for i in range(2):
                        sp.wait_ge(S("y_logits"), h * 2 + (8 * l + i - 1) + CREDIT)
                        sp.dma_start(SKs[i], a["mk"][h * 2 + (NS * l + i)]).then_inc(S(f"sk{i}"), 16)
                    for i in range(2):
                        sp.wait_ge(S("y_outmm"), h * 2 + (8 * l + i - 1))
                        sp.dma_start(SVs[i], a["mv"][h * 2 + (NS * l + i)]).then_inc(S(f"sv{i}"), 16)

            for l in range(2):
                if l == 1:
                    weights_in(sp, G_OIN)
                    pages_in(sp)
                    weights_in(sp, G_OOUT)
                for k in ("q",) if l else ("k", "v", "q"):
                    weights_in(sp, LD[l][k])
                cache_in(l)
                for k in ("o", "gu", "d"):
                    weights_in(sp, LD[l][k])

        @block.gpsimd
        def _(pool):
            nc.gpsimd.memset(ones[:, :], 1.0).then_inc(S("consts_set"), 1)
            for name in CREDITED:
                pool.sem_inc(S(name), CREDIT)
            for j, v in enumerate((EPS, GN_EPS, 1e-12)):
                nc.gpsimd.memset(eps[:, j:j + 1], v).then_inc(S("consts_set"), 1)
            pool.dma_start(cst[:, :], a["cst"]).then_inc(S("cst_in"), 16)
            taken(G_EIN)(pool)
            nc.gpsimd.memset(Sb, 0.0).then_inc(S("consts_set"), 1)
            for dst, name in ((WS, "ws"), (WSS, "wss"), (BS, "bs"), (BSS, "bss")):
                pool.dma_start(dst, a[name]).then_inc(S("a_in"), 16)
            for dst, name in ((LORA, "lora"), (SH0, "sh0"), (RESET, "reset"), (S0, "s0")):
                pool.dma_start(dst, a[name]).then_inc(S("b_in"), 16)
            pool.dma_start(PT[:, :], a["table"]).then_inc(S("b_in"), 16)
            pool.wait_ge(S("cst_in"), 16)
            pool.wait_ge(S("a_normed"), 1)
            pool.dma_start(out["cv"], A_V[:, :, TP:T]).then_inc(S("cv_stored"), 16)
            with pool.Fori(0, NRC) as n:
                chunk_pool(pool, n, LEVELS, False)
            chunk_pool(pool, NRC, 3, True)
            pool.wait_ge(S("b_shift"), LS + 2)
            pool.dma_start(out["sh"], SHO).then_inc(S("b_stored"), 16)
            pool.wait_ge(S("s_state"), NS)
            pool.dma_start(out["rs"], S0).then_inc(S("b_stored"), 16)
            for hh in range(2):
                r = slice(64 * hh, 64 * hh + 64)
                pool.dma_start(out["rp"][hh], Sb[r, :, r]).then_inc(S("b_stored"), 16)
            pool.wait_ge(S("b_stored"), 64)
            for l in range(2):
                if l == 1:
                    taken(G_OOUT)(pool)
                    pool.wait_ge(S("m1_stored"), 16 * 2 * KT)
                    pool.dma_start(MK, out["mk"][1]).then_inc(S("mem_in"), 16)
                    pool.dma_start(MV, out["mv"][1]).then_inc(S("mem_in"), 16)
                    cross_pool(pool, l)
                    break
                pool.wait_ge(S("b_out"), 1)
                pool.dma_start(MR, a["mem"]).then_inc(S("mem_in"), 16)
                cross_pool(pool, l)
                pool.dma_start(out["mk"][l], MK).then_inc(S("m_stored"), 16)
                pool.dma_start(out["mv"][l], MV).then_inc(S("m_stored"), 16)
                pool.wait_ge(S("m_stored"), 32)
                taken(LD[0]["d"])(pool)
                pool.dma_start(cst[:, :], a["cst"]).then_inc(S("cst_in"), 16)
                taken(G_OIN)(pool)
                pool.wait_ge(S("cst_in"), 32)
                for dst, name in ((WXA, "wxa"), (LH0, "lh0"), (LCV, "lcv")):
                    pool.dma_start(dst, a[name]).then_inc(S("lru_in"), 16)
                pool.dma_start(ROT, a["rot"]).then_inc(S("rotary_in"), 16)
                pool.wait_ge(S("l_conv_out"), 1 + NS)
                pool.dma_start(out["conv"], CO).then_inc(S("c_stored"), 16)
                pool.dma_start(out["v"], V1).then_inc(S("d_stored"), 16)
                d_rope_pool(pool)
                pool.wait_ge(S("l_h_out"), 2)
                pool.dma_start(out["h"], HO).then_inc(S("c_stored"), 16)
                pool.wait_ge(S("l_out"), 1)
                pool.dma_start(MR, a["mem"]).then_inc(S("mem_in"), 16)
                pool.wait_ge(S("d_ready"), 6)
                pool.dma_start(out["k"], K1).then_inc(S("d_stored"), 16)
                pool.dma_start(out["ki"], KR[0:32]).then_inc(S("d_stored"), 16)
                d_index_pool(pool)
                d_prompt_pool(pool)
                d_sample_pool(pool)
                pool.wait_ge(S("c_stored"), 32)
                pool.wait_ge(S("d_stored"), 48)
                pool.wait_ge(S("u_out"), 2 * NS + CREDIT)
            normed(pool, 6)
            pool.dma_start(out["y"], H).then_inc(S("y_stored"), 16)
            pool.wait_ge(S("y_stored"), 16)
            pool.wait_ge(S("cv_stored"), 16)

        @block.tensor
        def _(pe):
            pe.wait_ge(S("consts_set"), 4)
            norm_pe(pe, 0)
            split_product(pe, G_EIN)
            pe.wait_ge(S("cst_in"), 16)
            a_pe(pe)
            b_pre_pe(pe)
            pe.wait_ge(S("consts_set"), 5)
            turn_pe(pe, 0, 0)
            with pe.Fori(0, NRC) as n:
                chunk_pe(pe, n, LEVELS, False)
            chunk_pe(pe, NRC, 3, True)
            sample_state_pe(pe)
            b_post_pe(pe)
            split_product(pe, G_EOUT)
            for l in range(2):
                if l == 1:
                    norm_pe(pe, 3)
                    split_product(pe, G_OIN)
                    c_pe(pe)
                    pe.wait_ge(S("cst_in"), 32)
                    d_rope_pe(pe)
                    d_score_pe(pe)
                    mem_pe(pe, 1)
                    d_index_pe(pe)
                    d_prompt_pe(pe)
                    d_sample_pe(pe)
                    split_product(pe, G_OOUT)
                if l == 0:
                    mem_pe(pe, 0)
                norm_pe(pe, 1 + 3 * l)
                if l == 0:
                    pe.wait_ge(S("m_normed"), KT)
                    memory_product(pe, LD[0]["k"], True)
                    memory_product(pe, LD[0]["v"], False)
                product(pe, LD[l]["q"], H, norm=1 + 3 * l)
                cross_pe(pe, l)
                split_product(pe, LD[l]["o"])
                norm_pe(pe, 2 + 3 * l)
                split_product(pe, LD[l]["gu"], gate_free(pe, LD[l]["gu"], l))
                down_pe(pe, l)
            norm_pe(pe, 6)

        @block.scalar
        def _(act):
            act.wait_ge(S("consts_set"), 4)
            norm_act(act, 0, RES[0])
            act.wait_ge(S("par_in"), 16)
            split_high(act, G_EIN, normed_tiles(act, 0))
            a_act(act)
            b_pre_act(act)
            with act.Fori(0, NRC) as n:
                chunk_act(act, n, LEVELS, False)
            chunk_act(act, NRC, 3, True)
            b_post_act(act)
            act.wait_ge(S("b_stored"), 64)
            act.wait_ge(S("a_out"), 2)
            act.wait_ge(S("b_out"), 1)
            split_high(act, G_EOUT)
            for l in range(2):
                if l == 1:
                    norm_act(act, 3, RES[3])
                    split_high(act, G_OIN, normed_tiles(act, 3))
                    c_act(act)
                    d_score_act(act)
                    act.wait_ge(S("d_ready"), 6)
                    mem_act(act, 1)
                    d_index_act(act)
                    d_prompt_act(act)
                    d_sample_act(act)
                    act.wait_ge(S("p_out"), 16 + CREDIT)
                    act.wait_ge(S("u_out"), 2 * NS + CREDIT)
                    split_high(act, G_OOUT)
                if l == 0:
                    mem_act(act, 0)
                norm_act(act, 1 + 3 * l, RES[1 + 3 * l])
                cross_act(act, l)
                act.wait_ge(S("m_stored"), 32)
                act.wait_ge(S("x_out"), 8 * (l + 1) + CREDIT)
                act.wait_ge(S("y_out"), NS * (l + 1) + CREDIT)
                split_high(act, LD[l]["o"])
                norm_act(act, 2 + 3 * l, RES[2 + 3 * l])
                gate_act(act, l)
                down_act(act, l)
            norm_act(act, 6, RES[6])

        @block.vector
        def _(dve):
            link = Chain(dve, S("vector_chain"))
            dve.wait_ge(S("par_in"), 16)
            norm_dve(dve, 0, RES[0], GAINS[0], link, G_EIN)
            split_take(dve, G_EIN, PJ)
            dve.wait_ge(S("cst_in"), 16)
            dve.wait_ge(S("consts_set"), 5)
            a_dve(dve, link)
            b_pre_dve(dve, link)
            for x in range(4):
                spread_x(x, 0, 0)
            chunk_rest(0, 0)
            with dve.Fori(0, NRC) as n:
                link.enter(n, 1 + 2)
                chunk_dve(dve, n, LEVELS, False, link)
            link.leave(NRC)
            chunk_dve(dve, NRC, 3, True, link)
            sample_state_dve(dve, link)
            b_post_dve(dve, link)
            split_low(dve, G_EOUT)
            split_take(dve, G_EOUT, X, True)
            for l in range(2):
                if l == 1:
                    norm_dve(dve, 3, RES[3], GAINS[3], link, G_OIN)
                    split_take(dve, G_OIN, PJ)
                    c_dve(dve, link)
                    dve.wait_ge(S("cst_in"), 32)
                    d_rope_dve(dve, link)
                    d_score_dve(dve, link)
                    mem_dve(dve, 1, link)
                    d_index_dve(dve, link)
                    d_prompt_dve(dve, link)
                    d_sample_dve(dve, link)
                    split_low(dve, G_OOUT)
                    split_take(dve, G_OOUT, X, True)
                if l == 0:
                    mem_dve(dve, 0, link)
                norm_dve(dve, 1 + 3 * l, RES[1 + 3 * l], GAINS[1 + 3 * l], link)
                if l == 0:
                    memory_take(dve, LD[0]["k"], True)
                    memory_take(dve, LD[0]["v"], False)
                take(dve, LD[l]["q"], XQ, False)
                cross_dve(dve, l, link)
                split_low(dve, LD[l]["o"])
                split_take(dve, LD[l]["o"], X, True)
                norm_dve(dve, 2 + 3 * l, RES[2 + 3 * l], GAINS[2 + 3 * l], link, LD[l]["gu"])
                gate_dve(dve, l)
                down_dve(dve, l)
            norm_dve(dve, 6, RES[6], GAINS[6], link)


def tiles(v):
    v = np.asarray(v)
    return np.ascontiguousarray(v.reshape(v.shape[0] // P, P, *v.shape[1:]).swapaxes(0, 1))


def blocks_of(w, kt):
    k, n = w.shape
    b = w.reshape(k // (kt * P), kt, P, n // P, P).transpose(3, 0, 2, 1, 4)
    return np.ascontiguousarray(b).reshape(-1, P, kt * P)


B_COLS = np.concatenate([np.arange(0, 512), np.arange(576, 1600), np.arange(512, 576), np.arange(1600, 1792)])
HEADS = np.concatenate([np.r_[64 * j:64 * j + 64, 64 * (4 + j):64 * (4 + j) + 64] for j in range(4)])


def kernel(**i):
    import concourse.bacc as bacc
    from concourse.bass_utils import run_bass_kernel_spmd

    i = {k: np.asarray(v) for k, v in i.items()}
    f = np.float32
    n = {}
    x = np.concatenate([i["x_prompt"][0], i["x_sample"].reshape(TS, D)], 0)
    n["x"] = tiles(x.T)
    n["mem"] = tiles(i["mem_prompt"][0].T)
    vecs = []
    for l in range(2):
        vecs.append(("mix%d" % l, i["norm_mix"][l]))
        vecs.append(("x%d" % l, i["norm_x"][l]))
        vecs.append(("mem%d" % l, i["norm_mem"][l]))
        vecs.append(("ffn%d" % l, i["norm_ffn"][l]))
    vecs += [("final", i["norm_final"]), ("ln_g", i["a_ln_g"][0]), ("ln_b", i["a_ln_b"][0]), ("mu", i["b_mu"][0][B_COLS]),
             ("w0", i["b_w0"][0]), ("a0", i["b_a0"][0]), ("k_k", i["b_kk"][0]), ("k_a", i["b_ka"][0]),
             ("r_k", i["b_rk"][0].reshape(-1)), ("gn_g", i["b_gn_g"][0]), ("gn_b", i["b_gn_b"][0]),
             ("conv_w", i["c_conv_w"][0].reshape(-1)), ("conv_b", i["c_conv_b"][0]), ("bx", i["c_bx"][0]),
             ("ba", i["c_ba"][0]), ("lam", i["c_lambda"][0])]
    n["par"] = np.zeros((P, NPAR), f)
    for name, v in vecs:
        o, w = PCOL[name]
        n["par"][:, o:o + w] = tiles(v)
    n["cst"] = np.concatenate([CONST[k] for k in CCOL], 1)
    c64, s64 = rotary(64)
    c32, s32 = rotary(32)
    n["rot"] = np.ascontiguousarray(np.stack([c64, s64, c32, s32], 1))
    reset = np.ones((P, T), f)
    reset[:, 0:TP:RC] = 0
    reset[:, TP::LS] = 0
    n["reset"] = reset
    wt = i["a_ws"][0].transpose(2, 0, 1)
    n["ws"] = np.ascontiguousarray(wt)
    wss = np.zeros((TS, A_G, TS), f)
    bss = np.zeros((1, A_G, NS, LS), f)
    for b in range(NS):
        wss[b * LS:(b + 1) * LS, :, b * LS:(b + 1) * LS] = wt[:LS, :, :LS]
        bss[0, :, b] = i["a_bs"][0][:, :LS]
    n["wss"] = wss
    n["bs"] = i["a_bs"][0].reshape(1, -1)
    n["bss"] = bss.reshape(1, -1)
    n["lora"] = np.concatenate([np.concatenate([i["b_wB"][0], i["b_aB"][0]], 0), i["b_gB"][0]], 1)
    n["sh0"] = tiles(i["state_rwkv_shift"][0][:, B_COLS].T)
    s0 = i["state_rwkv"][0].reshape(NS, 4, 2, 64, 64)
    n["s0"] = np.ascontiguousarray(s0.transpose(2, 4, 0, 1, 3)).reshape(P, NS, 4, 64)
    n["table"] = i["page_table"].reshape(1, -1)
    n["mk"] = np.ascontiguousarray(i["cache_mem_k"].reshape(2 * NS, MEM, KT, P).transpose(0, 3, 2, 1))
    n["mv"] = np.ascontiguousarray(i["cache_mem_v"].reshape(2 * NS, 2, P, D).transpose(0, 2, 1, 3))
    wxa = np.zeros((P, 2, 4, P), f)
    for g, w in enumerate((i["c_wx"][0], i["c_wa"][0])):
        for k in range(8):
            r = slice(64 * (k % 2), 64 * (k % 2) + 64)
            wxa[r, g, k // 2, r] = w[k]
    n["wxa"] = wxa
    n["lh0"] = tiles(i["state_lru_h"][0].T)
    n["lcv"] = tiles(i["state_lru_conv"][0].transpose(2, 0, 1))
    n["pool_k"] = np.ascontiguousarray(i["cache_attn_k"][0].reshape(-1, PAGE, P).transpose(0, 2, 1))
    n["pool_v"] = i["cache_attn_v"][0].reshape(-1, PAGE, P)
    n["pool_ki"] = np.ascontiguousarray(i["cache_attn_kidx"][0].transpose(0, 2, 1))
    ein = i["e_w_in"][0]
    n["w_ein"] = blocks_of(np.concatenate([ein[:, :1024], ein[:, 1024:][:, B_COLS]], 1), KT)
    n["w_eout"] = blocks_of(i["e_w_out"][0], KT)
    oin = i["o_w_in"][0]
    oin = np.concatenate([oin[:, :1024], oin[:, 1024:1536][:, HEADS], oin[:, 1536:],
                          np.zeros((D, OW_T * P - oin.shape[1]), f)], 1)
    n["w_oin"] = blocks_of(oin, KT)
    oo = i["o_w_out"][0]
    n["w_oout"] = blocks_of(np.concatenate([oo[:512], oo[512:][HEADS]], 0), KT)
    for l in range(2):
        n[f"w_xk{l}"], n[f"w_xv{l}"] = blocks_of(i["w_xk"][l], KT), blocks_of(i["w_xv"][l], KT)
        n[f"w_xq{l}"], n[f"w_xo{l}"] = blocks_of(i["w_xq"][l], KT), blocks_of(i["w_xo"][l], KT)
        n[f"w_gu{l}"] = np.stack([blocks_of(i["w_ff_gate"][l], KT), blocks_of(i["w_ff_up"][l], KT)], 1).reshape(2 * FT, P, D)
        n[f"w_d{l}"] = blocks_of(i["w_ff_down"][l], FT // 2)
    shapes = dict(y=(P, KT, T), cv=(P, 4, TS), rp=(2, 64, 4, 64), rs=(P, NS, 4, 64), sh=(P, 14, 9), conv=(P, 4, 27),
                  h=(P, 4, 9), k=(P, T), v=(P, T), ki=(32, T), mk=(2, P, KT, MEM), mv=(2, P, 2, D))
    nc = bacc.Bacc("TRN2", target_bir_lowering=False, num_devices=1)
    arrays = {f"in_{k}": np.ascontiguousarray(v) for k, v in n.items()}
    a = {k: nc.dram_tensor(f"in_{k}", list(v.shape), mybir.dt.from_np(v.dtype), kind="ExternalInput").ap() for k, v in n.items()}
    o = {k: nc.dram_tensor(f"out_{k}", list(s), F32, kind="ExternalOutput").ap() for k, s in shapes.items()}
    build(nc, a, o)
    r = run_bass_kernel_spmd(nc, [arrays], core_ids=[0]).results[0]
    r = {k: np.asarray(r[f"out_{k}"]) for k in shapes}

    rows = lambda v: v.swapaxes(0, 1).reshape(-1, *v.shape[2:])
    y = rows(r["y"]).T
    sh = np.empty((9, 1792), f)
    sh[:, B_COLS] = rows(r["sh"]).T
    state = lambda s: s.reshape(2, 64, -1, 4, 64).transpose(2, 3, 0, 4, 1).reshape(1, -1, 8, 64, 64)
    rp = r["rp"].reshape(P, 1, 4, 64)
    conv = rows(r["conv"]).reshape(512, 9, 3).transpose(1, 2, 0)
    h = rows(r["h"]).T
    k, v, ki = r["k"].T, r["v"].T, r["ki"].T
    mk = r["mk"].transpose(0, 3, 2, 1).reshape(2, 1, MEM, XH, XHD)
    mv = r["mv"].transpose(0, 2, 1, 3).reshape(2, 1, MEM, XH, XHD)
    return (y[None, :TP], y[TP:].reshape(NS, LS, D),
            state(rp), sh[None, :1], h[None, :1], conv[None, :1],
            k[:TP].reshape(1, 1, TP, 2, 64), v[:TP].reshape(1, 1, TP, 2, 64), ki[:TP].reshape(1, 1, TP, 32), mk, mv,
            rows(r["cv"]).T.reshape(1, NS, LS, AW), state(r["rs"]), sh[None, 1:], h[None, 1:], conv[None, 1:],
            k[TP:].reshape(1, NS, LS, 2, 64), v[TP:].reshape(1, NS, LS, 2, 64), ki[TP:].reshape(1, NS, LS, 32))
```
